# Optimizing a Trainium2 kernel written in Bass

```python
import math
import functools
import jax
import jax.numpy as jnp
from jax import lax
import numpy as np

D_MODEL = 1024
BATCH = 1
SEQ = 256
DEPTH = 2

GRID_W = 64
CTX_LEN = 256
CHUNK = 128
NORM_EPS = 1e-6
ROPE_BASE = 10000.0
NEG_INF = -1e30

RET_HEADS = 4
RET_DK = 128
RET_DV = 256
RET_QK_W = RET_HEADS * RET_DK
RET_V_W = RET_HEADS * RET_DV

SSM_HEADS = 16
SSM_HEAD_DIM = 64
SSM_GROUPS = 2
SSM_STATE = 128
SSM_CONV = 3
SSM_INNER = SSM_HEADS * SSM_HEAD_DIM
SSM_BC_W = SSM_GROUPS * SSM_STATE
SSM_XBC_W = SSM_INNER + 2 * SSM_BC_W

ATT_HEADS = 8
ATT_KV_HEADS = 2
ATT_HEAD_DIM = 128
ATT_WINDOW = 128
ATT_BLOCK = 128
ATT_Q_W = ATT_HEADS * ATT_HEAD_DIM
ATT_KV_W = ATT_KV_HEADS * ATT_HEAD_DIM

N_BRANCH = 3
BRANCH_W = RET_V_W

D_FF = 2816
N_EXPERTS = 8
TOP_K = 2
MOE_BLOCK = 128
N_DENSE = (DEPTH + 1) // 2
N_MOE = DEPTH // 2

IN_SPLITS = (RET_QK_W, RET_QK_W, RET_V_W, RET_V_W, SSM_INNER, SSM_XBC_W, SSM_HEADS, ATT_Q_W, ATT_KV_W, ATT_KV_W, N_BRANCH * D_MODEL)
IN_W = sum(IN_SPLITS)

kernel_name = 'hybrid_ret_ssd_swa_moe_dit'

def split_cols(t, sizes):
    return jnp.split(t, np.cumsum(sizes)[:-1].tolist(), axis=-1)

def rms_norm(t, w):
    tf = t.astype(jnp.float32)
    y = tf * lax.rsqrt(jnp.mean(tf * tf, axis=-1, keepdims=True) + NORM_EPS)
    return (y * w.astype(jnp.float32)).astype(t.dtype)

def head_rms(t):
    return t * lax.rsqrt(jnp.mean(t * t, axis=-1, keepdims=True) + NORM_EPS)

def adaln(cond, w, b):
    m = jnp.dot(jax.nn.silu(cond), w) + b
    return m.reshape(*cond.shape[:-1], 6, D_MODEL)

def rope_angles(pos, dim):
    inv = ROPE_BASE ** (-jnp.arange(0, dim, 2, dtype=jnp.float32) / dim)
    return pos.astype(jnp.float32)[:, None] * inv[None, :]

def apply_rope(t, ang):
    half = t.shape[-1] // 2
    cos = jnp.cos(ang)[None, :, None, :]
    sin = jnp.sin(ang)[None, :, None, :]
    t1 = t[..., :half].astype(jnp.float32)
    t2 = t[..., half:].astype(jnp.float32)
    return jnp.concatenate([t1 * cos - t2 * sin, t1 * sin + t2 * cos], axis=-1).astype(t.dtype)

def axial_rope(t):
    n_tok, dim = t.shape[1], t.shape[-1]
    rows = n_tok // GRID_W
    row = jnp.repeat(jnp.arange(rows), GRID_W)
    col = jnp.tile(jnp.arange(GRID_W), rows)
    half = dim // 2
    return jnp.concatenate([apply_rope(t[..., :half], rope_angles(row, half)),
                            apply_rope(t[..., half:], rope_angles(col, half))], axis=-1)

def keep_seq(t):
    return t

def flip_seq(t):
    return jnp.flip(t, axis=1)

def retention_chunked(q, k, v, log_g, s0, with_out):
    bsz, T, H, dk = q.shape
    dv = v.shape[-1]
    n = T // CHUNK
    qc = q.reshape(bsz, n, CHUNK, H, dk)
    kc = k.reshape(bsz, n, CHUNK, H, dk)
    vc = v.reshape(bsz, n, CHUNK, H, dv)
    i = jnp.arange(CHUNK, dtype=jnp.float32)
    w_state = jnp.exp((CHUNK - 1 - i)[:, None] * log_g[None, :])
    u = jnp.einsum('bnjhd,bnjhe,jh->bnhde', kc, vc, w_state)
    chunk_decay = jnp.exp(CHUNK * log_g)[None, :, None, None]

    def step(s, u_n):
        return chunk_decay * s + u_n, s

    s_last, s_prev = lax.scan(step, s0, jnp.moveaxis(u, 1, 0))
    if not with_out:
        return None, s_last
    s_prev = jnp.moveaxis(s_prev, 0, 1)
    diff = i[:, None] - i[None, :]
    dmat = jnp.where(diff[None] >= 0, jnp.exp(jnp.maximum(diff, 0.0)[None] * log_g[:, None, None]), 0.0)
    scores = jnp.einsum('bnihd,bnjhd->bnhij', qc, kc) * dmat
    o = jnp.einsum('bnhij,bnjhe->bnihe', scores, vc)
    w_q = jnp.exp((i + 1)[:, None] * log_g[None, :])
    o = o + jnp.einsum('bnihd,bnhde,ih->bnihe', qc, s_prev, w_q)
    return o.reshape(bsz, T, H, dv), s_last

def retention_branch(q_c, k_c, v_c, g_c, q_x, k_x, v_x, g_x, ret_decay, need_ctx):
    bsz, S = q_x.shape[:2]
    L = q_c.shape[1]

    def heads(t, d):
        return t.astype(jnp.float32).reshape(bsz, t.shape[1], RET_HEADS, d)

    scale = RET_DK ** -0.5
    ang = rope_angles(jnp.arange(S), RET_DK)
    qc, kc, vc = heads(q_c, RET_DK), heads(k_c, RET_DK) * scale, heads(v_c, RET_DV)
    qx = apply_rope(heads(q_x, RET_DK), ang)
    kx = apply_rope(heads(k_x, RET_DK), ang) * scale
    vx = heads(v_x, RET_DV)
    log_g = jax.nn.log_sigmoid(ret_decay.astype(jnp.float32))
    s0 = jnp.zeros((bsz, RET_HEADS, RET_DK, RET_DV), jnp.float32)
    oc = 0.0
    ox = 0.0
    for d, o in enumerate((keep_seq, flip_seq)):
        oc_d, s_ctx = retention_chunked(o(qc), o(kc), o(vc), log_g[d], s0, need_ctx)
        ox_d, _ = retention_chunked(o(qx), o(kx), o(vx), log_g[d], s_ctx, True)
        ox = ox + o(ox_d)
        if need_ctx:
            oc = oc + o(oc_d)
    out_x = (jax.nn.silu(g_x.astype(jnp.float32)) * head_rms(ox).reshape(bsz, S, RET_V_W)).astype(g_x.dtype)
    out_c = None
    if need_ctx:
        out_c = (jax.nn.silu(g_c.astype(jnp.float32)) * head_rms(oc).reshape(bsz, L, RET_V_W)).astype(g_c.dtype)
    return out_c, out_x

def short_conv_silu(t, w, b):
    pad = SSM_CONV // 2
    y = lax.conv_general_dilated(t, w[:, None, :].astype(t.dtype), window_strides=(1,), padding=[(pad, pad)],
                                 dimension_numbers=('NWC', 'WIO', 'NWC'), feature_group_count=t.shape[-1])
    return jax.nn.silu(y + b)

def ssd_chunked(xh, dt, a, bmat, cmat, d_skip, s0, with_out):
    bsz, T, G, Hg, P = xh.shape
    N = bmat.shape[-1]
    n = T // CHUNK
    xc = xh.reshape(bsz, n, CHUNK, G, Hg, P)
    dtc = dt.reshape(bsz, n, CHUNK, G, Hg)
    bc = bmat.reshape(bsz, n, CHUNK, G, N)
    cc = cmat.reshape(bsz, n, CHUNK, G, N)
    cum = jnp.cumsum(dtc * a, axis=2)
    xdt = xc * dtc[..., None]
    w_state = jnp.exp(cum[:, :, -1:] - cum)
    u = jnp.einsum('bcjgs,bcjgh,bcjghp->bcghps', bc, w_state, xdt)
    chunk_decay = jnp.exp(cum[:, :, -1])

    def step(s, inp):
        u_c, dec = inp
        return dec[..., None, None] * s + u_c, s

    s_last, s_prev = lax.scan(step, s0, (jnp.moveaxis(u, 1, 0), jnp.moveaxis(chunk_decay, 1, 0)))
    if not with_out:
        return None, s_last
    s_prev = jnp.moveaxis(s_prev, 0, 1)
    cum_t = jnp.moveaxis(cum, 2, -1)
    seg = cum_t[..., :, None] - cum_t[..., None, :]
    lower_tri = jnp.tril(jnp.ones((CHUNK, CHUNK), bool))
    lmat = jnp.where(lower_tri, jnp.exp(jnp.where(lower_tri, seg, 0.0)), 0.0)
    cb = jnp.einsum('bcigs,bcjgs->bcgij', cc, bc)
    y = jnp.einsum('bcgij,bcghij,bcjghp->bcighp', cb, lmat, xdt)
    y = y + jnp.einsum('bcigs,bcghps,bcigh->bcighp', cc, s_prev, jnp.exp(cum))
    y = y + xc * d_skip[..., None]
    return y.reshape(bsz, T, G, Hg, P), s_last

def gated_group_rms(y, z, w):
    bsz, T = y.shape[:2]
    gw = SSM_INNER // SSM_GROUPS
    g = y.reshape(bsz, T, SSM_GROUPS, gw) * jax.nn.silu(z.astype(jnp.float32)).reshape(bsz, T, SSM_GROUPS, gw)
    g = head_rms(g).reshape(bsz, T, SSM_INNER)
    return (g * w.astype(jnp.float32)).astype(z.dtype)

def ssd_branch(z_c, xbc_c, dt_c, z_x, xbc_x, dt_x, conv_w, conv_b, dt_bias, a_log, d_skip, norm_w, need_ctx):
    hg = SSM_HEADS // SSM_GROUPS

    def prep(xbc, dt_raw):
        bsz, T = xbc.shape[:2]
        u = short_conv_silu(xbc, conv_w, conv_b).astype(jnp.float32)
        xs, bm, cm = split_cols(u, (SSM_INNER, SSM_BC_W, SSM_BC_W))
        return (xs.reshape(bsz, T, SSM_GROUPS, hg, SSM_HEAD_DIM),
                bm.reshape(bsz, T, SSM_GROUPS, SSM_STATE),
                cm.reshape(bsz, T, SSM_GROUPS, SSM_STATE),
                dt_raw.astype(jnp.float32).reshape(bsz, T, SSM_GROUPS, hg))

    xc, bc, cc, dtc = prep(xbc_c, dt_c)
    xx, bx, cx, dtx = prep(xbc_x, dt_x)
    s0 = jnp.zeros((xx.shape[0], SSM_GROUPS, hg, SSM_HEAD_DIM, SSM_STATE), jnp.float32)
    yc = 0.0
    yx = 0.0
    for d, o in enumerate((keep_seq, flip_seq)):
        a = -jnp.exp(a_log[d].astype(jnp.float32)).reshape(SSM_GROUPS, hg)
        bias = dt_bias[d].astype(jnp.float32).reshape(SSM_GROUPS, hg)
        skip = d_skip[d].astype(jnp.float32).reshape(SSM_GROUPS, hg)
        yc_d, s_ctx = ssd_chunked(o(xc), jax.nn.softplus(o(dtc) + bias), a, o(bc), o(cc), skip, s0, need_ctx)
        yx_d, _ = ssd_chunked(o(xx), jax.nn.softplus(o(dtx) + bias), a, o(bx), o(cx), skip, s_ctx, True)
        yx = yx + o(yx_d)
        if need_ctx:
            yc = yc + o(yc_d)
    out_x = gated_group_rms(yx, z_x, norm_w)
    out_c = gated_group_rms(yc, z_c, norm_w) if need_ctx else None
    return out_c, out_x

def window_attention_branch(q_c, k_c, v_c, q_x, k_x, v_x, sink, need_ctx):
    bsz, S = q_x.shape[:2]
    L = k_c.shape[1]
    G = ATT_HEADS // ATT_KV_HEADS
    nb = S // ATT_BLOCK
    scale = ATT_HEAD_DIM ** -0.5
    kc = k_c.reshape(bsz, L, ATT_KV_HEADS, ATT_HEAD_DIM)
    vc = v_c.reshape(bsz, L, ATT_KV_HEADS, ATT_HEAD_DIM)
    qx = axial_rope(q_x.reshape(bsz, S, ATT_HEADS, ATT_HEAD_DIM)) * scale
    kx = axial_rope(k_x.reshape(bsz, S, ATT_KV_HEADS, ATT_HEAD_DIM))
    vx = v_x.reshape(bsz, S, ATT_KV_HEADS, ATT_HEAD_DIM)
    sink_kg = sink.astype(jnp.float32).reshape(ATT_KV_HEADS, G)

    def banded(t):
        tp = jnp.pad(t, ((0, 0), (ATT_BLOCK, ATT_BLOCK), (0, 0), (0, 0)))
        tp = tp.reshape(bsz, nb + 2, ATT_BLOCK, ATT_KV_HEADS, ATT_HEAD_DIM)
        return jnp.concatenate([tp[:, :-2], tp[:, 1:-1], tp[:, 2:]], axis=2)

    qb = qx.reshape(bsz, nb, ATT_BLOCK, ATT_KV_HEADS, G, ATT_HEAD_DIM)
    kb, vb = banded(kx), banded(vx)
    s_win = jnp.einsum('bnikgd,bnjkd->bnkgij', qb, kb).astype(jnp.float32)
    qi = jnp.arange(ATT_BLOCK)[:, None]
    kj = jnp.arange(3 * ATT_BLOCK)[None, :]
    kpos = (jnp.arange(nb) * ATT_BLOCK - ATT_BLOCK)[:, None, None] + kj[None]
    valid = (jnp.abs(qi + ATT_BLOCK - kj) <= ATT_WINDOW)[None] & (kpos >= 0) & (kpos < S)
    s_win = jnp.where(valid[None, :, None, None], s_win, NEG_INF)
    s_ctx = jnp.einsum('bnikgd,bjkd->bnkgij', qb, kc).astype(jnp.float32)
    s_sink = jnp.broadcast_to(sink_kg[None, None, :, :, None, None], s_ctx.shape[:-1] + (1,))
    p = jax.nn.softmax(jnp.concatenate([s_sink, s_ctx, s_win], axis=-1), axis=-1)
    o = (jnp.einsum('bnkgij,bjkd->bnikgd', p[..., 1:1 + L], vc.astype(jnp.float32))
         + jnp.einsum('bnkgij,bnjkd->bnikgd', p[..., 1 + L:], vb.astype(jnp.float32)))
    out_x = o.reshape(bsz, S, ATT_Q_W).astype(q_x.dtype)
    out_c = None
    if need_ctx:
        qc = q_c.reshape(bsz, L, ATT_KV_HEADS, G, ATT_HEAD_DIM) * scale
        s_cc = jnp.einsum('bikgd,bjkd->bkgij', qc, kc).astype(jnp.float32)
        s_sink_c = jnp.broadcast_to(sink_kg[None, :, :, None, None], s_cc.shape[:-1] + (1,))
        pc = jax.nn.softmax(jnp.concatenate([s_sink_c, s_cc], axis=-1), axis=-1)
        out_c = jnp.einsum('bkgij,bjkd->bikgd', pc[..., 1:], vc.astype(jnp.float32)).reshape(bsz, L, ATT_Q_W).astype(q_c.dtype)
    return out_c, out_x

def merge_branches(outs, gate_logits, w_branch, w_out):
    br = jnp.einsum('btnw,nwd->btnd', jnp.stack(outs, axis=2), w_branch)
    g = jax.nn.sigmoid(gate_logits.astype(jnp.float32)).reshape(*gate_logits.shape[:-1], N_BRANCH, D_MODEL)
    merged = jnp.sum(g * br, axis=2).astype(outs[0].dtype)
    return merged @ w_out

def swiglu(h, w1, w3, w2):
    return (jax.nn.silu(h @ w1) * (h @ w3)) @ w2

def moe_swiglu(h, w_router, w1, w3, w2):
    bsz, T, D = h.shape
    n_tok = bsz * T
    u = h.reshape(n_tok, D)
    logits = jnp.dot(u, w_router).astype(jnp.float32)
    top_logit, top_e = lax.top_k(logits, TOP_K)
    top_w = jax.nn.softmax(top_logit, axis=-1)
    n_asg = n_tok * TOP_K
    flat_e = top_e.reshape(n_asg)
    flat_tok = jnp.repeat(jnp.arange(n_tok, dtype=jnp.int32), TOP_K)
    flat_w = top_w.reshape(n_asg)
    order = jnp.argsort(flat_e)
    e_sorted = flat_e[order]
    counts = jnp.bincount(flat_e, length=N_EXPERTS)
    padded = (counts + MOE_BLOCK - 1) // MOE_BLOCK * MOE_BLOCK
    start = jnp.cumsum(counts) - counts
    pend = jnp.cumsum(padded)
    pstart = pend - padded
    slot = pstart[e_sorted] + (jnp.arange(n_asg) - start[e_sorted])
    n_slots = (-(-n_asg // MOE_BLOCK) + N_EXPERTS) * MOE_BLOCK
    n_blocks = n_slots // MOE_BLOCK
    slot_tok = jnp.zeros((n_slots,), jnp.int32).at[slot].set(flat_tok[order])
    slot_w = jnp.zeros((n_slots,), jnp.float32).at[slot].set(flat_w[order])
    blk_e = jnp.minimum(jnp.searchsorted(pend, jnp.arange(n_blocks) * MOE_BLOCK, side='right'), N_EXPERTS - 1)
    xb = u[slot_tok].reshape(n_blocks, MOE_BLOCK, D)

    def expert_block(args):
        xe, e = args
        return (jax.nn.silu(xe @ w1[e]) * (xe @ w3[e])) @ w2[e]

    yb = lax.map(expert_block, (xb, blk_e)).reshape(n_slots, D)
    y = jnp.zeros((n_tok, D), jnp.float32).at[slot_tok].add(yb.astype(jnp.float32) * slot_w[:, None])
    return y.reshape(bsz, T, D).astype(h.dtype)

def mixer_sublayer(xc, x, mods_c, mods_x, n_pre, n_post, w_in, ret_decay, conv_w, conv_b, dt_bias, a_log,
                   d_skip, ssm_norm_w, sink, w_branch, w_out, need_ctx):
    L = xc.shape[1]
    hc = rms_norm(xc, n_pre) * (1 + mods_c[1]) + mods_c[0]
    hx = rms_norm(x, n_pre) * (1 + mods_x[1]) + mods_x[0]
    proj = jnp.concatenate([hc, hx], axis=1) @ w_in
    rq, rk, rv, rg, sz, sxbc, sdt, aq, ak, av, bgate = split_cols(proj, IN_SPLITS)

    def pc(t):
        return t[:, :L]

    def px(t):
        return t[:, L:]

    ret_c, ret_x = retention_branch(pc(rq), pc(rk), pc(rv), pc(rg), px(rq), px(rk), px(rv), px(rg), ret_decay, need_ctx)
    ssd_c, ssd_x = ssd_branch(pc(sz), pc(sxbc), pc(sdt), px(sz), px(sxbc), px(sdt), conv_w, conv_b, dt_bias,
                              a_log, d_skip, ssm_norm_w, need_ctx)
    att_c, att_x = window_attention_branch(pc(aq), pc(ak), pc(av), px(aq), px(ak), px(av), sink, need_ctx)
    if need_ctx:
        outs = [jnp.concatenate([oc, ox], axis=1) for oc, ox in ((ret_c, ret_x), (ssd_c, ssd_x), (att_c, att_x))]
        y = merge_branches(outs, bgate, w_branch, w_out)
        xc_new = xc + mods_c[2] * rms_norm(y[:, :L], n_post)
        y = y[:, L:]
    else:
        y = merge_branches([ret_x, ssd_x, att_x], px(bgate), w_branch, w_out)
        xc_new = None
    return xc_new, x + mods_x[2] * rms_norm(y, n_post)

def ffn_sublayer(xc, x, mods_c, mods_x, n_pre, n_post, ffn):
    hx = rms_norm(x, n_pre) * (1 + mods_x[4]) + mods_x[3]
    if xc is None:
        return None, x + mods_x[5] * rms_norm(ffn(hx), n_post)
    L = xc.shape[1]
    hc = rms_norm(xc, n_pre) * (1 + mods_c[4]) + mods_c[3]
    y = rms_norm(ffn(jnp.concatenate([hc, hx], axis=1)), n_post)
    return xc + mods_c[5] * y[:, :L], x + mods_x[5] * y[:, L:]

def setup_inputs(seed: int = 0) -> dict:
    key = jax.random.key(seed)
    ks = iter(jax.random.split(key, 40))
    D = D_MODEL

    def nrm(shape, scale):
        return jax.random.normal(next(ks), shape, jnp.float32) * scale

    def unif(shape, lo, hi):
        return jax.random.uniform(next(ks), shape, jnp.float32, lo, hi)

    p = 2.0 ** (-5.0 - jnp.arange(RET_HEADS, dtype=jnp.float32))
    ret_logit = jnp.log((1.0 - p) / p)
    ret_decay = jnp.stack([ret_logit, ret_logit[::-1]])[None] + nrm((DEPTH, 2, RET_HEADS), 0.05)
    dt0 = jnp.exp(unif((DEPTH, 2, SSM_HEADS), math.log(1e-3), math.log(1e-1)))
    dt_bias = dt0 + jnp.log(-jnp.expm1(-dt0))
    a_log = jnp.log(unif((DEPTH, 2, SSM_HEADS), 1.0, 16.0))
    return {
        'x': nrm((BATCH, SEQ, D), 1.0),
        'c': nrm((BATCH, D), 1.0),
        'ctx': nrm((BATCH, CTX_LEN, D), 1.0),
        'c_ctx': nrm((D,), 1.0),
        'ada_w': nrm((DEPTH, D, 6 * D), 0.5 * D ** -0.5),
        'ada_b': nrm((DEPTH, 6 * D), 0.02),
        'mix_norm_pre': 1.0 + nrm((DEPTH, D), 0.02),
        'mix_norm_post': 1.0 + nrm((DEPTH, D), 0.02),
        'ffn_norm_pre': 1.0 + nrm((DEPTH, D), 0.02),
        'ffn_norm_post': 1.0 + nrm((DEPTH, D), 0.02),
        'w_in': nrm((DEPTH, D, IN_W), D ** -0.5),
        'ret_decay': ret_decay,
        'ssm_conv_w': nrm((DEPTH, SSM_CONV, SSM_XBC_W), SSM_CONV ** -0.5),
        'ssm_conv_b': nrm((DEPTH, SSM_XBC_W), 0.02),
        'ssm_dt_bias': dt_bias,
        'ssm_a_log': a_log,
        'ssm_d': 1.0 + nrm((DEPTH, 2, SSM_HEADS), 0.1),
        'ssm_norm_w': 1.0 + nrm((DEPTH, SSM_INNER), 0.02),
        'att_sink': nrm((DEPTH, ATT_HEADS), 0.5),
        'w_branch': nrm((DEPTH, N_BRANCH, BRANCH_W, D), BRANCH_W ** -0.5),
        'w_out': nrm((DEPTH, D, D), D ** -0.5),
        'ffn_w1': nrm((N_DENSE, D, D_FF), D ** -0.5),
        'ffn_w3': nrm((N_DENSE, D, D_FF), D ** -0.5),
        'ffn_w2': nrm((N_DENSE, D_FF, D), D_FF ** -0.5),
        'moe_router': nrm((N_MOE, D, N_EXPERTS), D ** -0.5),
        'moe_w1': nrm((N_MOE, N_EXPERTS, D, D_FF), D ** -0.5),
        'moe_w3': nrm((N_MOE, N_EXPERTS, D, D_FF), D ** -0.5),
        'moe_w2': nrm((N_MOE, N_EXPERTS, D_FF, D), D_FF ** -0.5),
    }

def reference(x, c, ctx, c_ctx, ada_w, ada_b, mix_norm_pre, mix_norm_post, ffn_norm_pre, ffn_norm_post, w_in,
              ret_decay, ssm_conv_w, ssm_conv_b, ssm_dt_bias, ssm_a_log, ssm_d, ssm_norm_w, att_sink, w_branch,
              w_out, ffn_w1, ffn_w3, ffn_w2, moe_router, moe_w1, moe_w3, moe_w2):
    xc = ctx
    for i in range(DEPTH):
        need_ctx = i < DEPTH - 1
        m_x = adaln(c, ada_w[i], ada_b[i])
        m_c = adaln(c_ctx, ada_w[i], ada_b[i])
        mods_x = [m_x[:, None, k] for k in range(6)]
        mods_c = [m_c[k] for k in range(6)]
        xc, x = mixer_sublayer(xc, x, mods_c, mods_x, mix_norm_pre[i], mix_norm_post[i], w_in[i], ret_decay[i],
                               ssm_conv_w[i], ssm_conv_b[i], ssm_dt_bias[i], ssm_a_log[i], ssm_d[i], ssm_norm_w[i],
                               att_sink[i], w_branch[i], w_out[i], need_ctx)
        j = i // 2
        if i % 2 == 0:
            ffn = functools.partial(swiglu, w1=ffn_w1[j], w3=ffn_w3[j], w2=ffn_w2[j])
        else:
            ffn = functools.partial(moe_swiglu, w_router=moe_router[j], w1=moe_w1[j], w3=moe_w3[j], w2=moe_w2[j])
        xc, x = ffn_sublayer(xc, x, mods_c, mods_x, ffn_norm_pre[i], ffn_norm_post[i], ffn)
    return x


_drawn_inputs = setup_inputs


def setup_inputs(seed=0):
    import zlib

    import numpy as np

    out = dict(_drawn_inputs(seed))
    spreads = {}
    factors = {'ffn_norm_pre': 3.857,
     'ffn_norm_post': 3.437,
     'ssm_conv_b': 4.196,
     'ssm_norm_w': 5.237,
     'att_sink': 64.0,
     'mix_norm_post': 3.794}
    for name, (base, spread) in spreads.items():
        noise = np.random.default_rng([zlib.crc32(name.encode()), seed]).standard_normal(out[name].shape)
        drawn = base * np.exp(spread * noise) if base else spread * noise
        out[name] = jnp.asarray(drawn.astype(out[name].dtype))
    for name, factor in factors.items():
        out[name] = (out[name] * factor).astype(out[name].dtype)
    return out
```

```python
from contextlib import ExitStack

import numpy as np

import concourse.bass as bass
from concourse import mybir

F32 = mybir.dt.float32
F32R = mybir.dt.float32r
ACT = mybir.ActivationFunctionType
ALU = mybir.AluOpType
AX = mybir.AxisListType

P = 128
D = 1024
KD = D // P
SEQ, CTX = 256, 256
NT = (SEQ + CTX) // P
TOK = NT * P
X_TILES, ALL_TILES = [2, 3], [0, 1, 2, 3]
DEPTH = 2
EPS = 1e-6
GRID_W = 64
BLK = 512
RH, DK, DV = 4, 128, 256
SH, HD, SG, ST = 16, 64, 2, 128
HG = SH // SG
XBC = SH * HD + 2 * SG * ST
AH, KVH, AD = 8, 2, 128
AG = AH // KVH
FF = 2816
FT = FF // P
NE = 8
NEG = -1e30

SPLITS = dict(rq=RH * DK, rk=RH * DK, rv=RH * DV, rg=RH * DV, sz=SH * HD, xbc=XBC, dt=SH,
              aq=AH * AD, akv=2 * KVH * AD, gate=3 * D)
COL = {}
_at = 0
for _name, _width in SPLITS.items():
    COL[_name] = _at
    _at += _width
IN_W = _at

CONSTS = dict(ident=P, tri_f=P, tri_b=P, neg_up=P, neg_low=P, ones=P, dist_f=P, dist_b=P, iota=P,
              ret_w=4, sel=2, before=NE * NE,
              rq_cos=128, rq_sin=128, rk_cos=128, rk_sin=128, aq_cos=128, aq_sin=128, ak_cos=128, ak_sin=128)
CAT = {}
_at = 0
for _name, _width in CONSTS.items():
    CAT[_name] = _at
    _at += _width
N_CONST = _at

ROWS = dict(ada_b=48, mix_pre=8, ffn_pre=8, conv_w=36, conv_b=12, c=8, c_ctx=8)
ROW = {}
_at = 0
for _name, _width in ROWS.items():
    ROW[_name] = _at
    _at += _width


def constants():
    a = np.zeros((P, N_CONST), np.float32)
    i = np.arange(P, dtype=np.float32)
    row, col = i[:, None], i[None, :]

    def put(name, v):
        a[:, CAT[name]:CAT[name] + v.shape[1]] = v

    put("ident", np.eye(P, dtype=np.float32))
    put("tri_f", (row <= col).astype(np.float32))
    put("tri_b", (row >= col).astype(np.float32))
    put("neg_up", np.where(col > row, NEG, 0.0).astype(np.float32))
    put("neg_low", np.where(col < row, NEG, 0.0).astype(np.float32))
    put("ones", np.ones((P, P), np.float32))
    put("dist_f", np.maximum(col - row, 0.0))
    put("dist_b", np.maximum(row - col, 0.0))
    put("iota", np.broadcast_to(col, (P, P)))
    put("ret_w", np.stack([P - 1 - i, i, i + 1, P - i], 1))
    put("sel", (np.arange(P)[:, None] % 2 == np.arange(2)[None, :]).astype(np.float32))
    e = np.arange(NE)
    put("before", np.broadcast_to((e[None, :] < e[:, None]).astype(np.float32).reshape(1, NE * NE), (P, NE * NE)))
    pos = np.arange(SEQ, dtype=np.float32)

    def angles(p, dim):
        inv = np.float32(10000.0) ** (-np.arange(0, dim, 2, dtype=np.float32) / np.float32(dim))
        return p[:, None] * inv[None, :].astype(np.float32)

    grid_row, grid_col = np.floor(pos / GRID_W), pos % GRID_W
    ret = angles(pos, DK)
    att = np.concatenate([angles(grid_row, AD // 2), angles(grid_col, AD // 2)], 1)
    for name, ang, scale in (("rq", ret, 1.0), ("rk", ret, DK ** -0.5), ("aq", att, AD ** -0.5), ("ak", att, 1.0)):
        for part, fn in (("cos", np.cos), ("sin", np.sin)):
            t = (fn(ang).astype(np.float32) * np.float32(scale)).reshape(2, P, 64).transpose(1, 0, 2)
            put(f"{name}_{part}", t.reshape(P, 128))
    return a


class Steps:

    def __init__(self, sem):
        self.sem, self.n = sem, 0

    def __call__(self, eng, ins):
        self.n += 1
        ins.then_inc(self.sem, 1)
        eng.wait_ge(self.sem, self.n)


def program(nc, t):
    ctx = ExitStack()
    with ctx:
        top = [nc.sbuf_base + (-nc.sbuf_base) % 64]

        placed = {}

        def at(name, shape, dt, offset):
            if name not in placed:
                placed[name] = nc.alloc_sbuf_tensor_at(name, shape, dt, offset=offset)
            return placed[name]

        def size(shape):
            return int(np.prod(shape[1:])) * 4

        def sb(name, shape, dt=F32):
            offset = top[0]
            top[0] += size(shape) + (-size(shape)) % 64
            return at(name, shape, dt, offset)

        def sem(name):
            return ctx.enter_context(nc.semaphore(name))

        ps = [ctx.enter_context(nc.psum_tensor(f"bank{i}", [P, BLK], F32)) for i in range(8)]

        cst = sb("constants", [P, N_CONST])

        def const(name):
            return cst[:, CAT[name]:CAT[name] + CONSTS[name]]

        ident = const("ident")
        cols = [sb(f"param_cols{l}", [P, P]) for l in range(DEPTH)]
        norm_cols = [sb(f"norm_cols{l}", [P, 24]) for l in range(DEPTH)]
        mods = [sb(f"mods{l}", [P, 48, 2]) for l in range(DEPTH)]
        gains = [sb(f"gains{l}", [P, 4, KD, 2]) for l in range(DEPTH)]
        heads = [sb(f"head_params{l}", [P, 8 + 32 + 32 + 32 + 8]) for l in range(DEPTH)]
        xres = sb("xres", [P, NT, D])
        small = sb("small", [P, 128])
        ring_at = top[0]
        raw = sb("raw_units", [P, 2, 2048])
        whi = sb("unit_hi", [P, 2, 2048], F32R)
        wlo = sb("unit_lo", [P, 2, 2048], F32R)
        hT_at = top[0]
        hT = [sb(f"hT_{n}", [P, KD, TOK], F32R) for n in ("hi", "lo")]
        outT_at = top[0]
        outT = [sb(f"outT_{n}", [P, KD, TOK], F32R) for n in ("hi", "lo")]
        merged_at = top[0]
        merged = sb("merged", [P, NT, D])
        work = top[0]
        limit = nc.sbuf_usable_end - 64

        raw_loaded = [sem("raw_loaded0"), sem("raw_loaded1")]
        hi_ready, lo_ready, unit_used = sem("hi_ready"), sem("lo_ready"), sem("unit_used")
        dve_step, act_step, pool_step = Steps(sem("dve_step")), Steps(sem("act_step")), Steps(sem("pool_step"))
        units, span = [], {}

        def unit_block(w, col, width=BLK):
            v = w.rearrange("(k p) n -> p k n", p=P)
            for half in range(2):
                units.append(v[:, 4 * half:4 * half + 4, col:col + width])

        def stage_units(name, add):
            a = len(units)
            add()
            span[name] = (a, len(units))

        for l in range(DEPTH):
            w_in, ada, wb, wo = t["w_in"][l], t["ada_w"][l], t["w_branch"][l], t["w_out"][l]

            def cols_of(name, n):
                for b in range(n):
                    unit_block(w_in, COL[name] + b * BLK)

            def add_ssm():
                cols_of("xbc", 3)
                units.append(w_in.rearrange("(k p) n -> p k n", p=P)[:, :, COL["dt"]:COL["dt"] + SH])

            def add_merge(n):
                for b in range(2):
                    unit_block(w_in, COL["gate"] + n * D + b * BLK)
                    unit_block(wb[n], b * BLK)

            stage_units(f"ada{l}", lambda: [unit_block(ada, b * BLK) for b in range(12)])
            stage_units(f"ssm{l}", add_ssm)
            stage_units(f"z{l}", lambda: cols_of("sz", 2))
            stage_units(f"merge1_{l}", lambda: add_merge(1))
            stage_units(f"ret{l}", lambda: [cols_of("rq", 1), cols_of("rk", 1), cols_of("rv", 2)])
            stage_units(f"g{l}", lambda: cols_of("rg", 2))
            stage_units(f"merge0_{l}", lambda: add_merge(0))
            stage_units(f"att{l}", lambda: [cols_of("aq", 2), cols_of("akv", 1)])
            stage_units(f"merge2_{l}", lambda: add_merge(2))
            stage_units(f"out{l}", lambda: [unit_block(wo, b * BLK) for b in range(2)])
            if l == 0:
                w1, w3, w2 = t["ffn_w1"][0], t["ffn_w3"][0], t["ffn_w2"][0]

                def add_ffn():
                    for f in range(FF // 256):
                        for w in (w1, w3):
                            units.append(w.rearrange("(k p) n -> p k n", p=P)[:, :, f * 256:f * 256 + 256])

                stage_units("ffn_up", add_ffn)
                stage_units("ffn_down", lambda: [
                    units.append(w2.rearrange("(k p) n -> p k n", p=P)[:, 2 * u:2 * u + 2, :]) for u in range(FT // 2)])
        n_units = len(units)

        def view(buf, g):
            a, b = units[g].shape[1], units[g].shape[2]
            return buf[:, g % 2, 0:a * b].rearrange("p (a b) -> p a b", b=b)

        def load_unit(sp, g):
            if g >= n_units:
                return
            if g >= 2:
                sp.wait_ge(lo_ready, g - 1)
            sp.dma_start(view(raw, g), units[g]).then_inc(raw_loaded[g % 2], 16)

        def split_hi(act, g):
            if g >= n_units:
                return
            act.wait_ge(raw_loaded[g % 2], 16 * (g // 2 + 1))
            if g >= 2:
                act.wait_ge(unit_used, g - 1)
            act.activation(view(whi, g), view(raw, g), ACT.Copy).then_inc(hi_ready, 1)

        def split_lo(eng, g):
            if g >= n_units:
                return
            eng.wait_ge(hi_ready, g + 1)
            eng.tensor_tensor(view(wlo, g), view(raw, g), view(whi, g).bitcast(F32), ALU.subtract).then_inc(lo_ready, 1)

        def loads(sp, name):
            a, b = span[name]
            for g in range(a + 4, b + 4):
                load_unit(sp, g)

        def splits_lo(eng, name):
            a, b = span[name]
            for g in range(a + 2, b + 2):
                split_lo(eng, g)

        def three(pe, out, a, w, first, last):
            pe.matmul(out, a[0], w[0], start=first, stop=False)
            pe.matmul(out, a[0], w[1], start=False, stop=False)
            return pe.matmul(out, a[1], w[0], start=False, stop=last)

        def project(pe, g, banks, tiles, src=None):
            for u in range(2):
                pe.wait_ge(lo_ready, g + u + 1)
                w = [view(whi, g + u), view(wlo, g + u)]
                for k in range(4):
                    kk = 4 * u + k
                    for j, tile in enumerate(tiles):
                        a = [h[:, kk, tile * P:(tile + 1) * P] for h in (src or hT)]
                        last = three(pe, ps[banks[j]][:, :], a, [w[0][:, k, :], w[1][:, k, :]], kk == 0, kk == KD - 1)
                last.then_inc(unit_used, 1)

        def spread(col, n, m):
            return col.unsqueeze(2).to_broadcast([P, n, m])

        stage_no, in_use, cleared = [0], [], []

        def stage_sem(name):
            guard = nc.semaphore(f"{name}_{stage_no[0]}")
            in_use.append((guard, guard.__enter__()))
            return in_use[-1][1]

        def end_stage():
            for guard, handle in cleared:
                guard.__exit__(None, None, None)
            cleared[:] = in_use
            in_use.clear()
            for guard, handle in cleared:
                nc.sync.sem_clear(handle)
            stage_no[0] += 1

        def setup():
            rows = [at(f"param_rows{l}", [P, P], F32, work + 512 * l) for l in range(DEPTH)]
            nrows = [at(f"norm_rows{l}", [24, P], F32, work + 1024 + 512 * l) for l in range(DEPTH)]
            const_in, x_in, head_in, row_in = (stage_sem(n) for n in ("const_in", "x_in", "head_in", "row_in"))
            turned, cols_out = stage_sem("turned"), stage_sem("cols_out")
            n_rows = 0
            with nc.Block() as block:
                @block.sync
                def _(sp):
                    sp.dma_start(cst[:, :], t["consts"]).then_inc(const_in, 16)
                    for g in range(2):
                        load_unit(sp, g)
                    sp.dma_start(xres[:, 0:2, :], t["ctx"][0].rearrange("(t p) d -> p t d", p=P)).then_inc(x_in, 16)
                    sp.dma_start(xres[:, 2:4, :], t["x"][0].rearrange("(t p) d -> p t d", p=P)).then_inc(x_in, 16)
                    for g in range(2, 4):
                        load_unit(sp, g)
                    sp.wait_ge(x_in, 32)

                @block.scalar
                def _(act):
                    for l in range(DEPTH):
                        for name, src in (("ada_b", t["ada_b"][l].rearrange("(a p) -> a p", p=P)),
                                          ("mix_pre", t["mix_norm_pre"][l].rearrange("(a p) -> a p", p=P)),
                                          ("ffn_pre", t["ffn_norm_pre"][l].rearrange("(a p) -> a p", p=P)),
                                          ("conv_w", t["ssm_conv_w"][l].rearrange("w (a p) -> (w a) p", p=P)),
                                          ("conv_b", t["ssm_conv_b"][l].rearrange("(a p) -> a p", p=P)),
                                          ("c", t["c"][0].rearrange("(a p) -> a p", p=P)),
                                          ("c_ctx", t["c_ctx"].rearrange("(a p) -> a p", p=P))):
                            act.dma_start(rows[l][ROW[name]:ROW[name] + ROWS[name], :], src).then_inc(row_in, 16)
                        for j, name in enumerate(("mix_norm_post", "ffn_norm_post", "ssm_norm_w")):
                            act.dma_start(nrows[l][8 * j:8 * j + 8, :],
                                          t[name][l].rearrange("(a p) -> a p", p=P)).then_inc(row_in, 16)
                        for a, b, src in ((0, 8, t["ret_decay"][l].rearrange("a b -> (a b)")),
                                          (8, 40, t["ssm_dt_bias"][l].rearrange("a b -> (a b)")),
                                          (40, 72, t["ssm_a_log"][l].rearrange("a b -> (a b)")),
                                          (72, 104, t["ssm_d"][l].rearrange("a b -> (a b)")),
                                          (104, 112, t["att_sink"][l])):
                            act.dma_start(heads[l][:, a:b], src.partition_broadcast(P)).then_inc(head_in, 16)
                    act.wait_ge(head_in, 16 * 5 * DEPTH)
                    for g in range(2):
                        split_hi(act, g)

                @block.gpsimd
                def _(pool):
                    for g in range(2):
                        split_lo(pool, g)

                @block.tensor
                def _(pe):
                    pe.wait_ge(const_in, 16)
                    pe.wait_ge(row_in, 16 * 10 * DEPTH)
                    for l in range(DEPTH):
                        pe.transpose(ps[l][:, 0:P], rows[l][:, :], ident).then_inc(turned, 1)
                        pe.transpose(ps[2 + l][:, 0:24], nrows[l][:, :], ident[0:24, 0:24]).then_inc(turned, 1)

                @block.vector
                def _(dve):
                    for l in range(DEPTH):
                        dve.wait_ge(turned, 2 * l + 1)
                        dve.tensor_copy(cols[l][:, :], ps[l][:, 0:P]).then_inc(cols_out, 1)
                        dve.wait_ge(turned, 2 * l + 2)
                        dve.tensor_copy(norm_cols[l][:, :], ps[2 + l][:, 0:24]).then_inc(cols_out, 1)
            end_stage()

        def col(l, name, n=None):
            a = ROW[name]
            return cols[l][:, a:a + (n or ROWS[name])]

        def ada(l):
            cond = at("cond", [P, 16], F32, work)
            cond4 = at("cond_parts", [P, KD, 4], F32R, work + 64)
            mod_rows = at("mod_rows", [4, 6 * D], F32, work + 256)
            names = ("cond_silu", "cond_split", "rows_out", "cols_done", "mods_done")
            cond_silu, cond_split, rows_out, cols_done, mods_done = (stage_sem(n) for n in names)
            a0, b0 = span[f"ada{l}"]
            with nc.Block() as block:
                @block.sync
                def _(sp):
                    loads(sp, f"ada{l}")

                @block.scalar
                def _(act):
                    act.activation(cond[:, :], cols[l][:, ROW["c"]:ROW["c"] + 16], ACT.Silu).then_inc(cond_silu, 1)
                    for g in range(a0 + 2, b0 + 2):
                        split_hi(act, g)

                @block.vector
                def _(dve):
                    cv = cond[:, :].rearrange("p (c k) -> p k c", c=2)
                    dve.wait_ge(cond_silu, 1)
                    dve_step(dve, dve.tensor_copy(cond4[:, :, 0:2], cv))
                    dve.tensor_tensor(cond4[:, :, 2:4], cv, cond4[:, :, 0:2].bitcast(F32), ALU.subtract).then_inc(cond_split, 1)
                    for n in range(12):
                        for u in range(2):
                            split_lo(dve, a0 + 2 + 2 * n + u)
                        dve.wait_ge(unit_used, a0 + 2 * n + 2)
                        dve.tensor_copy(mod_rows[:, n * BLK:(n + 1) * BLK], ps[n % 2][0:4, :]).then_inc(rows_out, 1)
                    dve.wait_ge(cols_done, 1)
                    m = mods[l]
                    dve_step(dve, dve.tensor_tensor(m[:, :, :], ps[2][:, 0:96].rearrange("p (f c) -> p f c", c=2),
                                                    spread(col(l, "ada_b"), 48, 2), ALU.add))
                    gn = gains[l]
                    for j, (which, w) in enumerate(((1, col(l, "mix_pre")), (4, col(l, "ffn_pre")))):
                        dve_step(dve, dve.tensor_scalar(gn[:, j, :, :], m[:, 8 * which:8 * which + 8, :], 1.0, None, ALU.add))
                        dve_step(dve, dve.tensor_tensor(gn[:, j, :, :], gn[:, j, :, :], spread(w, KD, 2), ALU.mult))
                    for j, which in ((0, 2), (1, 5)):
                        w = norm_cols[l][:, 8 * j:8 * j + 8]
                        dve_step(dve, dve.tensor_tensor(gn[:, 2 + j, :, :], m[:, 8 * which:8 * which + 8, :],
                                                        spread(w, KD, 2), ALU.mult))

                @block.tensor
                def _(pe):
                    pe.wait_ge(cond_split, 1)
                    for n in range(12):
                        if n >= 2:
                            pe.wait_ge(rows_out, n - 1)
                        for u in range(2):
                            g = a0 + 2 * n + u
                            pe.wait_ge(lo_ready, g + 1)
                            for k in range(4):
                                kk = 4 * u + k
                                pe.matmul(ps[n % 2][0:4, :], cond4[:, kk, :], view(whi, g)[:, k, :], start=kk == 0, stop=False)
                                last = pe.matmul(ps[n % 2][0:4, :], cond4[:, kk, :], view(wlo, g)[:, k, :],
                                                 start=False, stop=kk == KD - 1)
                            last.then_inc(unit_used, 1)
                    pe.wait_ge(rows_out, 12)
                    for f in range(48):
                        last = pe.matmul(ps[2][:, 2 * f:2 * f + 2], mod_rows[:, f * P:(f + 1) * P],
                                         cst[0:4, CAT["sel"]:CAT["sel"] + 2], start=True, stop=True)
                    last.then_inc(cols_done, 1)
            end_stage()

        def norm(l, tiles, which):
            A, B = gains[l][:, which, :, :], mods[l][:, 24 * which:24 * which + 8, :]
            n = len(tiles)
            xn = at("normed", [P, NT, D], F32, work)
            tmp = at("affine", [P, 2, TOK], F32, work + NT * D * 4)
            squares, roots, normed, turned, affine, parts = (
                stage_sem(s) for s in ("squares", "roots", "normed", "turned", "affine", "parts"))
            ssq, rstd = small[:, 0:4], small[:, 4:8]
            with nc.Block() as block:
                @block.scalar
                def _(act):
                    for tile in tiles:
                        act.activation(xn[:, tile, :], xres[:, tile, :], ACT.Square,
                                       accum_out=ssq[:, tile:tile + 1]).then_inc(squares, 1)
                    act.wait_ge(roots, 1)
                    act.activation(rstd[:, :], rstd[:, :], ACT.Sqrt).then_inc(roots, 1)
                    for d in range(KD):
                        act.wait_ge(turned, d + 1)
                        if d >= 2:
                            act.wait_ge(parts, d - 1)
                        segs = [(0, 2 * P, 1), (2 * P, TOK, 0)] if n == NT else [(0, 2 * P, 0)]
                        for s, (a, b, c) in enumerate(segs):
                            ins = act.activation(tmp[:, d % 2, a:b], ps[d][:, a:b], ACT.Identity,
                                                 scale=A[:, d, c:c + 1], bias=B[:, d, c:c + 1])
                        ins.then_inc(affine, 1)

                @block.vector
                def _(dve):
                    lo, hi = tiles[0], tiles[-1] + 1
                    dve.wait_ge(squares, n)
                    dve_step(dve, dve.memset(rstd[:, :], 1.0))
                    dve.tensor_scalar(rstd[:, lo:hi], ssq[:, lo:hi], 1.0 / D, EPS, ALU.mult, ALU.add).then_inc(roots, 1)
                    dve.wait_ge(roots, 2)
                    dve_step(dve, dve.reciprocal(rstd[:, :], rstd[:, :]))
                    for tile in tiles:
                        dve.tensor_scalar(xn[:, tile, :], xres[:, tile, :], rstd[:, tile:tile + 1], None,
                                          ALU.mult).then_inc(normed, 1)
                    for d in range(KD):
                        dve.wait_ge(affine, d + 1)
                        w = n * P
                        dve_step(dve, dve.tensor_copy(hT[0][:, d, lo * P:hi * P], tmp[:, d % 2, 0:w]))
                        dve.tensor_tensor(hT[1][:, d, lo * P:hi * P], tmp[:, d % 2, 0:w],
                                          hT[0][:, d, lo * P:hi * P].bitcast(F32), ALU.subtract).then_inc(parts, 1)

                @block.tensor
                def _(pe):
                    pe.wait_ge(normed, n)
                    for d in range(KD):
                        for j, tile in enumerate(tiles):
                            last = pe.transpose(ps[d][:, j * P:(j + 1) * P], xn[:, tile, d * P:(d + 1) * P], ident)
                        last.then_inc(turned, 1)
            end_stage()

        def ssm_project(l):
            a0, b0 = span[f"ssm{l}"]
            ux = at("u_x", [P, 8, TOK], F32, work)
            bT, cT, btok, dtraw, xtok = ssm_tensors()[:5]
            acc = at("conv_acc", [P, 4, TOK], F32, work + 32768)
            acc_set, conv_done, u_ready, turned, turned_out, dt_sum = (
                stage_sem(s) for s in ("acc_set", "conv_done", "u_ready", "turned", "turned_out", "dt_sum"))
            cw, cb = col(l, "conv_w"), col(l, "conv_b")

            def u_of(i):
                return ux[:, i, :] if i < 8 else (bT if i < 10 else cT)[:, i % 2, :]

            with nc.Block() as block:
                @block.sync
                def _(sp):
                    loads(sp, f"ssm{l}")

                @block.gpsimd
                def _(pool):
                    splits_lo(pool, f"ssm{l}")

                @block.scalar
                def _(act):
                    for n in range(3):
                        for u in range(2):
                            split_hi(act, a0 + 2 * n + u + 2)
                        act.wait_ge(unit_used, a0 + 2 * n + 2)
                        for m in range(4):
                            i = 4 * n + m
                            act.activation(acc[:, m, :], ps[4 * (n % 2) + m][:, :], ACT.Identity,
                                           scale=cw[:, 12 + i:13 + i], bias=cb[:, i:i + 1]).then_inc(acc_set, 1)
                        for m in range(4):
                            i = 4 * n + m
                            act.wait_ge(conv_done, i + 1)
                            act.activation(u_of(i), acc[:, m, :], ACT.Silu).then_inc(u_ready, 1)
                        act.wait_ge(u_ready, 4 * n + 4)
                    split_hi(act, a0 + 8)

                @block.vector
                def _(dve):
                    for i in range(12):
                        n, m = divmod(i, 4)
                        s = ps[4 * (n % 2) + m][:, :].rearrange("p (s t) -> p s t", s=2)
                        o = acc[:, m, :].rearrange("p (s t) -> p s t", s=2)
                        dve.wait_ge(acc_set, i + 1)
                        dve_step(dve, dve.scalar_tensor_tensor(o[:, :, 1:], s[:, :, :-1], cw[:, i:i + 1], o[:, :, 1:],
                                                               ALU.mult, ALU.add))
                        dve.scalar_tensor_tensor(o[:, :, :-1], s[:, :, 1:], cw[:, 24 + i:25 + i], o[:, :, :-1],
                                                 ALU.mult, ALU.add).then_inc(conv_done, 1)
                    dve.wait_ge(dt_sum, 1)
                    dve.tensor_copy(dtraw[:, :, :], ps[4][:, 0:NT * SH].rearrange("p (t h) -> p t h", h=SH))
                    for i in range(10):
                        dve.wait_ge(turned, i + 1)
                        out = xtok[:, :, i * P:(i + 1) * P] if i < 8 else btok[:, :, (i - 8) * P:(i - 7) * P]
                        dve.tensor_copy(out, ps[5 + i % 3][:, :].rearrange("p (t f) -> p t f", t=NT)).then_inc(turned_out, 1)

                @block.tensor
                def _(pe):
                    for n in range(3):
                        if n == 2:
                            pe.wait_ge(conv_done, 4)
                        for u in range(2):
                            g = a0 + 2 * n + u
                            pe.wait_ge(lo_ready, g + 1)
                            wh, wl = view(whi, g), view(wlo, g)
                            for k in range(4):
                                kk = 4 * u + k
                                for m in range(4):
                                    a = [wh[:, k, m * P:(m + 1) * P], wl[:, k, m * P:(m + 1) * P]]
                                    last = three(pe, ps[4 * (n % 2) + m][:, :], a, [h[:, kk, :] for h in hT],
                                                 kk == 0, kk == KD - 1)
                            last.then_inc(unit_used, 1)
                    g = a0 + 6
                    pe.wait_ge(lo_ready, g + 1)
                    pe.wait_ge(conv_done, 8)
                    for tile in range(NT):
                        for k in range(KD):
                            a = [h[:, k, tile * P:(tile + 1) * P] for h in hT]
                            last = three(pe, ps[4][:, tile * SH:(tile + 1) * SH], a,
                                         [view(whi, g)[:, k, :], view(wlo, g)[:, k, :]], k == 0, k == KD - 1)
                    last.then_inc(unit_used, 1)
                    pe.transpose(ps[5][:, 0:P], ident, ident).then_inc(dt_sum, 1)
                    for i in range(10):
                        pe.wait_ge(u_ready, i + 1)
                        if i >= 3:
                            pe.wait_ge(turned_out, i - 2)
                        for tile in range(NT):
                            last = pe.transpose(ps[5 + i % 3][:, tile * P:(tile + 1) * P],
                                                u_of(i)[:, tile * P:(tile + 1) * P], ident)
                        last.then_inc(turned, 1)
            end_stage()

        def ssm_tensors():
            bT = at("B_T", [P, SG, TOK], F32, work + 16384)
            cT = at("C_T", [P, SG, TOK], F32, work + 20480)
            btok = at("B_tok", [P, NT, SG * ST], F32, work + 24576)
            dtraw = at("dt_raw", [P, NT, SH], F32, work + 28672)
            xtok = at("x_tok", [P, NT, D], F32, outT_at)
            y = at("y_ssm", [P, NT, D], F32, work)
            return bT, cT, btok, dtraw, xtok, y

        ORDER = ([0, 1, 2, 3], [1, 0, 3, 2])

        def ssm_mix(l, tiles):
            bT, cT, btok, dtraw, xtok, y = ssm_tensors()
            p0 = work + 28672 + 256
            dtv, dta, tmp1, cums, exps = (at(f"ssm_{n}", [P, w], F32, p0 + o) for n, w, o in (
                ("dt", 128, 0), ("dta", 128, 512), ("tmp", 128, 1024), ("cum_tot", 256, 1536), ("expa", 32, 2560)))
            ecum, wst, dec, skip = (at(f"ssm_{n}", [P, w], F32, p0 + 2688 + o) for n, w, o in (
                ("ecum", 128, 0), ("w_state", 128, 512), ("decay", 128, 1024), ("skip", 16, 1536)))
            cbs = at("CB", [P, 2, P], F32, work + 34816)
            state = at("ssm_state", [P, 2, SG, 512], F32, work + 36864)
            xw = at("x_weighted", [P, 512], F32, work + 45056)
            part = at("y_part", [P, 2, 512], F32, work + 47104)
            seg = at("segments", [P, 2, 2, HG, P], F32, outT_at + 16384)
            hp = heads[l]

            def d4(a, d):
                return a[:, d * 64:(d + 1) * 64].rearrange("p (t h) -> p t h", h=SH)

            def hg(a, d, tile, g):
                b = d * 64 + tile * SH + g * HG
                return a[:, b:b + HG]

            def wide(a):
                return spread(a, HG, HD)

            def by_head(a):
                return a.rearrange("p (h e) -> p h e", h=HG)

            names = ("dt_act", "dt_dve", "cum_sum", "cum_out", "exps_done", "seg_sum", "seg_out", "seg_exp", "mixed",
                     "intra", "intra_out", "weighted", "update", "update_out", "inter", "inter_out")
            (dt_act, dt_dve, cum_sum, cum_out, exps_done, seg_sum, seg_out, seg_exp, mixed,
             intra, intra_out, weighted, update, update_out, inter, inter_out) = (stage_sem(s) for s in names)
            jobs = [(tile, g) for tile in tiles for g in range(SG)]
            steps = [(s, d, g) for s in range(NT) for d in range(2) for g in range(SG)]
            updates = [x for x in steps if x[0] < NT - 1]
            inters = [x for x in steps if x[0] > 0 and ORDER[x[1]][x[0]] in tiles]
            with nc.Block() as block:
                @block.scalar
                def _(act):
                    act.wait_ge(dt_dve, 1)
                    act_step(act, act.activation(dta[:, :], tmp1[:, :], ACT.Exp, scale=-1.0))
                    act.activation(exps[:, :], hp[:, 40:72], ACT.Exp).then_inc(dt_act, 1)
                    act.wait_ge(dt_dve, 2)
                    act.activation(cums[:, 0:128], tmp1[:, :], ACT.Ln).then_inc(dt_act, 1)
                    act.wait_ge(cum_out, 1)
                    act.activation(ecum[:, :], cums[:, 0:128], ACT.Exp)
                    act.activation(dec[:, :], cums[:, 128:256], ACT.Exp)
                    act.activation(wst[:, :], wst[:, :], ACT.Exp).then_inc(exps_done, 1)
                    for n in range(len(jobs)):
                        act.wait_ge(seg_out, n + 1)
                        for d in range(2):
                            ins = act.activation(seg[:, n % 2, d, :, :], seg[:, n % 2, d, :, :], ACT.Exp)
                        ins.then_inc(seg_exp, 1)

                @block.vector
                def _(dve):
                    for d in range(2):
                        bias = hp[:, 8 + 16 * d:24 + 16 * d].unsqueeze(1).to_broadcast([P, NT, SH])
                        dve_step(dve, dve.tensor_tensor(d4(dtv, d), dtraw[:, :, :], bias, ALU.add))
                    dve.scalar_tensor_tensor(tmp1[:, :], dtv[:, :], -1.0, dtv[:, :], ALU.mult, ALU.max).then_inc(dt_dve, 1)
                    dve_step(dve, dve.tensor_tensor(skip[:, :], hp[:, 72:88], hp[:, 88:104], ALU.add))
                    dve.wait_ge(dt_act, 1)
                    dve.tensor_scalar(tmp1[:, :], dta[:, :], 1.0, None, ALU.add).then_inc(dt_dve, 1)
                    dve.wait_ge(dt_dve, 2)
                    dve_step(dve, dve.tensor_scalar(ecum[:, :], tmp1[:, :], -1.0, 1e-30, ALU.add, ALU.max))
                    dve_step(dve, dve.reciprocal(ecum[:, :], ecum[:, :]))
                    dve_step(dve, dve.tensor_tensor(ecum[:, :], ecum[:, :], dta[:, :], ALU.mult))
                    dve.wait_ge(dt_act, 2)
                    dve_step(dve, dve.tensor_tensor(ecum[:, :], ecum[:, :], cums[:, 0:128], ALU.mult))
                    dve_step(dve, dve.scalar_tensor_tensor(dtv[:, :], dtv[:, :], 0.0, ecum[:, :], ALU.max, ALU.add))
                    for d in range(2):
                        ea = exps[:, 16 * d:16 * d + 16].unsqueeze(1).to_broadcast([P, NT, SH])
                        ins = dve.scalar_tensor_tensor(d4(dta, d), d4(dtv, d), -1.0, ea, ALU.mult, ALU.mult)
                    ins.then_inc(dt_dve, 1)
                    dve.wait_ge(cum_sum, 1)
                    dve_step(dve, dve.tensor_copy(cums[:, :], ps[0][:, 0:256]))
                    dve.tensor_tensor(wst[:, :], cums[:, 128:256], cums[:, 0:128], ALU.subtract).then_inc(cum_out, 1)
                    dve.wait_ge(exps_done, 1)
                    dve_step(dve, dve.tensor_tensor(wst[:, :], wst[:, :], dtv[:, :], ALU.mult))
                    for n, (tile, g) in enumerate(jobs):
                        s = seg[:, n % 2, :, :, :]
                        dve.wait_ge(seg_sum, n + 1)
                        for d in range(2):
                            for h in range(HG):
                                bank = ps[2 * d + h // 4]
                                cum = hg(cums, d, tile, g)[:, h:h + 1]
                                dve.scalar_tensor_tensor(s[:, d, h, :], bank[:, (h % 4) * P:(h % 4 + 1) * P], cum,
                                                         const("neg_low" if d == 0 else "neg_up"), ALU.subtract, ALU.add)
                        dve.tensor_copy(cbs[:, n % 2, :], ps[4 + 2 * (n % 2)][:, 0:P]).then_inc(seg_out, 1)
                        dve.wait_ge(seg_exp, n + 1)
                        for d in range(2):
                            dve_step(dve, dve.tensor_tensor(s[:, d, :, :], s[:, d, :, :], spread(hg(dtv, d, tile, g), HG, P), ALU.mult))
                        dve_step(dve, dve.tensor_tensor(s[:, 0, :, :], s[:, 0, :, :], s[:, 1, :, :], ALU.add))
                        dve.tensor_tensor(s[:, 0, :, :], s[:, 0, :, :], cbs[:, n % 2, :].unsqueeze(1).to_broadcast([P, HG, P]),
                                          ALU.mult).then_inc(mixed, 1)
                        yo = y[:, tile, g * 512:(g + 1) * 512]
                        dve_step(dve, dve.tensor_tensor(by_head(yo), by_head(xtok[:, tile, g * 512:(g + 1) * 512]),
                                                        wide(skip[:, g * HG:(g + 1) * HG]), ALU.mult))
                        dve.wait_ge(intra, n + 1)
                        dve.tensor_tensor(yo, yo, ps[5 + 2 * (n % 2)][:, :], ALU.add).then_inc(intra_out, 1)
                    n_up = n_in = 0
                    for s, d, g in steps:
                        tile = ORDER[d][s]
                        if s < NT - 1:
                            if n_up:
                                dve.wait_ge(update, n_up)
                            dve.tensor_tensor(by_head(xw[:, :]), by_head(xtok[:, tile, g * 512:(g + 1) * 512]),
                                              wide(hg(wst, d, tile, g)), ALU.mult).then_inc(weighted, 1)
                        if (s, d, g) in inters:
                            dve.wait_ge(inter, n_in + 1)
                            yo = y[:, tile, g * 512:(g + 1) * 512]
                            pt = part[:, n_in % 2, :]
                            dve_step(dve, dve.tensor_tensor(by_head(pt), by_head(ps[2 + n_in % 2][:, :]),
                                                            wide(hg(ecum, d, tile, g)), ALU.mult))
                            dve.tensor_tensor(yo, yo, pt, ALU.add).then_inc(inter_out, 1)
                            n_in += 1
                        if s < NT - 1:
                            st = state[:, d, g, :]
                            if s:
                                dve_step(dve, dve.tensor_tensor(by_head(st), by_head(st), wide(hg(dec, d, tile, g)), ALU.mult))
                            dve.wait_ge(update, n_up + 1)
                            if s:
                                dve.tensor_tensor(st, st, ps[n_up % 2][:, :], ALU.add).then_inc(update_out, 1)
                            else:
                                dve.tensor_copy(st, ps[n_up % 2][:, :]).then_inc(update_out, 1)
                            n_up += 1

                @block.tensor
                def _(pe):
                    pe.wait_ge(dt_dve, 3)
                    for d, tri in enumerate(("tri_f", "tri_b")):
                        pe.matmul(ps[0][:, 64 * d:64 * d + 64], const(tri), dta[:, 64 * d:64 * d + 64], start=True, stop=True)
                        last = pe.matmul(ps[0][:, 128 + 64 * d:192 + 64 * d], const("ones"), dta[:, 64 * d:64 * d + 64],
                                         start=True, stop=True)
                    last.then_inc(cum_sum, 1)
                    pe.wait_ge(cum_out, 1)
                    for n in range(len(jobs) + 1):
                        if n < len(jobs):
                            tile, g = jobs[n]
                            tok = slice(tile * P, (tile + 1) * P)
                            if n:
                                pe.wait_ge(seg_out, n)
                            if n >= 2:
                                pe.wait_ge(intra_out, n - 1)
                            pe.matmul(ps[4 + 2 * (n % 2)][:, 0:P], bT[:, g, tok], cT[:, g, tok], start=True, stop=True)
                            for d, tri in enumerate(("tri_f", "tri_b")):
                                for h in range(HG):
                                    w = hg(dta, d, tile, g)[:, h:h + 1].to_broadcast([P, P])
                                    last = pe.matmul(ps[2 * d + h // 4][:, (h % 4) * P:(h % 4 + 1) * P], w, const(tri),
                                                     start=True, stop=True)
                            last.then_inc(seg_sum, 1)
                        if n >= 1:
                            tile, g = jobs[n - 1]
                            pe.wait_ge(mixed, n)
                            for h in range(HG):
                                c = (g * HG + h) * HD
                                last = pe.matmul(ps[5 + 2 * ((n - 1) % 2)][:, h * HD:(h + 1) * HD],
                                                 seg[:, (n - 1) % 2, 0, h, :], xtok[:, tile, c:c + HD], start=True, stop=True)
                            last.then_inc(intra, 1)
                    n_up = n_in = 0
                    for s, d, g in steps:
                        tile = ORDER[d][s]
                        if (s, d, g) in inters:
                            pe.wait_ge(update_out, 4 * (s - 1) + 2 * d + g + 1)
                            if n_in >= 2:
                                pe.wait_ge(inter_out, n_in - 1)
                            pe.matmul(ps[2 + n_in % 2][:, :], cT[:, g, tile * P:(tile + 1) * P], state[:, d, g, :],
                                      start=True, stop=True).then_inc(inter, 1)
                            n_in += 1
                        if s < NT - 1:
                            pe.wait_ge(weighted, n_up + 1)
                            if n_up >= 2:
                                pe.wait_ge(update_out, n_up - 1)
                            pe.matmul(ps[n_up % 2][:, :], btok[:, tile, g * ST:(g + 1) * ST], xw[:, :],
                                      start=True, stop=True).then_inc(update, 1)
                            n_up += 1
            end_stage()

        def turn_to_outT(pe, src, tiles, f_range, ready, turned, parts):
            for f in f_range:
                if ready is not None:
                    pe.wait_ge(*ready(f))
                if f >= 8:
                    pe.wait_ge(parts, f - 7)
                for j, tile in enumerate(tiles):
                    last = pe.transpose(ps[f % 8][:, j * P:(j + 1) * P], src[:, tile, f * P:(f + 1) * P], ident)
                last.then_inc(turned, 1)

        def outT_hi(act, tiles, f, turned, hi_out, scale=1.0):
            lo, n = tiles[0] * P, len(tiles) * P
            act.wait_ge(turned, f + 1)
            act.activation(outT[0][:, f, lo:lo + n], ps[f % 8][:, 0:n], ACT.Identity if not isinstance(scale, float) else ACT.Copy,
                           scale=scale).then_inc(hi_out, 1)

        def outT_lo(dve, tiles, f, hi_out, parts, scale=1.0):
            lo, n = tiles[0] * P, len(tiles) * P
            dve.wait_ge(hi_out, f + 1)
            dve.scalar_tensor_tensor(outT[1][:, f, lo:lo + n], ps[f % 8][:, 0:n], scale,
                                     outT[0][:, f, lo:lo + n].bitcast(F32), ALU.mult, ALU.subtract).then_inc(parts, 1)

        def ssm_gate(l, tiles):
            a0, b0 = span[f"z{l}"]
            y = ssm_tensors()[5]
            gate = at("z_gate", [P, NT, 512], F32, work + 16384)
            junk = at("squares_junk", [P, 512], F32, work + 24576)
            gated, silu_out, squared, roots, scaled, turned, hi_out, parts = (
                stage_sem(s) for s in ("gated", "silu_out", "squared", "roots", "scaled", "turned", "hi_out", "parts"))
            ssq = small[:, 8:16]
            n = len(tiles)
            lo = 2 * tiles[0]
            with nc.Block() as block:
                @block.sync
                def _(sp):
                    loads(sp, f"z{l}")

                @block.gpsimd
                def _(pool):
                    splits_lo(pool, f"z{l}")

                @block.scalar
                def _(act):
                    for g in range(SG):
                        for u in range(2):
                            split_hi(act, a0 + 2 * g + u + 2)
                        act.wait_ge(unit_used, a0 + 2 * g + 2)
                        if g:
                            act.wait_ge(gated, n)
                        for j in range(n):
                            act.activation(gate[:, j, :], ps[4 * g + j][:, :], ACT.Silu).then_inc(silu_out, 1)
                        for j, tile in enumerate(tiles):
                            act.wait_ge(gated, n * g + j + 1)
                            act_step(act, act.activation(junk[:, :], y[:, tile, g * 512:(g + 1) * 512], ACT.Square,
                                                         accum_out=ssq[:, 2 * tile + g:2 * tile + g + 1]))
                    act.activation(small[:, 16:17], small[:, 0:1], ACT.Copy).then_inc(squared, 1)
                    act.wait_ge(roots, 1)
                    act.activation(ssq[:, lo:8], ssq[:, lo:8], ACT.Sqrt).then_inc(roots, 1)
                    for f in range(KD):
                        outT_hi(act, tiles, f, turned, hi_out, norm_cols[l][:, 16 + f:17 + f])

                @block.vector
                def _(dve):
                    for g in range(SG):
                        for j, tile in enumerate(tiles):
                            dve.wait_ge(silu_out, n * g + j + 1)
                            yo = y[:, tile, g * 512:(g + 1) * 512]
                            dve.tensor_tensor(yo, yo, gate[:, j, :], ALU.mult).then_inc(gated, 1)
                    dve.wait_ge(squared, 1)
                    dve.tensor_scalar(ssq[:, lo:8], ssq[:, lo:8], 1.0 / 512, EPS, ALU.mult, ALU.add).then_inc(roots, 1)
                    dve.wait_ge(roots, 2)
                    dve_step(dve, dve.reciprocal(ssq[:, lo:8], ssq[:, lo:8]))
                    for g in range(SG):
                        for tile in tiles:
                            yo = y[:, tile, g * 512:(g + 1) * 512]
                            ins = dve.tensor_scalar(yo, yo, ssq[:, 2 * tile + g:2 * tile + g + 1], None, ALU.mult)
                        ins.then_inc(scaled, 1)
                    for f in range(KD):
                        outT_lo(dve, tiles, f, hi_out, parts, norm_cols[l][:, 16 + f:17 + f])

                @block.tensor
                def _(pe):
                    for g in range(SG):
                        project(pe, a0 + 2 * g, [4 * g + j for j in range(n)], tiles)
                    turn_to_outT(pe, y, tiles, range(KD), lambda f: (scaled, f // 4 + 1), turned, parts)
            end_stage()

        def merge(l, branch, tiles, first):
            a0, b0 = span[f"merge{branch}_{l}"]
            gate = at("merge_gate", [P, 2, NT, 512], F32, work)
            part = at("merge_part", [P, 2, 512], F32, work + 16384)
            gate_out, merged_out = stage_sem("gate_out"), stage_sem("merged_out")
            n = len(tiles)
            with nc.Block() as block:
                @block.sync
                def _(sp):
                    loads(sp, f"merge{branch}_{l}")

                @block.gpsimd
                def _(pool):
                    splits_lo(pool, f"merge{branch}_{l}")

                @block.scalar
                def _(act):
                    for b in range(2):
                        for u in range(2):
                            split_hi(act, a0 + 4 * b + u + 2)
                        act.wait_ge(unit_used, a0 + 4 * b + 2)
                        for j in range(n):
                            act.activation(gate[:, b, j, :], ps[j][:, :], ACT.Sigmoid).then_inc(gate_out, 1)
                        for u in range(2, 4):
                            split_hi(act, a0 + 4 * b + u + 2)

                @block.vector
                def _(dve):
                    for b in range(2):
                        dve.wait_ge(unit_used, a0 + 4 * b + 4)
                        for j, tile in enumerate(tiles):
                            dve.wait_ge(gate_out, n * b + j + 1)
                            out = merged[:, tile, b * 512:(b + 1) * 512]
                            if first:
                                dve.tensor_tensor(out, gate[:, b, j, :], ps[4 + j][:, :], ALU.mult).then_inc(merged_out, 1)
                            else:
                                pt = part[:, j % 2, :]
                                dve_step(dve, dve.tensor_tensor(pt, gate[:, b, j, :], ps[4 + j][:, :], ALU.mult))
                                dve.tensor_tensor(out, out, pt, ALU.add).then_inc(merged_out, 1)

                @block.tensor
                def _(pe):
                    for b in range(2):
                        if b:
                            pe.wait_ge(gate_out, n)
                        project(pe, a0 + 4 * b, range(n), tiles)
                        if b:
                            pe.wait_ge(merged_out, n)
                        project(pe, a0 + 4 * b + 2, [4 + j for j in range(n)], tiles, outT)
            end_stage()

        def rope(dve, out, src, tile, table, n_heads, tmp, axial):
            half = 32 if axial else 64
            pairs = n_heads * (2 if axial else 1)

            def parts(a):
                v = a.rearrange("p (h e w) -> p h e w", e=2, w=half)
                return v[:, :, 0, :], v[:, :, 1, :]

            def angle(kind):
                a = const(f"{table}_{kind}")[:, 64 * (tile - 2):64 * (tile - 1)]
                if axial:
                    return a.rearrange("p (e w) -> p e w", w=half).unsqueeze(1).to_broadcast([P, n_heads, 2, half])
                return a.unsqueeze(1).to_broadcast([P, n_heads, half])

            def shaped(a):
                return a.rearrange("p (h e) w -> p h e w", e=2) if axial else a

            w = pairs * half
            s1, s2 = (shaped(v) for v in parts(src))
            o1, o2 = (shaped(v) for v in parts(out))
            m = [shaped(tmp[:, i, 0:w].rearrange("p (h w) -> p h w", w=half)) for i in range(4)]
            cos, sin = angle("cos"), angle("sin")
            dve.tensor_tensor(m[0], s1, cos, ALU.mult)
            dve.tensor_tensor(m[1], s2, sin, ALU.mult)
            dve.tensor_tensor(m[2], s1, sin, ALU.mult)
            dve_step(dve, dve.tensor_tensor(m[3], s2, cos, ALU.mult))
            dve.tensor_tensor(o1, m[0], m[1], ALU.subtract)
            return dve.tensor_tensor(o2, m[2], m[3], ALU.add)

        def ret_tensors():
            ktok = at("k_tok", [P, NT, RH * DK], F32, work)
            qT = at("ret_qT", [P, RH, TOK], F32, work + 8192)
            kT = at("ret_kT", [P, RH, TOK], F32, work + 16384)
            o = at("ret_o", [P, NT, D], F32, work + 24576)
            qtok = at("q_tok", [P, NT, RH * DK], F32, work + 40960)
            v = at("ret_v", [P, NT, D], F32, outT_at)
            return ktok, qT, kT, o, qtok, v

        def ret_project(l, q_tiles):
            a0, b0 = span[f"ret{l}"]
            ktok, qT, kT, o, qtok, v = ret_tensors()
            tmp = at("rope_tmp", [P, 4, 256], F32, outT_at + 16384)
            out, turned, turned_out = stage_sem("out"), stage_sem("turned"), stage_sem("turned_out")
            blocks = [q_tiles, ALL_TILES, ALL_TILES, ALL_TILES]
            done = np.cumsum([len(b) for b in blocks]).tolist()
            banks = [[4 * (n % 2) + j for j in range(len(b))] for n, b in enumerate(blocks)]
            with nc.Block() as block:
                @block.sync
                def _(sp):
                    loads(sp, f"ret{l}")

                @block.gpsimd
                def _(pool):
                    splits_lo(pool, f"ret{l}")

                @block.scalar
                def _(act):
                    for n in range(4):
                        for u in range(2):
                            split_hi(act, a0 + 2 * n + u + 2)
                        if n >= 2:
                            act.wait_ge(unit_used, a0 + 2 * n + 2)
                            act.wait_ge(out, done[n - 1])
                            for j, tile in enumerate(blocks[n]):
                                act.activation(v[:, tile, (n - 2) * 512:(n - 1) * 512], ps[banks[n][j]][:, :],
                                               ACT.Copy).then_inc(out, 1)
                    for i in range(2 * RH):
                        act.wait_ge(turned, i + 1)
                        dst, h = (qT, i) if i < RH else (kT, i - RH)
                        lo = q_tiles[0] * P if i < RH else 0
                        act.activation(dst[:, h, lo:TOK], ps[i][:, 0:TOK - lo], ACT.Copy).then_inc(turned_out, 1)

                @block.vector
                def _(dve):
                    for n, (dst, table) in enumerate(((qtok, "rq"), (ktok, "rk"))):
                        dve.wait_ge(unit_used, a0 + 2 * n + 2)
                        for j, tile in enumerate(blocks[n]):
                            src = ps[banks[n][j]][:, :]
                            if tile < 2:
                                scale = 1.0 if n == 0 else DK ** -0.5
                                dve.tensor_scalar(dst[:, tile, :], src, scale, None, ALU.mult).then_inc(out, 1)
                            else:
                                rope(dve, dst[:, tile, :], src, tile, table, RH, tmp, False).then_inc(out, 1)
                                dve.wait_ge(out, (done[n - 1] if n else 0) + j + 1)

                @block.tensor
                def _(pe):
                    for n in range(4):
                        if n >= 2:
                            pe.wait_ge(out, done[n - 2])
                        project(pe, a0 + 2 * n, banks[n], blocks[n])
                    pe.wait_ge(out, done[3])
                    for i in range(2 * RH):
                        src, h, tiles = (qtok, i, q_tiles) if i < RH else (ktok, i - RH, ALL_TILES)
                        for j, tile in enumerate(tiles):
                            last = pe.transpose(ps[i][:, j * P:(j + 1) * P], src[:, tile, h * DK:(h + 1) * DK], ident)
                        last.then_inc(turned, 1)
            end_stage()

        def ret_mix(l, tiles):
            ktok, qT, kT, o, qtok, v = ret_tensors()
            base = outT_at + 16384
            decay = at("ret_decays", [P, RH, P], F32, base)
            state = at("ret_state", [P, 2, RH, DV], F32, base + 2048)
            kw = at("k_weighted", [P, RH * DK], F32, base + 10240)
            part = at("ret_part", [P, 2, 512], F32, base + 12288)
            mix = at("ret_mix", [P, 2, RH * P], F32, work + 40960)
            logs, t1, t2 = small[:, 20:28], small[:, 28:36], small[:, 36:44]
            wts, gam = small[:, 48:80], small[:, 80:88]
            names = ("lg_dve", "lg_act", "exps_done", "decay_done", "scores", "mixed", "intra", "intra_out",
                     "weighted", "update", "update_out", "inter", "inter_out")
            (lg_dve, lg_act, exps_done, decay_done, scores, mixed, intra, intra_out,
             weighted, update, update_out, inter, inter_out) = (stage_sem(s) for s in names)
            n = len(tiles)
            steps = [(s, d) for s in range(NT) for d in range(2)]
            tmp = at("decay_exps", [P, 8, P], F32, work + 45056)

            def w_of(kind, d):
                return wts[:, kind * 8 + d * 4:kind * 8 + d * 4 + 4]

            with nc.Block() as block:
                @block.scalar
                def _(act):
                    act.wait_ge(lg_dve, 1)
                    act.activation(t2, t1, ACT.Exp, scale=-1.0).then_inc(lg_act, 1)
                    act.wait_ge(lg_dve, 2)
                    act.activation(t2, t2, ACT.Ln).then_inc(lg_act, 1)
                    act.wait_ge(lg_dve, 3)
                    for d in range(2):
                        for h in range(RH):
                            act.activation(tmp[:, 4 * d + h, :], const("dist_f" if d == 0 else "dist_b"), ACT.Exp,
                                           scale=logs[:, 4 * d + h:4 * d + h + 1])
                    for kind in range(4):
                        act.activation(wts[:, kind * 8:kind * 8 + 8], logs, ACT.Exp,
                                       scale=const("ret_w")[:, kind:kind + 1])
                    act.activation(gam, logs, ACT.Exp, scale=float(P)).then_inc(exps_done, 1)
                    for j, tile in enumerate(tiles):
                        for b in range(2):
                            act.wait_ge(intra, 2 * j + b + 1)
                            act.activation(o[:, tile, b * 512:(b + 1) * 512], ps[2 + b][:, :], ACT.Copy).then_inc(intra_out, 1)

                @block.vector
                def _(dve):
                    r = heads[l][:, 0:8]
                    dve.scalar_tensor_tensor(t1, r, -1.0, r, ALU.mult, ALU.max).then_inc(lg_dve, 1)
                    dve.wait_ge(lg_act, 1)
                    dve.tensor_scalar(t2, t2, 1.0, None, ALU.add).then_inc(lg_dve, 1)
                    dve.wait_ge(lg_act, 2)
                    dve.scalar_tensor_tensor(logs, r, 0.0, t2, ALU.min, ALU.subtract).then_inc(lg_dve, 1)
                    dve.wait_ge(exps_done, 1)
                    for d in range(2):
                        tri = const("tri_f" if d == 0 else "tri_b").unsqueeze(1).to_broadcast([P, RH, P])
                        dve_step(dve, dve.tensor_tensor(tmp[:, 4 * d:4 * d + 4, :], tmp[:, 4 * d:4 * d + 4, :], tri, ALU.mult))
                    dve.tensor_tensor(decay[:, :, :], tmp[:, 0:4, :], tmp[:, 4:8, :], ALU.add).then_inc(decay_done, 1)
                    dve.wait_ge(decay_done, 1)
                    for j, tile in enumerate(tiles):
                        dve.wait_ge(scores, j + 1)
                        dve.tensor_tensor(mix[:, j % 2, :], ps[j % 2][:, :], decay[:, :, :].rearrange("p h i -> p (h i)"),
                                          ALU.mult).then_inc(mixed, 1)
                    n_in = n_up = 0
                    for s, d in steps:
                        tile = ORDER[d][s]
                        if s < NT - 1:
                            if n_up:
                                dve.wait_ge(update, n_up)
                            dve.tensor_tensor(kw[:, :].rearrange("p (h e) -> p h e", h=RH),
                                              ktok[:, tile, :].rearrange("p (h e) -> p h e", h=RH),
                                              spread(w_of(d, d), RH, DK), ALU.mult).then_inc(weighted, 1)
                        if s > 0 and tile in tiles:
                            if n_in == 0:
                                dve.wait_ge(intra_out, 2 * n)
                            for b in range(2):
                                dve.wait_ge(inter, n_in + 1)
                                pt = part[:, b, :]
                                dve_step(dve, dve.tensor_tensor(pt.rearrange("p (h e) -> p h e", h=2),
                                                                ps[4 + b][:, :].rearrange("p (h e) -> p h e", h=2),
                                                                spread(w_of(2 + d, d)[:, 2 * b:2 * b + 2], 2, DV), ALU.mult))
                                oo = o[:, tile, b * 512:(b + 1) * 512]
                                dve.tensor_tensor(oo, oo, pt, ALU.add).then_inc(inter_out, 1)
                                n_in += 1
                        if s < NT - 1:
                            dve.wait_ge(update, n_up + 1)
                            for h in range(RH):
                                st = state[:, d, h, :]
                                u = ps[6 + h // 2][:, (h % 2) * DV:(h % 2 + 1) * DV]
                                if s:
                                    ins = dve.scalar_tensor_tensor(st, st, gam[:, 4 * d + h:4 * d + h + 1], u, ALU.mult, ALU.add)
                                else:
                                    ins = dve.tensor_copy(st, u)
                            ins.then_inc(update_out, 1)
                            n_up += 1

                @block.tensor
                def _(pe):
                    for j in range(n + 1):
                        if j < n:
                            tok = slice(tiles[j] * P, (tiles[j] + 1) * P)
                            if j >= 2:
                                pe.wait_ge(mixed, j - 1)
                            for h in range(RH):
                                last = pe.matmul(ps[j % 2][:, h * P:(h + 1) * P], kT[:, h, tok], qT[:, h, tok], start=True, stop=True)
                            last.then_inc(scores, 1)
                        if j >= 1:
                            tile = tiles[j - 1]
                            pe.wait_ge(mixed, j)
                            for b in range(2):
                                if j >= 2:
                                    pe.wait_ge(intra_out, 2 * (j - 2) + b + 1)
                                for h in (2 * b, 2 * b + 1):
                                    last = pe.matmul(ps[2 + b][:, (h % 2) * DV:(h % 2 + 1) * DV],
                                                     mix[:, (j - 1) % 2, h * P:(h + 1) * P],
                                                     v[:, tile, h * DV:(h + 1) * DV], start=True, stop=True)
                                last.then_inc(intra, 1)
                    n_in = n_up = 0
                    for s, d in steps:
                        tile = ORDER[d][s]
                        if s > 0 and tile in tiles:
                            pe.wait_ge(update_out, 2 * (s - 1) + d + 1)
                            for b in range(2):
                                if n_in >= 2:
                                    pe.wait_ge(inter_out, n_in - 1)
                                for h in (2 * b, 2 * b + 1):
                                    last = pe.matmul(ps[4 + b][:, (h % 2) * DV:(h % 2 + 1) * DV],
                                                     qT[:, h, tile * P:(tile + 1) * P], state[:, d, h, :], start=True, stop=True)
                                last.then_inc(inter, 1)
                                n_in += 1
                        if s < NT - 1:
                            pe.wait_ge(weighted, n_up + 1)
                            if n_up:
                                pe.wait_ge(update_out, n_up)
                            for h in range(RH):
                                last = pe.matmul(ps[6 + h // 2][:, (h % 2) * DV:(h % 2 + 1) * DV],
                                                 kw[:, h * DK:(h + 1) * DK], v[:, tile, h * DV:(h + 1) * DV], start=True, stop=True)
                            last.then_inc(update, 1)
                            n_up += 1
            end_stage()

        def ret_gate(l, tiles):
            a0, b0 = span[f"g{l}"]
            o = ret_tensors()[3]
            gate = at("ret_silu", [P, NT, 512], F32, work)
            junk = at("ret_junk", [P, DV], F32, work + 8192)
            squared, roots, silu_out, gated, turned, hi_out, parts = (
                stage_sem(s) for s in ("squared", "roots", "silu_out", "gated", "turned", "hi_out", "parts"))
            ssq = small[:, 0:16]
            n, lo = len(tiles), 4 * tiles[0]
            with nc.Block() as block:
                @block.sync
                def _(sp):
                    loads(sp, f"g{l}")

                @block.gpsimd
                def _(pool):
                    splits_lo(pool, f"g{l}")

                @block.scalar
                def _(act):
                    for tile in tiles:
                        for h in range(RH):
                            ins = act.activation(junk[:, :], o[:, tile, h * DV:(h + 1) * DV], ACT.Square,
                                                 accum_out=ssq[:, 4 * tile + h:4 * tile + h + 1])
                            act_step(act, ins)
                    act.activation(small[:, 16:17], small[:, lo:lo + 1], ACT.Copy).then_inc(squared, 1)
                    act.wait_ge(roots, 1)
                    act.activation(ssq[:, lo:16], ssq[:, lo:16], ACT.Sqrt).then_inc(roots, 1)
                    for b in range(2):
                        for u in range(2):
                            split_hi(act, a0 + 2 * b + u + 2)
                        act.wait_ge(unit_used, a0 + 2 * b + 2)
                        if b:
                            act.wait_ge(gated, n)
                        for j in range(n):
                            act.activation(gate[:, j, :], ps[4 * b + j][:, :], ACT.Silu).then_inc(silu_out, 1)
                    for f in range(KD):
                        outT_hi(act, tiles, f, turned, hi_out)

                @block.vector
                def _(dve):
                    dve.wait_ge(squared, 1)
                    dve.tensor_scalar(ssq[:, lo:16], ssq[:, lo:16], 1.0 / DV, EPS, ALU.mult, ALU.add).then_inc(roots, 1)
                    dve.wait_ge(roots, 2)
                    dve_step(dve, dve.reciprocal(ssq[:, lo:16], ssq[:, lo:16]))
                    for b in range(2):
                        for j, tile in enumerate(tiles):
                            dve.wait_ge(silu_out, n * b + j + 1)
                            for h in range(2):
                                hh = 2 * b + h
                                oo = o[:, tile, hh * DV:(hh + 1) * DV]
                                ins = dve.scalar_tensor_tensor(oo, oo, ssq[:, 4 * tile + hh:4 * tile + hh + 1],
                                                               gate[:, j, h * DV:(h + 1) * DV], ALU.mult, ALU.mult)
                            ins.then_inc(gated, 1)
                    for f in range(KD):
                        outT_lo(dve, tiles, f, hi_out, parts)

                @block.tensor
                def _(pe):
                    for b in range(2):
                        project(pe, a0 + 2 * b, [4 * b + j for j in range(n)], tiles)
                    turn_to_outT(pe, o, tiles, range(KD), lambda f: (gated, n * (f // 4 + 1)), turned, parts)
            end_stage()

        def att_tensors():
            qT = at("att_qT", [P, AH, TOK], F32, work)
            kT = at("att_kT", [P, KVH, TOK], F32, work + 16384)
            v = at("att_v", [P, NT, KVH * AD], F32, work + 20480)
            tok = at("att_tok", [P, NT, 512], F32, work + 24576)
            return qT, kT, v, tok

        def att_project(l, q_tiles):
            a0, b0 = span[f"att{l}"]
            qT, kT, v, tok = att_tensors()
            tmp = at("att_rope_tmp", [P, 4, 256], F32, work + 32768)
            out, turned, turned_out = stage_sem("out"), stage_sem("turned"), stage_sem("turned_out")
            blocks = [q_tiles, q_tiles, ALL_TILES]
            heads_of = [4, 4, 2]
            done = np.cumsum([len(b) for b in blocks]).tolist()
            turns = [0, 4, 8, 10]
            bank0 = [0, 4, 0]
            with nc.Block() as block:
                @block.sync
                def _(sp):
                    loads(sp, f"att{l}")

                @block.gpsimd
                def _(pool):
                    splits_lo(pool, f"att{l}")

                @block.scalar
                def _(act):
                    for n in range(3):
                        for u in range(2):
                            split_hi(act, a0 + 2 * n + u + 2)
                        for i in range(turns[n], turns[n + 1]):
                            m = i - turns[n]
                            act.wait_ge(turned, i + 1)
                            dst = qT[:, i, :] if n < 2 else kT[:, m, :]
                            lo = q_tiles[0] * P if n < 2 else 0
                            act.activation(dst[:, lo:TOK], ps[bank0[n] + m][:, 0:TOK - lo], ACT.Copy).then_inc(turned_out, 1)

                @block.vector
                def _(dve):
                    for n in range(3):
                        w = heads_of[n] * AD
                        dve.wait_ge(unit_used, a0 + 2 * n + 2)
                        if n:
                            dve.wait_ge(turned, turns[n])
                        for j, tile in enumerate(blocks[n]):
                            src = ps[bank0[n] + j]
                            if n == 2:
                                dve.tensor_copy(v[:, tile, :], src[:, 256:512])
                            if tile < 2:
                                dve.tensor_scalar(tok[:, tile, 0:w], src[:, 0:w], AD ** -0.5 if n < 2 else 1.0, None,
                                                  ALU.mult).then_inc(out, 1)
                            else:
                                rope(dve, tok[:, tile, 0:w], src[:, 0:w], tile, "aq" if n < 2 else "ak", heads_of[n],
                                     tmp, True).then_inc(out, 1)
                                dve.wait_ge(out, (done[n - 1] if n else 0) + j + 1)

                @block.tensor
                def _(pe):
                    for n in range(3):
                        if n == 2:
                            pe.wait_ge(turned_out, turns[1])
                        project(pe, a0 + 2 * n, [bank0[n] + j for j in range(len(blocks[n]))], blocks[n])
                        pe.wait_ge(out, done[n])
                        for i in range(turns[n], turns[n + 1]):
                            m = i - turns[n]
                            for j, tile in enumerate(blocks[n]):
                                last = pe.transpose(ps[bank0[n] + m][:, j * P:(j + 1) * P], tok[:, tile, m * AD:(m + 1) * AD], ident)
                            last.then_inc(turned, 1)
            end_stage()

        def att_mix(l, tiles):
            qT, kT, v, tok = att_tensors()
            pr = at("att_probs", [P, 2, AG, 512], F32, work + 24576)
            pT = at("att_probs_T", [P, NT, AG * P], F32, work + 40960)
            scores, maxed, summed, normed, turned, turned_out, summed_v, hi_out, parts = (
                stage_sem(s) for s in ("scores", "maxed", "summed", "normed", "turned", "turned_out", "summed_v", "hi_out", "parts"))
            sink = heads[l][:, 104:112]
            jobs = [(tile, kv) for tile in tiles for kv in range(KVH)]

            def sc(i, job):
                a = 32 + 16 * (job % 2) + 4 * i
                return small[:, a:a + 4]

            def keys(tile):
                return 2 if tile < 2 else NT

            with nc.Block() as block:
                @block.scalar
                def _(act):
                    for n, (tile, kv) in enumerate(jobs):
                        w = keys(tile) * P
                        act.wait_ge(maxed, n + 1)
                        for h in range(AG):
                            act.activation(pr[:, n % 2, h, 0:w], ps[h][:, 0:w], ACT.Exp, bias=sc(0, n)[:, h:h + 1],
                                           accum_out=sc(2, n)[:, h:h + 1])
                        act.activation(sc(1, n), sc(1, n), ACT.Exp).then_inc(summed, 1)
                        act.wait_ge(summed_v, n + 1)
                        act.activation(outT[0][:, 4 * kv:4 * kv + 4, tile * P:(tile + 1) * P],
                                       ps[6 + n % 2][:, :].rearrange("p (h t) -> p h t", h=AG), ACT.Copy).then_inc(hi_out, 1)

                @block.vector
                def _(dve):
                    def tail(n):
                        tile, kv = jobs[n]
                        dve.wait_ge(hi_out, n + 1)
                        s = slice(tile * P, (tile + 1) * P)
                        dve.tensor_tensor(outT[1][:, 4 * kv:4 * kv + 4, s], ps[6 + n % 2][:, :].rearrange("p (h t) -> p h t", h=AG),
                                          outT[0][:, 4 * kv:4 * kv + 4, s].bitcast(F32), ALU.subtract).then_inc(parts, 1)

                    n_turn = 0
                    for n, (tile, kv) in enumerate(jobs):
                        nk = keys(tile)
                        w = nk * P
                        dve.wait_ge(scores, n + 1)
                        if tile >= 2:
                            other = 5 - tile
                            for h in range(AG):
                                s = ps[h][:, other * P:(other + 1) * P]
                                ins = dve.tensor_tensor(s, s, const("neg_up" if tile == 2 else "neg_low"), ALU.add)
                            dve_step(dve, ins)
                        mx = sc(0, n)
                        for h in range(AG):
                            ins = dve.tensor_reduce(mx[:, h:h + 1], ps[h][:, 0:w], AX.X, ALU.max)
                        dve_step(dve, ins)
                        sk = sink[:, 4 * kv:4 * kv + 4]
                        dve_step(dve, dve.tensor_tensor(mx, mx, sk, ALU.max))
                        dve_step(dve, dve.tensor_tensor(sc(1, n), sk, mx, ALU.subtract))
                        dve.tensor_scalar(mx, mx, -1.0, None, ALU.mult).then_inc(maxed, 1)
                        dve.wait_ge(summed, n + 1)
                        dve_step(dve, dve.tensor_tensor(sc(2, n), sc(2, n), sc(1, n), ALU.add))
                        dve_step(dve, dve.reciprocal(sc(2, n), sc(2, n)))
                        for h in range(AG):
                            ins = dve.tensor_scalar(pr[:, n % 2, h, 0:w], pr[:, n % 2, h, 0:w], sc(2, n)[:, h:h + 1], None, ALU.mult)
                        ins.then_inc(normed, 1)
                        if n:
                            dve.wait_ge(summed_v, n)
                        for k in range(nk):
                            dve.wait_ge(turned, n_turn + 1)
                            dve.tensor_copy(pT[:, k, :], ps[4 + k % 2][:, :]).then_inc(turned_out, 1)
                            n_turn += 1
                        if n:
                            tail(n - 1)
                    tail(len(jobs) - 1)

                @block.tensor
                def _(pe):
                    n_turn = 0
                    for n, (tile, kv) in enumerate(jobs):
                        nk = keys(tile)
                        if n:
                            pe.wait_ge(summed, n)
                        for h in range(AG):
                            last = pe.matmul(ps[h][:, 0:nk * P], qT[:, AG * kv + h, tile * P:(tile + 1) * P],
                                             kT[:, kv, 0:nk * P], start=True, stop=True)
                        last.then_inc(scores, 1)
                        pe.wait_ge(normed, n + 1)
                        for k in range(nk):
                            if n_turn >= 2:
                                pe.wait_ge(turned_out, n_turn - 1)
                            for h in range(AG):
                                last = pe.transpose(ps[4 + k % 2][:, h * P:(h + 1) * P], pr[:, n % 2, h, k * P:(k + 1) * P], ident)
                            last.then_inc(turned, 1)
                            n_turn += 1
                        if n >= 2:
                            pe.wait_ge(parts, n - 1)
                        pe.wait_ge(turned_out, n_turn)
                        for k in range(nk):
                            last = pe.matmul(ps[6 + n % 2][:, :], v[:, k, kv * AD:(kv + 1) * AD], pT[:, k, :],
                                             start=k == 0, stop=k == nk - 1)
                        last.then_inc(summed_v, 1)
            end_stage()

        def post_rows_pe(pe, l, which, conds, rows_sum, rows_out, banks):
            for i, c in enumerate(conds):
                for half in range(2):
                    m = 2 * i + half
                    if m >= len(banks):
                        pe.wait_ge(rows_out, m - len(banks) + 1)
                    for d in range(4):
                        w = gains[l][:, 2 + which, 4 * half + d, c:c + 1].to_broadcast([P, P])
                        last = pe.matmul(ps[banks[m % len(banks)]][:, d * P:(d + 1) * P], w, ident, start=True, stop=True)
                    last.then_inc(rows_sum, 1)

        def post_rows_act(act, rows, conds, rows_sum, rows_out, banks):
            for i, c in enumerate(conds):
                for half in range(2):
                    m = 2 * i + half
                    act.wait_ge(rows_sum, m + 1)
                    act.activation(rows[:, c, half * 512:(half + 1) * 512], ps[banks[m % len(banks)]][:, :],
                                   ACT.Copy).then_inc(rows_out, 1)

        def post_norm_act(act, yb, tiles, ssq, junk, y_out, squared, roots):
            for j, tile in enumerate(tiles):
                act.wait_ge(y_out, 2 * j + 2)
                act_step(act, act.activation(junk[:, :], yb[:, tile, :], ACT.Square, accum_out=ssq[:, tile:tile + 1]))
            act.activation(small[:, 126:127], small[:, 125:126], ACT.Copy).then_inc(squared, 1)
            act.wait_ge(roots, 1)
            lo = tiles[0]
            act.activation(ssq[:, lo:NT], ssq[:, lo:NT], ACT.Sqrt).then_inc(roots, 1)

        def post_norm_dve(dve, yb, rows, tiles, ssq, squared, roots, rows_out, n_rows, x_out):
            lo = tiles[0]
            dve.wait_ge(squared, 1)
            dve.tensor_scalar(ssq[:, lo:NT], ssq[:, lo:NT], 1.0 / D, EPS, ALU.mult, ALU.add).then_inc(roots, 1)
            dve.wait_ge(roots, 2)
            dve_step(dve, dve.reciprocal(ssq[:, lo:NT], ssq[:, lo:NT]))
            dve.wait_ge(rows_out, n_rows)
            for tile in tiles:
                yt = yb[:, tile, :]
                dve_step(dve, dve.scalar_tensor_tensor(yt, yt, ssq[:, tile:tile + 1], rows[:, 1 if tile < 2 else 0, :],
                                                       ALU.mult, ALU.mult))
                dve.tensor_tensor(xres[:, tile, :], xres[:, tile, :], yt, ALU.add).then_inc(x_out, 1)

        def out_project(l, tiles):
            a0, b0 = span[f"out{l}"]
            yb = at("y_out", [P, NT, D], F32, work)
            rows = at("post_rows", [P, 2, D], F32, work + 16384)
            junk = at("post_junk", [P, D], F32, work + 24576)
            conds = [1, 0] if len(tiles) == NT else [0]
            n = len(tiles)
            rows_sum, rows_out, turned, hi_out, parts, y_out, squared, roots, x_out = (
                stage_sem(s) for s in ("rows_sum", "rows_out", "turned", "hi_out", "parts", "y_out", "squared", "roots", "x_out"))
            ssq = small[:, 0:4]
            with nc.Block() as block:
                @block.sync
                def _(sp):
                    loads(sp, f"out{l}")

                @block.gpsimd
                def _(pool):
                    splits_lo(pool, f"out{l}")

                @block.scalar
                def _(act):
                    post_rows_act(act, rows, conds, rows_sum, rows_out, [0, 1, 2, 3])
                    for f in range(KD):
                        outT_hi(act, tiles, f, turned, hi_out)
                    for g in range(a0 + 2, b0 + 2):
                        split_hi(act, g)
                    post_norm_act(act, yb, tiles, ssq, junk, y_out, squared, roots)

                @block.vector
                def _(dve):
                    dve_step(dve, dve.memset(small[:, 125:126], 0.0))
                    for f in range(KD):
                        outT_lo(dve, tiles, f, hi_out, parts)
                    dve.wait_ge(unit_used, a0 + 4)
                    for j, tile in enumerate(tiles):
                        for b in range(2):
                            dve.tensor_copy(yb[:, tile, b * 512:(b + 1) * 512], ps[4 * b + j][:, :]).then_inc(y_out, 1)
                    post_norm_dve(dve, yb, rows, tiles, ssq, squared, roots, rows_out, 2 * len(conds), x_out)

                @block.tensor
                def _(pe):
                    post_rows_pe(pe, l, 0, conds, rows_sum, rows_out, [0, 1, 2, 3])
                    pe.wait_ge(rows_out, 2 * len(conds))
                    turn_to_outT(pe, merged, tiles, range(KD), None, turned, parts)
                    pe.wait_ge(parts, KD)
                    for b in range(2):
                        project(pe, a0 + 2 * b, [4 * b + j for j in range(n)], tiles, outT)
            end_stage()

        def ffn_tensors():
            gT = [at(f"ffn_gT_{n}", [P, FT, TOK], F32R, outT_at + i * FT * TOK * 4) for i, n in enumerate(("hi", "lo"))]
            return gT, outT_at + 2 * FT * TOK * 4

        def ffn_up():
            a0, b0 = span["ffn_up"]
            gT, free = ffn_tensors()
            silu = at("ffn_silu", [P, 2, TOK], F32, free)
            prod = at("ffn_prod", [P, 2, TOK], F32, free + 4096)
            rounds = FF // 256
            silu_out, g_done, chain = stage_sem("silu_out"), stage_sem("g_done"), stage_sem("chain")
            w1, w3, w2 = (t[f"ffn_w{i}"][0].rearrange("(k p) n -> p k n", p=P) for i in (1, 3, 2))

            def flat(buf, g):
                return buf[:, g % 2, :]

            with nc.Block() as block:
                @block.sync
                def _(sp):
                    with sp.Fori(0, rounds - 2) as i:
                        for u, w in enumerate((w1, w3)):
                            g = a0 + 4 + u
                            sp.wait_ge(lo_ready, 2 * i + g - 1)
                            sp.dma_start(view(raw, g), w[:, :, bass.ds((i + 2) * 256, 256)]).then_inc(raw_loaded[g % 2], 16)
                    for g in range(b0, b0 + 4):
                        load_unit(sp, g)

                @block.gpsimd
                def _(pool):
                    with pool.Fori(0, rounds) as i:
                        for g in (a0 + 2, a0 + 3):
                            pool.wait_ge(hi_ready, 2 * i + g + 1)
                            pool.tensor_tensor(flat(wlo, g), flat(raw, g), flat(whi, g).bitcast(F32), ALU.subtract).then_inc(lo_ready, 1)

                @block.scalar
                def _(act):
                    act.sem_inc(silu_out, 2)
                    with act.Fori(0, rounds) as i:
                        for u in range(2):
                            g = a0 + 2 + u
                            act.wait_ge(raw_loaded[g % 2], 16 * (g // 2 + 1) + 16 * i)
                            act.wait_ge(unit_used, 2 * i + g - 1)
                            act.activation(flat(whi, g), flat(raw, g), ACT.Copy).then_inc(hi_ready, 1)
                            if u == 0:
                                for j in range(2):
                                    act.wait_ge(g_done, 2 * i + j + 1)
                                    act.activation(silu[:, j, :], ps[j][:, :], ACT.Silu).then_inc(silu_out, 1)

                @block.vector
                def _(dve):
                    dve.sem_inc(g_done, 2)
                    with dve.Fori(0, rounds) as i:
                        dve.wait_ge(unit_used, 2 * i + a0 + 2)
                        for j in range(2):
                            dve.wait_ge(silu_out, 2 * i + j + 3)
                            dve.tensor_tensor(prod[:, j, :], silu[:, j, :], ps[2 + j][:, :], ALU.mult).then_inc(chain, 1)
                            dve.wait_ge(chain, 4 * i + 2 * j + 1)
                            hi, lo = (g[:, bass.ds(2 * i + j, 1), :].rearrange("p a t -> p (a t)") for g in gT)
                            dve.tensor_copy(hi, prod[:, j, :]).then_inc(chain, 1)
                            dve.wait_ge(chain, 4 * i + 2 * j + 2)
                            dve.tensor_tensor(lo, prod[:, j, :], hi.bitcast(F32), ALU.subtract).then_inc(g_done, 1)

                @block.tensor
                def _(pe):
                    with pe.Fori(0, rounds) as i:
                        for u in range(2):
                            g = a0 + u
                            pe.wait_ge(lo_ready, 2 * i + g + 1)
                            pe.wait_ge(silu_out if u == 0 else g_done, 2 * i + 2)
                            wh, wl = view(whi, g), view(wlo, g)
                            for j in range(2):
                                for k in range(KD):
                                    a = [wh[:, k, j * P:(j + 1) * P], wl[:, k, j * P:(j + 1) * P]]
                                    last = three(pe, ps[2 * u + j][:, :], a, [h[:, k, :] for h in hT], k == 0, k == KD - 1)
                            last.then_inc(unit_used, 1)
            end_stage()

        def ffn_down(l):
            a0, b0 = span["ffn_down"]
            gT, free = ffn_tensors()
            yb = at("ffn_y", [P, NT, D], F32, hT_at)
            rows = at("ffn_rows", [P, 2, D], F32, hT_at + 16384)
            junk = at("ffn_junk", [P, D], F32, hT_at + 24576)
            rows_sum, rows_out, y_out, squared, roots, x_out = (
                stage_sem(s) for s in ("rows_sum", "rows_out", "y_out", "squared", "roots", "x_out"))
            ssq = small[:, 0:4]
            with nc.Block() as block:
                @block.sync
                def _(sp):
                    loads(sp, "ffn_down")

                @block.gpsimd
                def _(pool):
                    splits_lo(pool, "ffn_down")

                @block.scalar
                def _(act):
                    post_rows_act(act, rows, [1, 0], rows_sum, rows_out, [0, 1, 2, 3])
                    for g in range(a0 + 2, b0 + 2):
                        split_hi(act, g)
                    post_norm_act(act, yb, ALL_TILES, ssq, junk, y_out, squared, roots)

                @block.vector
                def _(dve):
                    dve.wait_ge(unit_used, b0)
                    for tile in ALL_TILES:
                        for b in range(2):
                            dve.tensor_copy(yb[:, tile, b * 512:(b + 1) * 512], ps[2 * tile + b][:, :]).then_inc(y_out, 1)
                    post_norm_dve(dve, yb, rows, ALL_TILES, ssq, squared, roots, rows_out, 4, x_out)

                @block.tensor
                def _(pe):
                    post_rows_pe(pe, l, 1, [1, 0], rows_sum, rows_out, [0, 1, 2, 3])
                    pe.wait_ge(rows_out, 4)
                    for g in range(a0, b0):
                        pe.wait_ge(lo_ready, g + 1)
                        wh, wl = view(whi, g), view(wlo, g)
                        for k in range(2):
                            kk = 2 * (g - a0) + k
                            for tile in ALL_TILES:
                                a = [x[:, kk, tile * P:(tile + 1) * P] for x in gT]
                                for b in range(2):
                                    s = slice(b * 512, (b + 1) * 512)
                                    last = three(pe, ps[2 * tile + b][:, :], a, [wh[:, k, s], wl[:, k, s]],
                                                 kk == 0, kk == FT - 1)
                        last.then_inc(unit_used, 1)
            end_stage()

        R0 = ring_at
        moe_raw = at("moe_raw", [P, 3, 2048], F32, R0)
        moe_hi = at("moe_unit_hi", [P, 3, 2048], F32R, R0 + 24576)
        moe_lo = at("moe_unit_lo", [P, 3, 2048], F32R, R0 + 2 * 24576)
        M0 = R0 + 80 * 1024
        htok = [at(f"moe_h_{n}", [P, 2, D], F32R, M0 + 8192 * i) for i, n in enumerate(("hi", "lo"))]
        route = at("moe_route", [P, 3, 2, 2 * NE + 1], F32, M0 + 16384)
        n_pass = at("moe_passes", [P, 1], mybir.dt.int32, M0 + 16384 + 448)
        slot_of, chosen, weight = route[:, 0, :, :], route[:, 1, :, :], route[:, 2, :, :]

        def moe_route(l):
            rows = at("moe_rows", [P, 2, D], F32, work)
            xn = at("moe_xn", [P, 2, D], F32, work + 8192)
            wr = at("router", [P, KD, NE], F32, work + 16384)
            wr2 = [at(f"router_{n}", [P, KD, NE], F32R, work + 16640 + 256 * i) for i, n in enumerate(("hi", "lo"))]
            lg = at("logits", [P, 2, NE], F32, work + 17152)
            cmp = at("compare", [P, 2, 2, NE * NE], F32, work + 17280)
            sc = at("route_scratch", [P, 64], F32, work + 18304)
            names = ("router_in", "squares", "roots", "rows_sum", "rows_out", "h_done", "turned", "hi_out", "parts",
                     "logits_sum", "logits_out", "exps", "sel_done", "counted")
            (router_in, squares, roots, rows_sum, rows_out, h_done, turned, hi_out, parts,
             logits_sum, logits_out, exps, sel_done, counted) = (stage_sem(s) for s in names)
            ssq = small[:, 0:2]
            negm, ssum, most = sc[:, 0:2], sc[:, 2:4], sc[:, 4:5]
            ex = sc[:, 16:32].rearrange("p (j e) -> p j e", j=2)
            sel = sc[:, 32:48].rearrange("p (j e) -> p j e", j=2)
            gain, shift = gains[l][:, 1, :, 0:1], mods[l][:, 24:32, 0:1]
            with nc.Block() as block:
                @block.sync
                def _(sp):
                    sp.dma_start(wr[:, :, :], t["moe_router"][0].rearrange("(k p) n -> p k n", p=P)).then_inc(router_in, 16)
                    sp.wait_ge(router_in, 16)

                @block.scalar
                def _(act):
                    for j in range(2):
                        act.activation(xn[:, j, :], xres[:, 2 + j, :], ACT.Square, accum_out=ssq[:, j:j + 1]).then_inc(squares, 1)
                    act.wait_ge(roots, 1)
                    act.activation(ssq, ssq, ACT.Sqrt).then_inc(roots, 1)
                    for m in range(4):
                        act.wait_ge(rows_sum, m + 1)
                        act.activation(rows[:, m // 2, (m % 2) * 512:(m % 2 + 1) * 512], ps[m][:, :], ACT.Copy).then_inc(rows_out, 1)
                    for f in range(KD):
                        act.wait_ge(turned, f + 1)
                        act.activation(hT[0][:, f, 2 * P:TOK], ps[f][:, 0:2 * P], ACT.Copy).then_inc(hi_out, 1)
                    act.wait_ge(logits_out, 2)
                    for j in range(2):
                        ins = act.activation(ex[:, j, :], lg[:, j, :], ACT.Exp, bias=negm[:, j:j + 1])
                    ins.then_inc(exps, 1)

                @block.vector
                def _(dve):
                    dve.wait_ge(router_in, 16)
                    dve_step(dve, dve.tensor_copy(wr2[0][:, :, :], wr[:, :, :]))
                    dve_step(dve, dve.tensor_tensor(wr2[1][:, :, :], wr[:, :, :], wr2[0][:, :, :].bitcast(F32), ALU.subtract))
                    dve.wait_ge(squares, 2)
                    dve.tensor_scalar(ssq, ssq, 1.0 / D, EPS, ALU.mult, ALU.add).then_inc(roots, 1)
                    dve.wait_ge(roots, 2)
                    dve_step(dve, dve.reciprocal(ssq, ssq))
                    dve.wait_ge(rows_out, 4)
                    for j in range(2):
                        h = xn[:, j, :]
                        dve_step(dve, dve.scalar_tensor_tensor(h, xres[:, 2 + j, :], ssq[:, j:j + 1], rows[:, 0, :], ALU.mult, ALU.mult))
                        dve.tensor_tensor(h, h, rows[:, 1, :], ALU.add).then_inc(h_done, 1)
                        dve.wait_ge(h_done, j + 1)
                        dve_step(dve, dve.tensor_copy(htok[0][:, j, :], h))
                        dve_step(dve, dve.tensor_tensor(htok[1][:, j, :], h, htok[0][:, j, :].bitcast(F32), ALU.subtract))
                    for f in range(KD):
                        dve.wait_ge(hi_out, f + 1)
                        dve.tensor_tensor(hT[1][:, f, 2 * P:TOK], ps[f][:, 0:2 * P], hT[0][:, f, 2 * P:TOK].bitcast(F32),
                                          ALU.subtract).then_inc(parts, 1)
                    dve.wait_ge(logits_sum, 1)
                    dve_step(dve, dve.tensor_copy(lg[:, :, :], ps[0][:, 0:2 * NE].rearrange("p (j e) -> p j e", j=2)))
                    dve.tensor_reduce(negm, lg[:, :, :], AX.X, ALU.max).then_inc(logits_out, 1)
                    dve.wait_ge(logits_out, 1)
                    dve.tensor_scalar(negm, negm, -1.0, None, ALU.mult).then_inc(logits_out, 1)
                    for j in range(2):
                        shape = [P, NE, NE]
                        inner, outer = lg[:, j, :].unsqueeze(1).to_broadcast(shape), lg[:, j, :].unsqueeze(2).to_broadcast(shape)
                        gt, eq = (cmp[:, j, i, :].rearrange("p (a b) -> p a b", a=NE) for i in range(2))
                        dve.tensor_tensor(gt, inner, outer, ALU.is_gt)
                        dve_step(dve, dve.tensor_tensor(eq, inner, outer, ALU.is_equal))
                        dve_step(dve, dve.tensor_tensor(cmp[:, j, 1, :], cmp[:, j, 1, :], const("before"), ALU.mult))
                        dve_step(dve, dve.tensor_tensor(cmp[:, j, 0, :], cmp[:, j, 0, :], cmp[:, j, 1, :], ALU.add))
                        dve_step(dve, dve.tensor_reduce(sel[:, j, :], gt, AX.X, ALU.add))
                    dve.tensor_scalar(sc[:, 32:48], sc[:, 32:48], 2.0, None, ALU.is_lt).then_inc(sel_done, 1)
                    dve.wait_ge(exps, 1)
                    dve.wait_ge(sel_done, 1)
                    dve_step(dve, dve.tensor_tensor(ex, ex, sel, ALU.mult))
                    dve_step(dve, dve.tensor_reduce(ssum, ex, AX.X, ALU.add))
                    dve_step(dve, dve.reciprocal(ssum, ssum))
                    dve_step(dve, dve.tensor_tensor(ex, ex, spread(ssum, 2, NE), ALU.mult))
                    dve.wait_ge(counted, 1)
                    pos = ps[1][:, 0:2 * NE].rearrange("p (j e) -> p j e", j=2)
                    for r in range(2):
                        s = slice(r * NE, (r + 1) * NE)
                        dve.tensor_copy(chosen[:, :, s], sel)
                        dve.tensor_copy(weight[:, :, s], ex)
                        dve.scalar_tensor_tensor(slot_of[:, :, s], pos, -float(r * P), sel, ALU.add, ALU.subtract)
                    for a in (slot_of, chosen, weight):
                        dve.memset(a[:, :, 2 * NE:2 * NE + 1], -1.0)
                    dve_step(dve, dve.tensor_reduce(most, ps[1][:, 2 * NE:3 * NE], AX.X, ALU.max))
                    dve_step(dve, dve.tensor_scalar(n_pass[:, :], most, float(P), 1.0, ALU.is_gt, ALU.add))

                @block.tensor
                def _(pe):
                    for i, cols_of_row in enumerate((gain, shift)):
                        for half in range(2):
                            for d in range(4):
                                last = pe.matmul(ps[2 * i + half][:, d * P:(d + 1) * P],
                                                 cols_of_row[:, 4 * half + d, :].to_broadcast([P, P]), ident, start=True, stop=True)
                            last.then_inc(rows_sum, 1)
                    pe.wait_ge(h_done, 2)
                    for f in range(KD):
                        for j in range(2):
                            last = pe.transpose(ps[f][:, j * P:(j + 1) * P], xn[:, j, f * P:(f + 1) * P], ident)
                        last.then_inc(turned, 1)
                    pe.wait_ge(parts, KD)
                    for j in range(2):
                        for k in range(KD):
                            a = [h[:, k, (2 + j) * P:(3 + j) * P] for h in hT]
                            last = three(pe, ps[0][:, j * NE:(j + 1) * NE], a, [w[:, k, :] for w in wr2], k == 0, k == KD - 1)
                    last.then_inc(logits_sum, 1)
                    pe.wait_ge(sel_done, 1)
                    pe.matmul(ps[1][:, 0:NE], const("tri_f"), sel[:, 0, :], start=True, stop=True)
                    pe.matmul(ps[1][:, NE:2 * NE], const("tri_f"), sel[:, 1, :], start=True, stop=False)
                    pe.matmul(ps[1][:, NE:2 * NE], const("ones"), sel[:, 0, :], start=False, stop=True)
                    for j in range(2):
                        last = pe.matmul(ps[1][:, 2 * NE:3 * NE], const("ones"), sel[:, j, :], start=j == 0, stop=j == 1)
                    last.then_inc(counted, 1)
            end_stage()

        yacc = at("moe_y", [P, NT, D], F32, M0 + 17408)

        def moe_experts():
            m = M0 + 17408 + 16384
            xeT = [at(f"xe_T_{n}", [P, KD, P], F32R, m + 4096 * i) for i, n in enumerate(("hi", "lo"))]
            m += 8192
            gT = [at(f"moe_gT_{n}", [P, FT, P], F32R, m + FT * P * 4 * i) for i, n in enumerate(("hi", "lo"))]
            m += 2 * FT * P * 4
            pick = at("pick", [P, 2, P], F32, m)
            pick_r = at("pick_r", [P, 2, P], F32R, m + 1024)
            put = at("put", [P, 2 * P], F32R, m + 2048)
            w_slot = at("w_slot", [P, 1], F32, m + 3072)
            m += 3136
            silu = at("moe_silu", [P, 2, 512], F32, m)
            prod = at("moe_prod", [P, 2, 512], F32, m + 4096)
            ytmp = at("moe_ytmp", [P, D], F32, m + 8192)
            ye = [at(f"moe_ye_{n}", [P, D], F32R, m + 12288 + 4096 * i) for i, n in enumerate(("hi", "lo"))]

            w1, w3 = (t[f"moe_w{i}"][0].rearrange("e (k p) n -> p e k n", p=P) for i in (1, 3))
            w2 = t["moe_w2"][0].rearrange("e (k p) n -> p e k n", p=P)
            NB = 6
            plan = []
            for b in range(NB - 1):
                plan += [(w, 4 * half, 4, b * 512, 512) for w in (w1, w3) for half in range(2)]
            plan += [(w, 0, KD, (NB - 1) * 512, 256) for w in (w1, w3)]
            up = len(plan)
            plan += [(w2, 2 * j, 2, 0, D) for j in range(FT // 2)]
            U, RING, AHEAD = len(plan), 3, 2
            assert U % RING == 0
            CUT = 1408
            h1_end = [4 * b + 1 for b in range(NB - 1)] + [up - 2]
            h3_end = [4 * b + 3 for b in range(NB - 1)] + [up - 1]
            turn_after = [h1_end[b + 1] for b in range(NB - 1)] + [up + 1]
            gather_after = up + 4
            names = ("hi_m", "lo_dve", "lo_pool", "used", "pick_ready", "gathered", "xe_act", "xe_dve", "put_sum",
                     "put_out", "ws_out", "silu_out", "g_done", "turned", "hi_out", "lo_done", "ye_out", "ye_ready",
                     "combined", "added", "dve_loop", "slot_free")
            (hi_m, lo_dve, lo_pool, used, pick_ready, gathered, xe_act, xe_dve, put_sum,
             put_out, ws_out, silu_out, g_done, turned, hi_out, lo_done, ye_out, ye_ready,
             combined, added, dve_loop, slot_free) = (stage_sem(s) for s in names)
            raw_m = [stage_sem(f"moe_raw_loaded{i}") for i in range(RING)]

            def part(buf, v):
                _, _, a, _, b = plan[v % U]
                return buf[:, v % RING, 0:a * b].rearrange("p (a b) -> p a b", b=b)

            def load(sp, e, v):
                w, k, a, c, b = plan[v % U]
                src = w[:, bass.ds(e, 1), k:k + a, c:c + b].rearrange("p e k n -> p (e k) n")
                sp.dma_start(part(moe_raw, v), src).then_inc(raw_m[v % RING], 16)

            def hi(act, n, v):
                act.wait_ge(raw_m[v % RING], 16 * (U // RING) * n + 16 * (v // RING + 1))
                act.activation(moe_hi[:, v % RING, :], moe_raw[:, v % RING, :], ACT.Copy).then_inc(hi_m, 1)

            def lo(eng, n, v, a, b, done):
                eng.wait_ge(hi_m, U * n + v + 1)
                s = v % RING
                eng.tensor_tensor(moe_lo[:, s, a:b], moe_raw[:, s, a:b], moe_hi[:, s, a:b].bitcast(F32), ALU.subtract).then_inc(done, 1)

            class LoopSteps:

                def __init__(self, sem, per, n):
                    self.sem, self.per, self.n, self.k = sem, per, n, 0

                def __call__(self, eng, ins):
                    self.k += 1
                    ins.then_inc(self.sem, 1)
                    eng.wait_ge(self.sem, self.per * self.n + self.k)

                def end(self):
                    assert self.k == self.per, self.k

            def build_pick(dve, step, nn):
                for j in range(2):
                    dve.tensor_scalar(pick[:, j, :], const("iota"), slot_of[:, j, bass.ds(nn, 1)], chosen[:, j, bass.ds(nn, 1)],
                                      ALU.is_equal, ALU.mult).then_inc(pick_ready, 1)
                dve.wait_ge(pick_ready, 3 * nn + 2)
                dve.tensor_copy(pick_r[:, :, :], pick[:, :, :]).then_inc(pick_ready, 1)

            def gather(pe, nn):
                pe.wait_ge(pick_ready, 3 * nn + 3)
                for i in range(4):
                    src, half = htok[i // 2], i % 2
                    if i >= 2:
                        pe.wait_ge(xe_act if half == 0 else xe_dve, 2 * nn + 1)
                    for d in range(4):
                        dd = 4 * half + d
                        for j in range(2):
                            last = pe.matmul(ps[4 + half][:, d * P:(d + 1) * P], src[:, j, dd * P:(dd + 1) * P], pick_r[:, j, :],
                                             start=j == 0, stop=j == 1)
                    last.then_inc(gathered, 1)

            def xe_out(copy, nn, half, done, eng):
                for i in range(2):
                    eng.wait_ge(gathered, 4 * nn + 2 * i + half + 1)
                    copy(xeT[i][:, 4 * half:4 * half + 4, :], ps[4 + half][:, :].rearrange("p (d s) -> p d s", d=4)).then_inc(done, 1)

            with nc.Block() as block:
                @block.sync
                def _(sp):
                    passes = sp.value_load(n_pass[0:1, 0:1], min_val=1, max_val=2)
                    for v in range(RING):
                        load(sp, 0, v)
                    with sp.Fori(0, passes * NE) as n:
                        experts = [sp.snap(n % NE), sp.snap((n + 1) % NE)]
                        for v in range(RING, U + RING):
                            split = sp.snap(U * n + v - RING + 1)
                            sp.wait_ge(lo_dve, split)
                            sp.wait_ge(lo_pool, split)
                            sp.sem_inc(slot_free, 1)
                            load(sp, experts[v // U], v)
                    for s in range(RING):
                        sp.wait_ge(raw_m[s], passes * (NE * (U // RING) * 16) + 16)
                        sp.sem_inc(slot_free, 1)

                @block.gpsimd
                def _(pool):
                    passes = pool.value_load(n_pass[0:1, 0:1], min_val=1, max_val=2)
                    for v in range(AHEAD):
                        lo(pool, 0, v, CUT, 2048, lo_pool)
                    with pool.Fori(0, passes * NE) as n:
                        for v in range(AHEAD, U + AHEAD):
                            lo(pool, n, v, CUT, 2048, lo_pool)

                @block.scalar
                def _(act):
                    passes = act.value_load(n_pass[0:1, 0:1], min_val=1, max_val=2)

                    def copy(out, in_):
                        return act.activation(out, in_, ACT.Copy)

                    act.sem_inc(silu_out, 2)
                    act.sem_inc(ye_out, 1)
                    for v in range(AHEAD):
                        hi(act, 0, v)
                    xe_out(copy, 0, 0, xe_act, act)
                    with act.Fori(0, passes * NE) as n:
                        for u in range(U):
                            act.wait_ge(used, U * n + u + 1)
                            hi(act, n, u + AHEAD)
                            if u == 1:
                                act.wait_ge(put_sum, n + 1)
                                act.activation(put[:, :], ps[4][:, 0:2 * P], ACT.Copy).then_inc(put_out, 1)
                            for b in range(NB):
                                if u == h1_end[b] + 1:
                                    w = plan[h1_end[b]][4]
                                    act.wait_ge(g_done, NB * n + b + 1)
                                    act.activation(silu[:, b % 2, 0:w], ps[b % 2][:, 0:w], ACT.Silu).then_inc(silu_out, 1)
                                if u == turn_after[b] + 1:
                                    k = 4 if b < NB - 1 else 2
                                    act.wait_ge(turned, NB * n + b + 1)
                                    act.activation(gT[0][:, 4 * b:4 * b + k, :],
                                                   ps[4 + b % 2][:, 0:k * P].rearrange("p (k s) -> p k s", k=k),
                                                   ACT.Copy).then_inc(hi_out, 1)
                            if u == gather_after + 1:
                                xe_out(copy, n + 1, 0, xe_act, act)
                        act.wait_ge(used, U * n + U + 1)
                        act.wait_ge(ws_out, n + 1)
                        act.activation(ytmp[:, 0:512], ps[6][:, :], ACT.Copy, scale=w_slot[:, 0:1])
                        act.activation(ytmp[:, 512:D], ps[7][:, :], ACT.Copy, scale=w_slot[:, 0:1]).then_inc(ye_out, 1)

                @block.vector
                def _(dve):
                    passes = dve.value_load(n_pass[0:1, 0:1], min_val=1, max_val=2)
                    dve.sem_inc(g_done, 2)
                    dve.sem_inc(lo_done, 2)
                    build_pick(dve, None, 0)
                    dve.memset(yacc[:, 2:4, :], 0.0).then_inc(added, 4)
                    for v in range(AHEAD):
                        lo(dve, 0, v, 0, CUT, lo_dve)
                    xe_out(dve.tensor_copy, 0, 1, xe_dve, dve)
                    with dve.Fori(0, passes * NE) as n:
                        step = LoopSteps(dve_loop, 1, n)
                        for u in range(U):
                            lo(dve, n, u + AHEAD, 0, CUT, lo_dve)
                            if u == 2:
                                dve.wait_ge(put_sum, n + 1)
                                dve.tensor_copy(w_slot[:, :], ps[5][:, 0:1]).then_inc(ws_out, 1)
                            for b in range(NB):
                                if u == h3_end[b] + 1:
                                    w = plan[h3_end[b]][4]
                                    dve.wait_ge(silu_out, NB * n + b + 3)
                                    dve.wait_ge(used, U * n + h3_end[b] + 2)
                                    dve.tensor_tensor(prod[:, b % 2, 0:w], silu[:, b % 2, 0:w], ps[2 + b % 2][:, 0:w],
                                                      ALU.mult).then_inc(g_done, 1)
                                if u == turn_after[b] + 2:
                                    k = 4 if b < NB - 1 else 2
                                    dve.wait_ge(hi_out, NB * n + b + 1)
                                    dve.tensor_tensor(gT[1][:, 4 * b:4 * b + k, :],
                                                      ps[4 + b % 2][:, 0:k * P].rearrange("p (k s) -> p k s", k=k),
                                                      gT[0][:, 4 * b:4 * b + k, :].bitcast(F32), ALU.subtract).then_inc(lo_done, 1)
                            if u == up + 1:
                                build_pick(dve, None, n + 1)
                            if u == gather_after + 1:
                                xe_out(dve.tensor_copy, n + 1, 1, xe_dve, dve)
                        dve.wait_ge(ye_out, n + 2)
                        step(dve, dve.tensor_copy(ye[0][:, :], ytmp[:, :]))
                        dve.tensor_tensor(ye[1][:, :], ytmp[:, :], ye[0][:, :].bitcast(F32), ALU.subtract).then_inc(ye_ready, 1)
                        for c in range(4):
                            dve.wait_ge(combined, 4 * n + c + 1)
                            a = yacc[:, 2 + c // 2, (c % 2) * 512:(c % 2 + 1) * 512]
                            dve.tensor_tensor(a, a, ps[4 + c % 2][:, :], ALU.add).then_inc(added, 1)
                        step.end()

                @block.tensor
                def _(pe):
                    passes = pe.value_load(n_pass[0:1, 0:1], min_val=1, max_val=2)
                    pe.sem_inc(used, 1)
                    gather(pe, 0)
                    pe.wait_ge(xe_act, 2)
                    pe.wait_ge(xe_dve, 2)
                    with pe.Fori(0, passes * NE) as n:
                        for u in range(U):
                            v, s = u, u % RING
                            pe.wait_ge(lo_dve, U * n + u + 1)
                            pe.wait_ge(lo_pool, U * n + u + 1)
                            _, k0, a, _, w = plan[u]
                            wh, wl = part(moe_hi, v), part(moe_lo, v)
                            if u < up:
                                b = min(u // 4, NB - 1)
                                is_h3 = plan[u][0] is w3
                                if u in (4 * b, 4 * b + 2) or b == NB - 1:
                                    pe.wait_ge(g_done if is_h3 else silu_out, NB * n + b + 1)
                                bank = ps[2 * is_h3 + b % 2]
                                for k in range(a):
                                    kk = k0 + k
                                    last = three(pe, bank[:, 0:w], [x[:, kk, :] for x in xeT], [wh[:, k, :], wl[:, k, :]],
                                                 kk == 0, kk == KD - 1)
                            else:
                                if u == up:
                                    pe.wait_ge(ye_out, n + 1)
                                for k in range(a):
                                    kk = k0 + k
                                    if kk % 4 == 0:
                                        pe.wait_ge(lo_done, NB * n + kk // 4 + 3)
                                    for half in range(2):
                                        c = slice(half * 512, (half + 1) * 512)
                                        last = three(pe, ps[6 + half][:, :], [x[:, kk, :] for x in gT], [wh[:, k, c], wl[:, k, c]],
                                                     kk == 0, kk == FT - 1)
                            last.then_inc(used, 1)
                            if u == 0:
                                pe.wait_ge(added, 4 * n + 4)
                                for j in range(2):
                                    pe.transpose(ps[4][:, j * P:(j + 1) * P], pick[:, j, :], ident)
                                for j in range(2):
                                    last = pe.matmul(ps[5][:, 0:1], pick[:, j, :], weight[:, j, bass.ds(n, 1)], start=j == 0, stop=j == 1)
                                last.then_inc(put_sum, 1)
                            for b in range(NB):
                                if u == turn_after[b]:
                                    if b < 2:
                                        pe.wait_ge(put_out if b == 0 else ws_out, n + 1)
                                    pe.wait_ge(g_done, NB * n + b + 3)
                                    pe.wait_ge(lo_done, NB * n + b + 1)
                                    for k in range(4 if b < NB - 1 else 2):
                                        last = pe.transpose(ps[4 + b % 2][:, k * P:(k + 1) * P], prod[:, b % 2, k * P:(k + 1) * P], ident)
                                    last.then_inc(turned, 1)
                            if u == gather_after:
                                pe.wait_ge(lo_done, NB * n + NB + 2)
                                gather(pe, n + 1)
                        pe.wait_ge(ye_ready, n + 1)
                        pe.wait_ge(xe_act, 2 * n + 4)
                        pe.wait_ge(xe_dve, 2 * n + 4)
                        for c in range(4):
                            if c >= 2:
                                pe.wait_ge(added, 4 * n + c + 3)
                            j, half = divmod(c, 2)
                            for i in range(2):
                                last = pe.matmul(ps[4 + c % 2][:, :], put[:, j * P:(j + 1) * P], ye[i][:, half * 512:(half + 1) * 512],
                                                 start=i == 0, stop=i == 1)
                            last.then_inc(combined, 1)
            end_stage()

        def finish(l):
            rows = at("last_rows", [P, 2, D], F32, R0)
            junk = at("last_junk", [P, D], F32, R0 + 8192)
            rows_sum, rows_out, y_out, squared, roots, x_out, stored = (
                stage_sem(s) for s in ("rows_sum", "rows_out", "y_out", "squared", "roots", "x_out", "stored"))
            ssq = small[:, 0:4]
            with nc.Block() as block:
                @block.sync
                def _(sp):
                    for j in range(2):
                        sp.wait_ge(x_out, j + 1)
                        sp.dma_start(t["out"][0, j * P:(j + 1) * P, :], xres[:, 2 + j, :]).then_inc(stored, 16)
                    sp.wait_ge(stored, 32)

                @block.scalar
                def _(act):
                    post_rows_act(act, rows, [0], rows_sum, rows_out, [0, 1, 2, 3])
                    post_norm_act(act, yacc, X_TILES, ssq, junk, y_out, squared, roots)

                @block.vector
                def _(dve):
                    dve.sem_inc(y_out, 4)
                    post_norm_dve(dve, yacc, rows, X_TILES, ssq, squared, roots, rows_out, 2, x_out)

                @block.tensor
                def _(pe):
                    post_rows_pe(pe, l, 1, [0], rows_sum, rows_out, [0, 1, 2, 3])
            end_stage()

        setup()
        for l in range(DEPTH):
            tiles = ALL_TILES if l == 0 else X_TILES
            ada(l)
            norm(l, ALL_TILES, 0)
            ssm_project(l)
            ssm_mix(l, tiles)
            ssm_gate(l, tiles)
            merge(l, 1, tiles, True)
            ret_project(l, tiles)
            ret_mix(l, tiles)
            ret_gate(l, tiles)
            merge(l, 0, tiles, False)
            att_project(l, tiles)
            att_mix(l, tiles)
            merge(l, 2, tiles, False)
            out_project(l, tiles)
            if l == 0:
                norm(l, ALL_TILES, 1)
                ffn_up()
                ffn_down(l)
            else:
                moe_route(l)
                moe_experts()
                finish(l)


INPUTS = ["x", "c", "ctx", "c_ctx", "ada_w", "ada_b", "mix_norm_pre", "mix_norm_post", "ffn_norm_pre",
          "ffn_norm_post", "w_in", "ret_decay", "ssm_conv_w", "ssm_conv_b", "ssm_dt_bias", "ssm_a_log", "ssm_d",
          "ssm_norm_w", "att_sink", "w_branch", "w_out", "ffn_w1", "ffn_w3", "ffn_w2", "moe_router", "moe_w1",
          "moe_w3", "moe_w2"]


def kernel(**inputs):
    import concourse.bacc as bacc
    from concourse.bass_utils import run_bass_kernel_spmd

    nc = bacc.Bacc("TRN2", target_bir_lowering=False, num_devices=1)
    arrays = {name: np.ascontiguousarray(inputs[name]) for name in INPUTS}
    arrays["consts"] = constants()
    t = {name: nc.dram_tensor(f"in_{name}", a.shape, F32, kind="ExternalInput").ap() for name, a in arrays.items()}
    t["out"] = nc.dram_tensor("out", (1, SEQ, D), F32, kind="ExternalOutput").ap()
    program(nc, t)
    r = run_bass_kernel_spmd(nc, [{f"in_{name}": a for name, a in arrays.items()}], core_ids=[0])
    return r.results[0]["out"]
```

```python
from contextlib import ExitStack

import numpy as np

import concourse.bass as bass
from concourse import mybir

F32 = mybir.dt.float32
F32R = mybir.dt.float32r
ACT = mybir.ActivationFunctionType
ALU = mybir.AluOpType
AX = mybir.AxisListType

P = 128
D = 1024
KD = D // P
SEQ, CTX = 256, 256
NT = (SEQ + CTX) // P
TOK = NT * P
X_TILES, ALL_TILES = [2, 3], [0, 1, 2, 3]
DEPTH = 2
EPS = 1e-6
GRID_W = 64
BLK = 512
RH, DK, DV = 4, 128, 256
SH, HD, SG, ST = 16, 64, 2, 128
HG = SH // SG
XBC = SH * HD + 2 * SG * ST
AH, KVH, AD = 8, 2, 128
AG = AH // KVH
FF = 2816
FT = FF // P
NE = 8
NEG = -1e30

SPLITS = dict(rq=RH * DK, rk=RH * DK, rv=RH * DV, rg=RH * DV, sz=SH * HD, xbc=XBC, dt=SH,
              aq=AH * AD, akv=2 * KVH * AD, gate=3 * D)
COL = {}
_at = 0
for _name, _width in SPLITS.items():
    COL[_name] = _at
    _at += _width
IN_W = _at

CONSTS = dict(ident=P, tri_f=P, tri_b=P, neg_up=P, neg_low=P, ones=P, dist_f=P, dist_b=P, iota=P,
              ret_w=4, sel=2, before=NE * NE,
              rq_cos=128, rq_sin=128, rk_cos=128, rk_sin=128, aq_cos=128, aq_sin=128, ak_cos=128, ak_sin=128)
CAT = {}
_at = 0
for _name, _width in CONSTS.items():
    CAT[_name] = _at
    _at += _width
N_CONST = _at

ROWS = dict(ada_b=48, mix_pre=8, ffn_pre=8, conv_w=36, conv_b=12)
ROW = {}
_at = 0
for _name, _width in ROWS.items():
    ROW[_name] = _at
    _at += _width
N_ROWS = _at


def constants():
    a = np.zeros((P, N_CONST), np.float32)
    i = np.arange(P, dtype=np.float32)
    row, col = i[:, None], i[None, :]

    def put(name, v):
        a[:, CAT[name]:CAT[name] + v.shape[1]] = v

    put("ident", np.eye(P, dtype=np.float32))
    put("tri_f", (row <= col).astype(np.float32))
    put("tri_b", (row >= col).astype(np.float32))
    put("neg_up", np.where(col > row, NEG, 0.0).astype(np.float32))
    put("neg_low", np.where(col < row, NEG, 0.0).astype(np.float32))
    put("ones", np.ones((P, P), np.float32))
    put("dist_f", np.maximum(col - row, 0.0))
    put("dist_b", np.maximum(row - col, 0.0))
    put("iota", np.broadcast_to(col, (P, P)))
    put("ret_w", np.stack([P - 1 - i, i, i + 1, P - i], 1))
    put("sel", (np.arange(P)[:, None] % 2 == np.arange(2)[None, :]).astype(np.float32))
    e = np.arange(NE)
    put("before", np.broadcast_to((e[None, :] < e[:, None]).astype(np.float32).reshape(1, NE * NE), (P, NE * NE)))
    pos = np.arange(SEQ, dtype=np.float32)

    def angles(p, dim):
        inv = np.float32(10000.0) ** (-np.arange(0, dim, 2, dtype=np.float32) / np.float32(dim))
        return p[:, None] * inv[None, :].astype(np.float32)

    grid_row, grid_col = np.floor(pos / GRID_W), pos % GRID_W
    ret = angles(pos, DK)
    att = np.concatenate([angles(grid_row, AD // 2), angles(grid_col, AD // 2)], 1)
    for name, ang, scale in (("rq", ret, 1.0), ("rk", ret, DK ** -0.5), ("aq", att, AD ** -0.5), ("ak", att, 1.0)):
        for part, fn in (("cos", np.cos), ("sin", np.sin)):
            t = (fn(ang).astype(np.float32) * np.float32(scale)).reshape(2, P, 64).transpose(1, 0, 2)
            put(f"{name}_{part}", t.reshape(P, 128))
    return a


class Steps:

    def __init__(self, sem):
        self.sem, self.n = sem, 0

    def __call__(self, eng, ins):
        self.n += 1
        ins.then_inc(self.sem, 1)
        eng.wait_ge(self.sem, self.n)


def program(nc, t):
    ctx = ExitStack()
    with ctx:
        top = [nc.sbuf_base + (-nc.sbuf_base) % 64]

        placed = {}

        def at(name, shape, dt, offset):
            if name not in placed:
                placed[name] = nc.alloc_sbuf_tensor_at(name, shape, dt, offset=offset)
            return placed[name]

        def size(shape):
            return int(np.prod(shape[1:])) * 4

        def sb(name, shape, dt=F32):
            offset = top[0]
            top[0] += size(shape) + (-size(shape)) % 64
            return at(name, shape, dt, offset)

        def sem(name):
            return ctx.enter_context(nc.semaphore(name))

        ps = [ctx.enter_context(nc.psum_tensor(f"bank{i}", [P, BLK], F32)) for i in range(8)]

        cst = sb("constants", [P, N_CONST])

        def const(name):
            return cst[:, CAT[name]:CAT[name] + CONSTS[name]]

        ident = const("ident")
        cols = [sb(f"param_cols{l}", [P, P]) for l in range(DEPTH)]
        norm_cols = [sb(f"norm_cols{l}", [P, 24]) for l in range(DEPTH)]
        cond = sb("cond", [P, KD, 2])
        mods = [sb(f"mods{l}", [P, 48, 2]) for l in range(DEPTH)]
        gains = [sb(f"gains{l}", [P, 4, KD, 2]) for l in range(DEPTH)]
        heads = [sb(f"head_params{l}", [P, 8 + 32 + 32 + 32 + 8]) for l in range(DEPTH)]
        xres = sb("xres", [P, NT, D])
        small = sb("small", [P, 128])
        ring_at = top[0]
        raw = sb("raw_units", [P, 2, 2048])
        whi = sb("unit_hi", [P, 2, 2048], F32R)
        wlo = sb("unit_lo", [P, 2, 2048], F32R)
        hT_at = top[0]
        hT = [sb(f"hT_{n}", [P, KD, TOK], F32R) for n in ("hi", "lo")]
        outT_at = top[0]
        outT = [sb(f"outT_{n}", [P, KD, TOK], F32R) for n in ("hi", "lo")]
        merged_at = top[0]
        merged = sb("merged", [P, NT, D])
        work = top[0]
        limit = nc.sbuf_usable_end - 64

        raw_loaded = [sem("raw_loaded0"), sem("raw_loaded1")]
        hi_ready, lo_ready, unit_used = sem("hi_ready"), sem("lo_ready"), sem("unit_used")
        x_in = [sem("ctx_in"), sem("x_in")]
        params_in = sem("params_in")
        dve_step, act_step, pool_step = Steps(sem("dve_step")), Steps(sem("act_step")), Steps(sem("pool_step"))
        units, span = [], {}

        def unit_block(w, col, width=BLK):
            v = w.rearrange("(k p) n -> p k n", p=P)
            for half in range(2):
                units.append(v[:, 4 * half:4 * half + 4, col:col + width])

        def stage_units(name, add):
            a = len(units)
            add()
            span[name] = (a, len(units))

        for l in range(DEPTH):
            w_in, wb, wo = t["w_in"][l], t["w_branch"][l], t["w_out"][l]

            def cols_of(name, n):
                for b in range(n):
                    unit_block(w_in, COL[name] + b * BLK)

            def add_ssm():
                cols_of("xbc", 3)
                units.append(w_in.rearrange("(k p) n -> p k n", p=P)[:, :, COL["dt"]:COL["dt"] + SH])

            def add_merge(n):
                for b in range(2):
                    unit_block(w_in, COL["gate"] + n * D + b * BLK)
                    unit_block(wb[n], b * BLK)

            stage_units(f"ssm{l}", add_ssm)
            stage_units(f"z{l}", lambda: cols_of("sz", 2))
            stage_units(f"merge1_{l}", lambda: add_merge(1))
            stage_units(f"ret{l}", lambda: [cols_of("rq", 1), cols_of("rk", 1), cols_of("rv", 2)])
            stage_units(f"g{l}", lambda: cols_of("rg", 2))
            stage_units(f"merge0_{l}", lambda: add_merge(0))
            stage_units(f"att{l}", lambda: [cols_of("aq", 2), cols_of("akv", 1)])
            stage_units(f"merge2_{l}", lambda: add_merge(2))
            stage_units(f"out{l}", lambda: [unit_block(wo, b * BLK) for b in range(2)])
            if l == 0:
                w1, w3, w2 = t["ffn_w1"][0], t["ffn_w3"][0], t["ffn_w2"][0]

                def add_ffn():
                    for f in range(FF // 256):
                        for w in (w1, w3):
                            units.append(w.rearrange("(k p) n -> p k n", p=P)[:, :, f * 256:f * 256 + 256])

                stage_units("ffn_up", add_ffn)
                stage_units("ffn_down", lambda: [
                    units.append(w2.rearrange("(k p) n -> p k n", p=P)[:, 2 * u:2 * u + 2, :]) for u in range(FT // 2)])
        n_units = len(units)

        def view(buf, g):
            a, b = units[g].shape[1], units[g].shape[2]
            return buf[:, g % 2, 0:a * b].rearrange("p (a b) -> p a b", b=b)

        def load_unit(sp, g):
            if g >= n_units:
                return
            if g >= 2:
                sp.wait_ge(lo_ready, g - 1)
            sp.dma_start(view(raw, g), units[g]).then_inc(raw_loaded[g % 2], 16)

        def split_hi(act, g):
            if g >= n_units:
                return
            act.wait_ge(raw_loaded[g % 2], 16 * (g // 2 + 1))
            if g >= 2:
                act.wait_ge(unit_used, g - 1)
            act.activation(view(whi, g), view(raw, g), ACT.Copy).then_inc(hi_ready, 1)

        def split_lo(eng, g):
            if g >= n_units:
                return
            eng.wait_ge(hi_ready, g + 1)
            eng.tensor_tensor(view(wlo, g), view(raw, g), view(whi, g).bitcast(F32), ALU.subtract).then_inc(lo_ready, 1)

        def loads(sp, name):
            a, b = span[name]
            for g in range(a + 4, b + 4):
                load_unit(sp, g)

        def splits_lo(eng, name):
            a, b = span[name]
            for g in range(a + 2, b + 2):
                split_lo(eng, g)

        def three(pe, out, a, w, first, last):
            pe.matmul(out, a[0], w[0], start=first, stop=False)
            pe.matmul(out, a[0], w[1], start=False, stop=False)
            return pe.matmul(out, a[1], w[0], start=False, stop=last)

        def project(pe, g, banks, tiles, src=None):
            for u in range(2):
                pe.wait_ge(lo_ready, g + u + 1)
                w = [view(whi, g + u), view(wlo, g + u)]
                for k in range(4):
                    kk = 4 * u + k
                    for j, tile in enumerate(tiles):
                        a = [h[:, kk, tile * P:(tile + 1) * P] for h in (src or hT)]
                        last = three(pe, ps[banks[j]][:, :], a, [w[0][:, k, :], w[1][:, k, :]], kk == 0, kk == KD - 1)
                last.then_inc(unit_used, 1)

        def spread(col, n, m):
            return col.unsqueeze(2).to_broadcast([P, n, m])

        stage_no, in_use, cleared = [0], [], []

        def stage_sem(name):
            guard = nc.semaphore(f"{name}_{stage_no[0]}")
            in_use.append((guard, guard.__enter__()))
            return in_use[-1][1]

        def end_stage():
            for guard, handle in cleared:
                guard.__exit__(None, None, None)
            cleared[:] = in_use
            in_use.clear()
            for guard, handle in cleared:
                nc.sync.sem_clear(handle)
            stage_no[0] += 1

        ADA_U = 4

        def ada_unit(l, chunk, u):
            c = chunk * D + u * 256
            return t["ada_w"][l].rearrange("(k p) n -> p k n", p=P)[:, :, c:c + 256]

        def ada_rows(pe, out, buf):
            for k in range(KD):
                last = pe.matmul(out, cond[:, k, :], buf[:, k, :], start=k == 0, stop=k == KD - 1)
            return last

        def ada_turn(pe, out, rows, u):
            for m in range(2):
                f = 2 * u + m
                last = pe.matmul(out[:, 2 * f:2 * f + 2], rows[:, m * P:(m + 1) * P], ident[0:2, 0:2], start=True, stop=True)
            return last

        def ada_finish(dve, l, chunk, out):
            m = mods[l][:, 8 * chunk:8 * chunk + 8, :]
            dve_step(dve, dve.tensor_tensor(m, out.rearrange("p (f c) -> p f c", c=2),
                                            spread(col(l, "ada_b")[:, 8 * chunk:8 * chunk + 8], KD, 2), ALU.add))
            if chunk in (1, 4):
                gn = gains[l][:, chunk // 4, :, :]
                dve_step(dve, dve.tensor_scalar(gn, m, 1.0, None, ALU.add))
                dve_step(dve, dve.tensor_tensor(gn, gn, spread(col(l, "mix_pre" if chunk == 1 else "ffn_pre"), KD, 2), ALU.mult))
            if chunk in (2, 5):
                j = (chunk - 2) // 3
                dve_step(dve, dve.tensor_tensor(gains[l][:, 2 + j, :, :], m, spread(norm_cols[l][:, 8 * j:8 * j + 8], KD, 2), ALU.mult))

        def param_rows(eng, l, done):
            rows, nrows = row_bufs(l)
            for name, src in (("ada_b", t["ada_b"][l]), ("mix_pre", t["mix_norm_pre"][l]), ("ffn_pre", t["ffn_norm_pre"][l]),
                              ("conv_w", t["ssm_conv_w"][l].rearrange("w n -> (w n)")), ("conv_b", t["ssm_conv_b"][l])):
                eng.dma_start(rows[ROW[name]:ROW[name] + ROWS[name], :], src.rearrange("(a p) -> a p", p=P)).then_inc(done, 16)
            for j, name in enumerate(("mix_norm_post", "ffn_norm_post", "ssm_norm_w")):
                eng.dma_start(nrows[8 * j:8 * j + 8, :], t[name][l].rearrange("(a p) -> a p", p=P)).then_inc(done, 16)

        def row_bufs(l):
            return (at(f"param_rows{l}", [N_ROWS, P], F32, merged_at + 512 * (l + 1)),
                    at(f"norm_rows{l}", [24, P], F32, merged_at + 1536 + 512 * l))

        def turn_params(pe, l, turned):
            rows, nrows = row_bufs(l)
            pe.transpose(ps[0][:, 0:N_ROWS], rows[:, :], ident[0:N_ROWS, 0:N_ROWS])
            pe.transpose(ps[0][:, N_ROWS:N_ROWS + 24], nrows[:, :], ident[0:24, 0:24]).then_inc(turned, 1)

        def take_params(dve, l, turned):
            dve.wait_ge(turned, 1)
            dve_step(dve, dve.tensor_copy(cols[l][:, 0:N_ROWS], ps[0][:, 0:N_ROWS]))
            dve_step(dve, dve.tensor_copy(norm_cols[l][:, :], ps[0][:, N_ROWS:N_ROWS + 24]))

        def setup():
            cond_rows = at("cond_rows", [16, P], F32, merged_at)
            bufs = [at(f"ada_first{i}", [P, KD, 256], F32, hT_at + 8192 * i) for i in range(8)]
            row_buf = at("mod_rows", [2, 2, 256], F32, work)
            const_in, cond_in, row_in = (stage_sem(n) for n in ("const_in", "cond_in", "row_in"))
            turned, cond_turned, cond_out, summed, rows_out, ada_done = (
                stage_sem(n) for n in ("turned", "cond_turned", "cond_out", "summed", "rows_out", "ada_done"))
            unit_in = [stage_sem(f"ada_unit_in{i}") for i in range(8)]
            with nc.Block() as block:
                @block.sync
                def _(sp):
                    sp.dma_start(cst[:, :], t["consts"]).then_inc(const_in, 16)
                    for i in range(8):
                        sp.dma_start(bufs[i][:, :, :], ada_unit(0, i // 4, i % 4)).then_inc(unit_in[i], 16)
                    for j, src in enumerate((t["ctx"], t["x"])):
                        sp.dma_start(xres[:, 2 * j:2 * j + 2, :], src[0].rearrange("(t p) d -> p t d", p=P)).then_inc(x_in[j], 16)
                    param_rows(sp, 1, params_in)
                    for l in range(DEPTH):
                        for a, b, src in ((0, 8, t["ret_decay"][l].rearrange("a b -> (a b)")),
                                          (8, 40, t["ssm_dt_bias"][l].rearrange("a b -> (a b)")),
                                          (40, 72, t["ssm_a_log"][l].rearrange("a b -> (a b)")),
                                          (72, 104, t["ssm_d"][l].rearrange("a b -> (a b)")),
                                          (104, 112, t["att_sink"][l])):
                            sp.dma_start(heads[l][:, a:b], src.partition_broadcast(P)).then_inc(params_in, 16)
                    for g in range(2):
                        load_unit(sp, g)

                @block.scalar
                def _(act):
                    act.dma_start(cond_rows[0:8, :], t["c"][0].rearrange("(a p) -> a p", p=P)).then_inc(cond_in, 16)
                    act.dma_start(cond_rows[8:16, :], t["c_ctx"].rearrange("(a p) -> a p", p=P)).then_inc(cond_in, 16)
                    param_rows(act, 0, row_in)
                    act.wait_ge(cond_turned, 1)
                    act.activation(cond[:, :, :], ps[4][:, 0:16].rearrange("p (c k) -> p k c", c=2), ACT.Silu).then_inc(cond_out, 1)
                    for i in range(8):
                        act.wait_ge(summed, i + 1)
                        act.activation(row_buf[:, i % 2, :], ps[6 + i % 2][0:2, 0:256], ACT.Copy).then_inc(rows_out, 1)

                @block.tensor
                def _(pe):
                    pe.wait_ge(const_in, 16)
                    pe.wait_ge(cond_in, 32)
                    pe.transpose(ps[4][:, 0:16], cond_rows[:, :], ident[0:16, 0:16]).then_inc(cond_turned, 1)
                    pe.wait_ge(cond_out, 1)
                    for i in range(9):
                        if i < 8:
                            pe.wait_ge(unit_in[i], 16)
                            ada_rows(pe, ps[6 + i % 2][0:2, 0:256], bufs[i]).then_inc(summed, 1)
                        if i:
                            n = i - 1
                            pe.wait_ge(rows_out, n + 1)
                            last = ada_turn(pe, ps[5][:, 16 * (n // 4):16 * (n // 4) + 16], row_buf[:, n % 2, :], n % 4)
                    last.then_inc(ada_done, 1)
                    pe.wait_ge(row_in, 16 * 8)
                    turn_params(pe, 0, turned)

                @block.vector
                def _(dve):
                    take_params(dve, 0, turned)
                    dve.wait_ge(ada_done, 1)
                    for chunk in range(2):
                        ada_finish(dve, 0, chunk, ps[5][:, 16 * chunk:16 * chunk + 16])
            end_stage()

        def other_params():
            turned = stage_sem("turned")
            with nc.Block() as block:
                @block.sync
                def _(sp):
                    for g in range(2, 4):
                        load_unit(sp, g)

                @block.scalar
                def _(act):
                    for g in range(2):
                        split_hi(act, g)

                @block.gpsimd
                def _(pool):
                    for g in range(2):
                        split_lo(pool, g)

                @block.tensor
                def _(pe):
                    pe.wait_ge(params_in, 16 * (8 + 5 * DEPTH))
                    turn_params(pe, 1, turned)

                @block.vector
                def _(dve):
                    take_params(dve, 1, turned)
            end_stage()

        def col(l, name, n=None):
            a = ROW[name]
            return cols[l][:, a:a + (n or ROWS[name])]

        def norm(l, tiles, which):
            A, B = gains[l][:, which, :, :], mods[l][:, 24 * which:24 * which + 8, :]
            n = len(tiles)
            xn = at("normed", [P, NT, D], F32, work)
            tmp = at("affine", [P, 2, TOK], F32, work + NT * D * 4)
            squares, roots, normed, turned, affine, parts = (
                stage_sem(s) for s in ("squares", "roots", "normed", "turned", "affine", "parts"))
            ssq, rstd = small[:, 0:4], small[:, 4:8]
            with nc.Block() as block:
                @block.scalar
                def _(act):
                    for tile in tiles:
                        act.wait_ge(x_in[tile // 2], 16)
                        act.activation(xn[:, tile, :], xres[:, tile, :], ACT.Square,
                                       accum_out=ssq[:, tile:tile + 1]).then_inc(squares, 1)
                    act.wait_ge(roots, 1)
                    act.activation(rstd[:, :], rstd[:, :], ACT.Sqrt).then_inc(roots, 1)
                    for d in range(KD):
                        act.wait_ge(turned, d + 1)
                        if d >= 2:
                            act.wait_ge(parts, d - 1)
                        segs = [(0, 2 * P, 1), (2 * P, TOK, 0)] if n == NT else [(0, 2 * P, 0)]
                        for s, (a, b, c) in enumerate(segs):
                            ins = act.activation(tmp[:, d % 2, a:b], ps[d][:, a:b], ACT.Identity,
                                                 scale=A[:, d, c:c + 1], bias=B[:, d, c:c + 1])
                        ins.then_inc(affine, 1)

                @block.vector
                def _(dve):
                    lo, hi = tiles[0], tiles[-1] + 1
                    dve.wait_ge(squares, n)
                    dve_step(dve, dve.memset(rstd[:, :], 1.0))
                    dve.tensor_scalar(rstd[:, lo:hi], ssq[:, lo:hi], 1.0 / D, EPS, ALU.mult, ALU.add).then_inc(roots, 1)
                    dve.wait_ge(roots, 2)
                    dve_step(dve, dve.reciprocal(rstd[:, :], rstd[:, :]))
                    for tile in tiles:
                        dve.tensor_scalar(xn[:, tile, :], xres[:, tile, :], rstd[:, tile:tile + 1], None,
                                          ALU.mult).then_inc(normed, 1)
                    for d in range(KD):
                        dve.wait_ge(affine, d + 1)
                        w = n * P
                        dve_step(dve, dve.tensor_copy(hT[0][:, d, lo * P:hi * P], tmp[:, d % 2, 0:w]))
                        dve.tensor_tensor(hT[1][:, d, lo * P:hi * P], tmp[:, d % 2, 0:w],
                                          hT[0][:, d, lo * P:hi * P].bitcast(F32), ALU.subtract).then_inc(parts, 1)

                @block.tensor
                def _(pe):
                    pe.wait_ge(normed, n)
                    for d in range(KD):
                        for j, tile in enumerate(tiles):
                            last = pe.transpose(ps[d][:, j * P:(j + 1) * P], xn[:, tile, d * P:(d + 1) * P], ident)
                        last.then_inc(turned, 1)
            end_stage()

        def ssm_project(l):
            a0, b0 = span[f"ssm{l}"]
            ux = at("u_x", [P, 8, TOK], F32, work)
            bT, cT, btok, dtraw, xtok = ssm_tensors()[:5]
            acc = at("conv_acc", [P, 4, TOK], F32, work + 32768)
            acc_set, conv_done, u_ready, turned, turned_out, dt_sum = (
                stage_sem(s) for s in ("acc_set", "conv_done", "u_ready", "turned", "turned_out", "dt_sum"))
            cw, cb = col(l, "conv_w"), col(l, "conv_b")

            def u_of(i):
                return ux[:, i, :] if i < 8 else (bT if i < 10 else cT)[:, i % 2, :]

            with nc.Block() as block:
                @block.sync
                def _(sp):
                    loads(sp, f"ssm{l}")

                @block.gpsimd
                def _(pool):
                    splits_lo(pool, f"ssm{l}")

                @block.scalar
                def _(act):
                    for n in range(3):
                        for u in range(2):
                            split_hi(act, a0 + 2 * n + u + 2)
                        act.wait_ge(unit_used, a0 + 2 * n + 2)
                        for m in range(4):
                            i = 4 * n + m
                            act.activation(acc[:, m, :], ps[4 * (n % 2) + m][:, :], ACT.Identity,
                                           scale=cw[:, 12 + i:13 + i], bias=cb[:, i:i + 1]).then_inc(acc_set, 1)
                        for m in range(4):
                            i = 4 * n + m
                            act.wait_ge(conv_done, i + 1)
                            act.activation(u_of(i), acc[:, m, :], ACT.Silu).then_inc(u_ready, 1)
                        act.wait_ge(u_ready, 4 * n + 4)
                    split_hi(act, a0 + 8)

                @block.vector
                def _(dve):
                    for i in range(12):
                        n, m = divmod(i, 4)
                        s = ps[4 * (n % 2) + m][:, :].rearrange("p (s t) -> p s t", s=2)
                        o = acc[:, m, :].rearrange("p (s t) -> p s t", s=2)
                        dve.wait_ge(acc_set, i + 1)
                        dve_step(dve, dve.scalar_tensor_tensor(o[:, :, 1:], s[:, :, :-1], cw[:, i:i + 1], o[:, :, 1:],
                                                               ALU.mult, ALU.add))
                        dve.scalar_tensor_tensor(o[:, :, :-1], s[:, :, 1:], cw[:, 24 + i:25 + i], o[:, :, :-1],
                                                 ALU.mult, ALU.add).then_inc(conv_done, 1)
                    dve.wait_ge(dt_sum, 1)
                    dve.tensor_copy(dtraw[:, :, :], ps[4][:, 0:NT * SH].rearrange("p (t h) -> p t h", h=SH))
                    for i in range(10):
                        dve.wait_ge(turned, i + 1)
                        out = xtok[:, :, i * P:(i + 1) * P] if i < 8 else btok[:, :, (i - 8) * P:(i - 7) * P]
                        dve.tensor_copy(out, ps[5 + i % 3][:, :].rearrange("p (t f) -> p t f", t=NT)).then_inc(turned_out, 1)

                @block.tensor
                def _(pe):
                    for n in range(3):
                        if n == 2:
                            pe.wait_ge(conv_done, 4)
                        for u in range(2):
                            g = a0 + 2 * n + u
                            pe.wait_ge(lo_ready, g + 1)
                            wh, wl = view(whi, g), view(wlo, g)
                            for k in range(4):
                                kk = 4 * u + k
                                for m in range(4):
                                    a = [wh[:, k, m * P:(m + 1) * P], wl[:, k, m * P:(m + 1) * P]]
                                    last = three(pe, ps[4 * (n % 2) + m][:, :], a, [h[:, kk, :] for h in hT],
                                                 kk == 0, kk == KD - 1)
                            last.then_inc(unit_used, 1)
                    g = a0 + 6
                    pe.wait_ge(lo_ready, g + 1)
                    pe.wait_ge(conv_done, 8)
                    for tile in range(NT):
                        for k in range(KD):
                            a = [h[:, k, tile * P:(tile + 1) * P] for h in hT]
                            last = three(pe, ps[4][:, tile * SH:(tile + 1) * SH], a,
                                         [view(whi, g)[:, k, :], view(wlo, g)[:, k, :]], k == 0, k == KD - 1)
                    last.then_inc(unit_used, 1)
                    pe.transpose(ps[5][:, 0:P], ident, ident).then_inc(dt_sum, 1)
                    for i in range(10):
                        pe.wait_ge(u_ready, i + 1)
                        if i >= 3:
                            pe.wait_ge(turned_out, i - 2)
                        for tile in range(NT):
                            last = pe.transpose(ps[5 + i % 3][:, tile * P:(tile + 1) * P],
                                                u_of(i)[:, tile * P:(tile + 1) * P], ident)
                        last.then_inc(turned, 1)
            end_stage()

        def ssm_tensors():
            bT = at("B_T", [P, SG, TOK], F32, work + 16384)
            cT = at("C_T", [P, SG, TOK], F32, work + 20480)
            btok = at("B_tok", [P, NT, SG * ST], F32, work + 24576)
            dtraw = at("dt_raw", [P, NT, SH], F32, work + 28672)
            xtok = at("x_tok", [P, NT, D], F32, outT_at)
            y = at("y_ssm", [P, NT, D], F32, work)
            return bT, cT, btok, dtraw, xtok, y

        ORDER = ([0, 1, 2, 3], [1, 0, 3, 2])

        def ssm_mix(l, tiles, ada_chunks):
            ada_buf = [at(f"ada_unit{i}", [P, KD, 256], F32, merged_at + 8192 * i) for i in range(2)]
            ada_in = [stage_sem(f"ada_in{i}") for i in range(2)]
            ada_used, ada_out, ada_turned = stage_sem("ada_used"), stage_sem("ada_out"), stage_sem("ada_turned")
            ada_row = at("ada_row", [2, 256], F32, work + 51200)
            ada_units = [(la, c, u) for la, c in ada_chunks for u in range(ADA_U)]

            def ada_cols(i):
                return ps[6][:, 256 + 16 * i:272 + 16 * i]

            bT, cT, btok, dtraw, xtok, y = ssm_tensors()
            p0 = work + 28672 + 256
            dtv, dta, tmp1, cums, exps = (at(f"ssm_{n}", [P, w], F32, p0 + o) for n, w, o in (
                ("dt", 128, 0), ("dta", 128, 512), ("tmp", 128, 1024), ("cum_tot", 256, 1536), ("expa", 32, 2560)))
            ecum, wst, dec, skip = (at(f"ssm_{n}", [P, w], F32, p0 + 2688 + o) for n, w, o in (
                ("ecum", 128, 0), ("w_state", 128, 512), ("decay", 128, 1024), ("skip", 16, 1536)))
            cbs = at("CB", [P, 2, P], F32, work + 34816)
            state = at("ssm_state", [P, 2, SG, 512], F32, work + 36864)
            xw = at("x_weighted", [P, 512], F32, work + 45056)
            part = at("y_part", [P, 2, 512], F32, work + 47104)
            seg = at("segments", [P, 2, 2, HG, P], F32, outT_at + 16384)
            hp = heads[l]

            def d4(a, d):
                return a[:, d * 64:(d + 1) * 64].rearrange("p (t h) -> p t h", h=SH)

            def hg(a, d, tile, g):
                b = d * 64 + tile * SH + g * HG
                return a[:, b:b + HG]

            def wide(a):
                return spread(a, HG, HD)

            def by_head(a):
                return a.rearrange("p (h e) -> p h e", h=HG)

            names = ("skipped", "dt_act", "dt_dve", "cum_sum", "cum_out", "exps_done", "seg_sum", "seg_out", "seg_exp", "mixed",
                     "intra", "intra_out", "weighted", "update", "update_out", "inter", "inter_out")
            (skipped, dt_act, dt_dve, cum_sum, cum_out, exps_done, seg_sum, seg_out, seg_exp, mixed,
             intra, intra_out, weighted, update, update_out, inter, inter_out) = (stage_sem(s) for s in names)
            jobs = [(tile, g) for tile in tiles for g in range(SG)]
            steps = [(s, d, g) for s in range(NT) for d in range(2) for g in range(SG)]
            updates = [x for x in steps if x[0] < NT - 1]
            inters = [x for x in steps if x[0] > 0 and ORDER[x[1]][x[0]] in tiles]
            def skips(pool):
                pool_step(pool, pool.tensor_tensor(skip[:, :], hp[:, 72:88], hp[:, 88:104], ALU.add))
                for tile, g in jobs:
                    pool.tensor_tensor(by_head(y[:, tile, g * 512:(g + 1) * 512]), by_head(xtok[:, tile, g * 512:(g + 1) * 512]),
                                       wide(skip[:, g * HG:(g + 1) * HG]), ALU.mult).then_inc(skipped, 1)

            def ada_copy(act, i):
                act.wait_ge(ada_used, i + 1)
                if i:
                    act.wait_ge(ada_turned, i)
                act.activation(ada_row[:, :], ps[6][0:2, 0:256], ACT.Copy).then_inc(ada_out, 1)

            with nc.Block() as block:
                @block.sync
                def _(sp):
                    for i, (la, c, u) in enumerate(ada_units):
                        if i >= 2:
                            sp.wait_ge(ada_used, i - 1)
                        sp.dma_start(ada_buf[i % 2][:, :, :], ada_unit(la, c, u)).then_inc(ada_in[i % 2], 16)

                @block.gpsimd
                def _(pool):
                    skips(pool)

                @block.scalar
                def _(act):
                    act.wait_ge(dt_dve, 1)
                    act_step(act, act.activation(dta[:, :], tmp1[:, :], ACT.Exp, scale=-1.0))
                    act.activation(exps[:, :], hp[:, 40:72], ACT.Exp).then_inc(dt_act, 1)
                    act.wait_ge(dt_dve, 2)
                    act.activation(cums[:, 0:128], tmp1[:, :], ACT.Ln).then_inc(dt_act, 1)
                    act.wait_ge(cum_out, 1)
                    act.activation(ecum[:, :], cums[:, 0:128], ACT.Exp)
                    act.activation(dec[:, :], cums[:, 128:256], ACT.Exp)
                    act.activation(wst[:, :], wst[:, :], ACT.Exp).then_inc(exps_done, 1)
                    for n in range(len(jobs)):
                        act.wait_ge(seg_out, n + 1)
                        for d in range(2):
                            ins = act.activation(seg[:, n % 2, d, :, :], seg[:, n % 2, d, :, :], ACT.Exp)
                        ins.then_inc(seg_exp, 1)
                        ada_copy(act, n)
                    for i in range(len(jobs), len(ada_units)):
                        ada_copy(act, i)

                @block.vector
                def _(dve):
                    for d in range(2):
                        bias = hp[:, 8 + 16 * d:24 + 16 * d].unsqueeze(1).to_broadcast([P, NT, SH])
                        dve_step(dve, dve.tensor_tensor(d4(dtv, d), dtraw[:, :, :], bias, ALU.add))
                    dve.scalar_tensor_tensor(tmp1[:, :], dtv[:, :], -1.0, dtv[:, :], ALU.mult, ALU.max).then_inc(dt_dve, 1)
                    dve.wait_ge(dt_act, 1)
                    dve.tensor_scalar(tmp1[:, :], dta[:, :], 1.0, None, ALU.add).then_inc(dt_dve, 1)
                    dve.wait_ge(dt_dve, 2)
                    dve_step(dve, dve.tensor_scalar(ecum[:, :], tmp1[:, :], -1.0, 1e-30, ALU.add, ALU.max))
                    dve_step(dve, dve.reciprocal(ecum[:, :], ecum[:, :]))
                    dve_step(dve, dve.tensor_tensor(ecum[:, :], ecum[:, :], dta[:, :], ALU.mult))
                    dve.wait_ge(dt_act, 2)
                    dve_step(dve, dve.tensor_tensor(ecum[:, :], ecum[:, :], cums[:, 0:128], ALU.mult))
                    dve_step(dve, dve.scalar_tensor_tensor(dtv[:, :], dtv[:, :], 0.0, ecum[:, :], ALU.max, ALU.add))
                    for d in range(2):
                        ea = exps[:, 16 * d:16 * d + 16].unsqueeze(1).to_broadcast([P, NT, SH])
                        ins = dve.scalar_tensor_tensor(d4(dta, d), d4(dtv, d), -1.0, ea, ALU.mult, ALU.mult)
                    ins.then_inc(dt_dve, 1)
                    dve.wait_ge(cum_sum, 1)
                    dve_step(dve, dve.tensor_copy(cums[:, :], ps[0][:, 0:256]))
                    dve.tensor_tensor(wst[:, :], cums[:, 128:256], cums[:, 0:128], ALU.subtract).then_inc(cum_out, 1)
                    dve.wait_ge(exps_done, 1)
                    dve_step(dve, dve.tensor_tensor(wst[:, :], wst[:, :], dtv[:, :], ALU.mult))
                    def segments(n):
                        tile, g = jobs[n]
                        s = seg[:, n % 2, :, :, :]
                        dve.wait_ge(seg_sum, n + 1)
                        for d in (1, 0):
                            if n >= 2 and d == 0:
                                dve.wait_ge(intra, n - 1)
                            for h in range(HG):
                                bank = ps[2 * d + h // 4]
                                cum = hg(cums, d, tile, g)[:, h:h + 1]
                                dve.scalar_tensor_tensor(s[:, d, h, :], bank[:, (h % 4) * P:(h % 4 + 1) * P], cum,
                                                         const("neg_low" if d == 0 else "neg_up"), ALU.subtract, ALU.add)
                        dve.tensor_copy(cbs[:, n % 2, :], ps[4][:, 0:P]).then_inc(seg_out, 1)

                    def mix(n):
                        tile, g = jobs[n]
                        s = seg[:, n % 2, :, :, :]
                        dve.wait_ge(seg_exp, n + 1)
                        for d in range(2):
                            dt = spread(hg(dtv, d, tile, g), HG, P)
                            dve_step(dve, dve.tensor_tensor(s[:, d, :, :], s[:, d, :, :], dt, ALU.mult))
                        dve_step(dve, dve.tensor_tensor(s[:, 0, :, :], s[:, 0, :, :], s[:, 1, :, :], ALU.add))
                        dve.tensor_tensor(s[:, 0, :, :], s[:, 0, :, :], cbs[:, n % 2, :].unsqueeze(1).to_broadcast([P, HG, P]),
                                          ALU.mult).then_inc(mixed, 1)

                    def add_intra(n):
                        tile, g = jobs[n]
                        yo = y[:, tile, g * 512:(g + 1) * 512]
                        dve.wait_ge(skipped, n + 1)
                        dve.wait_ge(intra, n + 1)
                        dve.tensor_tensor(yo, yo, ps[5 + 2 * (n % 2)][:, :], ALU.add).then_inc(intra_out, 1)

                    segments(0)
                    for n in range(len(jobs)):
                        if n + 1 < len(jobs):
                            segments(n + 1)
                        mix(n)
                        if n:
                            add_intra(n - 1)
                    add_intra(len(jobs) - 1)
                    n_up = n_in = 0
                    for s, d, g in steps:
                        tile = ORDER[d][s]
                        if s < NT - 1:
                            if n_up:
                                dve.wait_ge(update, n_up)
                            dve.tensor_tensor(by_head(xw[:, :]), by_head(xtok[:, tile, g * 512:(g + 1) * 512]),
                                              wide(hg(wst, d, tile, g)), ALU.mult).then_inc(weighted, 1)
                        if (s, d, g) in inters:
                            dve.wait_ge(inter, n_in + 1)
                            yo = y[:, tile, g * 512:(g + 1) * 512]
                            pt = part[:, n_in % 2, :]
                            dve_step(dve, dve.tensor_tensor(by_head(pt), by_head(ps[2 + n_in % 2][:, :]),
                                                            wide(hg(ecum, d, tile, g)), ALU.mult))
                            dve.tensor_tensor(yo, yo, pt, ALU.add).then_inc(inter_out, 1)
                            n_in += 1
                        if s < NT - 1:
                            st = state[:, d, g, :]
                            if s:
                                dve_step(dve, dve.tensor_tensor(by_head(st), by_head(st), wide(hg(dec, d, tile, g)), ALU.mult))
                            dve.wait_ge(update, n_up + 1)
                            if s:
                                dve.tensor_tensor(st, st, ps[n_up % 2][:, :], ALU.add).then_inc(update_out, 1)
                            else:
                                dve.tensor_copy(st, ps[n_up % 2][:, :]).then_inc(update_out, 1)
                            n_up += 1
                    dve.wait_ge(ada_turned, len(ada_units))
                    for i, (la, c) in enumerate(ada_chunks):
                        ada_finish(dve, la, c, ada_cols(i))

                @block.tensor
                def _(pe):
                    todo = list(enumerate(ada_units))

                    def turn_row(i):
                        pe.wait_ge(ada_out, i + 1)
                        ada_turn(pe, ada_cols(i // ADA_U), ada_row, ada_units[i][2]).then_inc(ada_turned, 1)

                    def modulation():
                        if todo:
                            i, _ = todo.pop(0)
                            if i:
                                turn_row(i - 1)
                            pe.wait_ge(ada_in[i % 2], 16 * (i // 2 + 1))
                            ada_rows(pe, ps[6][0:2, 0:256], ada_buf[i % 2]).then_inc(ada_used, 1)

                    pe.wait_ge(dt_dve, 3)
                    for d, tri in enumerate(("tri_f", "tri_b")):
                        pe.matmul(ps[0][:, 64 * d:64 * d + 64], const(tri), dta[:, 64 * d:64 * d + 64], start=True, stop=True)
                        last = pe.matmul(ps[0][:, 128 + 64 * d:192 + 64 * d], const("ones"), dta[:, 64 * d:64 * d + 64],
                                         start=True, stop=True)
                    last.then_inc(cum_sum, 1)
                    pe.wait_ge(cum_out, 1)
                    for n in range(len(jobs) + 2):
                        if n < len(jobs):
                            tile, g = jobs[n]
                            tok = slice(tile * P, (tile + 1) * P)
                            if n:
                                pe.wait_ge(seg_out, n)
                            pe.matmul(ps[4][:, 0:P], bT[:, g, tok], cT[:, g, tok], start=True, stop=True)
                            for d, tri in enumerate(("tri_f", "tri_b")):
                                for h in range(HG):
                                    w = hg(dta, d, tile, g)[:, h:h + 1].to_broadcast([P, P])
                                    last = pe.matmul(ps[2 * d + h // 4][:, (h % 4) * P:(h % 4 + 1) * P], w, const(tri),
                                                     start=True, stop=True)
                            last.then_inc(seg_sum, 1)
                        if n >= 2:
                            tile, g = jobs[n - 2]
                            pe.wait_ge(mixed, n - 1)
                            if n >= 4:
                                pe.wait_ge(intra_out, n - 3)
                            for h in range(HG):
                                c = (g * HG + h) * HD
                                last = pe.matmul(ps[5 + 2 * (n % 2)][:, h * HD:(h + 1) * HD],
                                                 seg[:, n % 2, 0, h, :], xtok[:, tile, c:c + HD], start=True, stop=True)
                            last.then_inc(intra, 1)
                        if n < len(jobs):
                            modulation()
                    n_up = n_in = 0
                    for s, d, g in steps:
                        modulation()
                        tile = ORDER[d][s]
                        if (s, d, g) in inters:
                            pe.wait_ge(update_out, 4 * (s - 1) + 2 * d + g + 1)
                            if n_in >= 2:
                                pe.wait_ge(inter_out, n_in - 1)
                            pe.matmul(ps[2 + n_in % 2][:, :], cT[:, g, tile * P:(tile + 1) * P], state[:, d, g, :],
                                      start=True, stop=True).then_inc(inter, 1)
                            n_in += 1
                        if s < NT - 1:
                            pe.wait_ge(weighted, n_up + 1)
                            if n_up >= 2:
                                pe.wait_ge(update_out, n_up - 1)
                            pe.matmul(ps[n_up % 2][:, :], btok[:, tile, g * ST:(g + 1) * ST], xw[:, :],
                                      start=True, stop=True).then_inc(update, 1)
                            n_up += 1
                    while todo:
                        modulation()
                    turn_row(len(ada_units) - 1)
            end_stage()

        def turn_to_outT(pe, src, tiles, f_range, ready, turned, parts):
            for f in f_range:
                if ready is not None:
                    pe.wait_ge(*ready(f))
                if f >= 8:
                    pe.wait_ge(parts, f - 7)
                for j, tile in enumerate(tiles):
                    last = pe.transpose(ps[f % 8][:, j * P:(j + 1) * P], src[:, tile, f * P:(f + 1) * P], ident)
                last.then_inc(turned, 1)

        def outT_hi(act, tiles, f, turned, hi_out, scale=1.0):
            lo, n = tiles[0] * P, len(tiles) * P
            act.wait_ge(turned, f + 1)
            act.activation(outT[0][:, f, lo:lo + n], ps[f % 8][:, 0:n], ACT.Identity if not isinstance(scale, float) else ACT.Copy,
                           scale=scale).then_inc(hi_out, 1)

        def outT_lo(dve, tiles, f, hi_out, parts, scale=1.0):
            lo, n = tiles[0] * P, len(tiles) * P
            dve.wait_ge(hi_out, f + 1)
            dve.scalar_tensor_tensor(outT[1][:, f, lo:lo + n], ps[f % 8][:, 0:n], scale,
                                     outT[0][:, f, lo:lo + n].bitcast(F32), ALU.mult, ALU.subtract).then_inc(parts, 1)

        def ssm_gate(l, tiles):
            a0, b0 = span[f"z{l}"]
            y = ssm_tensors()[5]
            gate = at("z_gate", [P, NT, 512], F32, work + 16384)
            junk = at("squares_junk", [P, 512], F32, work + 24576)
            gated, silu_out, squared, roots, scaled, turned, hi_out, parts = (
                stage_sem(s) for s in ("gated", "silu_out", "squared", "roots", "scaled", "turned", "hi_out", "parts"))
            ssq = small[:, 8:16]
            n = len(tiles)
            lo = 2 * tiles[0]
            with nc.Block() as block:
                @block.sync
                def _(sp):
                    loads(sp, f"z{l}")

                @block.gpsimd
                def _(pool):
                    splits_lo(pool, f"z{l}")

                @block.scalar
                def _(act):
                    for g in range(SG):
                        for u in range(2):
                            split_hi(act, a0 + 2 * g + u + 2)
                        act.wait_ge(unit_used, a0 + 2 * g + 2)
                        if g:
                            act.wait_ge(gated, n)
                        for j in range(n):
                            act.activation(gate[:, j, :], ps[4 * g + j][:, :], ACT.Silu).then_inc(silu_out, 1)
                        for j, tile in enumerate(tiles):
                            act.wait_ge(gated, n * g + j + 1)
                            act_step(act, act.activation(junk[:, :], y[:, tile, g * 512:(g + 1) * 512], ACT.Square,
                                                         accum_out=ssq[:, 2 * tile + g:2 * tile + g + 1]))
                    act.activation(small[:, 16:17], small[:, 0:1], ACT.Copy).then_inc(squared, 1)
                    act.wait_ge(roots, 1)
                    act.activation(ssq[:, lo:8], ssq[:, lo:8], ACT.Sqrt).then_inc(roots, 1)
                    for f in range(KD):
                        outT_hi(act, tiles, f, turned, hi_out, norm_cols[l][:, 16 + f:17 + f])

                @block.vector
                def _(dve):
                    for g in range(SG):
                        for j, tile in enumerate(tiles):
                            dve.wait_ge(silu_out, n * g + j + 1)
                            yo = y[:, tile, g * 512:(g + 1) * 512]
                            dve.tensor_tensor(yo, yo, gate[:, j, :], ALU.mult).then_inc(gated, 1)
                    dve.wait_ge(squared, 1)
                    dve.tensor_scalar(ssq[:, lo:8], ssq[:, lo:8], 1.0 / 512, EPS, ALU.mult, ALU.add).then_inc(roots, 1)
                    dve.wait_ge(roots, 2)
                    dve_step(dve, dve.reciprocal(ssq[:, lo:8], ssq[:, lo:8]))
                    for g in range(SG):
                        for tile in tiles:
                            yo = y[:, tile, g * 512:(g + 1) * 512]
                            ins = dve.tensor_scalar(yo, yo, ssq[:, 2 * tile + g:2 * tile + g + 1], None, ALU.mult)
                        ins.then_inc(scaled, 1)
                    for f in range(KD):
                        outT_lo(dve, tiles, f, hi_out, parts, norm_cols[l][:, 16 + f:17 + f])

                @block.tensor
                def _(pe):
                    for g in range(SG):
                        project(pe, a0 + 2 * g, [4 * g + j for j in range(n)], tiles)
                    turn_to_outT(pe, y, tiles, range(KD), lambda f: (scaled, f // 4 + 1), turned, parts)
            end_stage()

        def merge(l, branch, tiles, first):
            a0, b0 = span[f"merge{branch}_{l}"]
            gate = at("merge_gate", [P, 2, NT, 512], F32, work)
            part = at("merge_part", [P, 2, 512], F32, work + 16384)
            gate_out, merged_out = stage_sem("gate_out"), stage_sem("merged_out")
            n = len(tiles)
            with nc.Block() as block:
                @block.sync
                def _(sp):
                    loads(sp, f"merge{branch}_{l}")

                @block.gpsimd
                def _(pool):
                    splits_lo(pool, f"merge{branch}_{l}")

                @block.scalar
                def _(act):
                    for b in range(2):
                        for u in range(2):
                            split_hi(act, a0 + 4 * b + u + 2)
                        act.wait_ge(unit_used, a0 + 4 * b + 2)
                        for j in range(n):
                            act.activation(gate[:, b, j, :], ps[j][:, :], ACT.Sigmoid).then_inc(gate_out, 1)
                        for u in range(2, 4):
                            split_hi(act, a0 + 4 * b + u + 2)

                @block.vector
                def _(dve):
                    for b in range(2):
                        dve.wait_ge(unit_used, a0 + 4 * b + 4)
                        for j, tile in enumerate(tiles):
                            dve.wait_ge(gate_out, n * b + j + 1)
                            out = merged[:, tile, b * 512:(b + 1) * 512]
                            if first:
                                dve.tensor_tensor(out, gate[:, b, j, :], ps[4 + j][:, :], ALU.mult).then_inc(merged_out, 1)
                            else:
                                pt = part[:, j % 2, :]
                                dve_step(dve, dve.tensor_tensor(pt, gate[:, b, j, :], ps[4 + j][:, :], ALU.mult))
                                dve.tensor_tensor(out, out, pt, ALU.add).then_inc(merged_out, 1)

                @block.tensor
                def _(pe):
                    for b in range(2):
                        if b:
                            pe.wait_ge(gate_out, n)
                        project(pe, a0 + 4 * b, range(n), tiles)
                        if b:
                            pe.wait_ge(merged_out, n)
                        project(pe, a0 + 4 * b + 2, [4 + j for j in range(n)], tiles, outT)
            end_stage()

        def rope(dve, out, src, tile, table, n_heads, tmp, axial):
            half = 32 if axial else 64
            pairs = n_heads * (2 if axial else 1)

            def parts(a):
                v = a.rearrange("p (h e w) -> p h e w", e=2, w=half)
                return v[:, :, 0, :], v[:, :, 1, :]

            def angle(kind):
                a = const(f"{table}_{kind}")[:, 64 * (tile - 2):64 * (tile - 1)]
                if axial:
                    return a.rearrange("p (e w) -> p e w", w=half).unsqueeze(1).to_broadcast([P, n_heads, 2, half])
                return a.unsqueeze(1).to_broadcast([P, n_heads, half])

            def shaped(a):
                return a.rearrange("p (h e) w -> p h e w", e=2) if axial else a

            w = pairs * half
            s1, s2 = (shaped(v) for v in parts(src))
            o1, o2 = (shaped(v) for v in parts(out))
            m = [shaped(tmp[:, i, 0:w].rearrange("p (h w) -> p h w", w=half)) for i in range(4)]
            cos, sin = angle("cos"), angle("sin")
            dve.tensor_tensor(m[0], s1, cos, ALU.mult)
            dve.tensor_tensor(m[1], s2, sin, ALU.mult)
            dve.tensor_tensor(m[2], s1, sin, ALU.mult)
            dve_step(dve, dve.tensor_tensor(m[3], s2, cos, ALU.mult))
            dve.tensor_tensor(o1, m[0], m[1], ALU.subtract)
            return dve.tensor_tensor(o2, m[2], m[3], ALU.add)

        def ret_tensors():
            ktok = at("k_tok", [P, NT, RH * DK], F32, work)
            qT = at("ret_qT", [P, RH, TOK], F32, work + 8192)
            kT = at("ret_kT", [P, RH, TOK], F32, work + 16384)
            o = at("ret_o", [P, NT, D], F32, work + 24576)
            qtok = at("q_tok", [P, NT, RH * DK], F32, work + 40960)
            v = at("ret_v", [P, NT, D], F32, outT_at)
            return ktok, qT, kT, o, qtok, v

        def ret_project(l, q_tiles):
            a0, b0 = span[f"ret{l}"]
            ktok, qT, kT, o, qtok, v = ret_tensors()
            tmp = at("rope_tmp", [P, 4, 256], F32, outT_at + 16384)
            out, turned, turned_out = stage_sem("out"), stage_sem("turned"), stage_sem("turned_out")
            blocks = [q_tiles, ALL_TILES, ALL_TILES, ALL_TILES]
            done = np.cumsum([len(b) for b in blocks]).tolist()
            banks = [[4 * (n % 2) + j for j in range(len(b))] for n, b in enumerate(blocks)]
            with nc.Block() as block:
                @block.sync
                def _(sp):
                    loads(sp, f"ret{l}")

                @block.gpsimd
                def _(pool):
                    splits_lo(pool, f"ret{l}")

                @block.scalar
                def _(act):
                    for n in range(4):
                        for u in range(2):
                            split_hi(act, a0 + 2 * n + u + 2)
                        if n >= 2:
                            act.wait_ge(unit_used, a0 + 2 * n + 2)
                            act.wait_ge(out, done[n - 1])
                            for j, tile in enumerate(blocks[n]):
                                act.activation(v[:, tile, (n - 2) * 512:(n - 1) * 512], ps[banks[n][j]][:, :],
                                               ACT.Copy).then_inc(out, 1)
                    for i in range(2 * RH):
                        act.wait_ge(turned, i + 1)
                        dst, h = (qT, i) if i < RH else (kT, i - RH)
                        lo = q_tiles[0] * P if i < RH else 0
                        act.activation(dst[:, h, lo:TOK], ps[i][:, 0:TOK - lo], ACT.Copy).then_inc(turned_out, 1)

                @block.vector
                def _(dve):
                    for n, (dst, table) in enumerate(((qtok, "rq"), (ktok, "rk"))):
                        dve.wait_ge(unit_used, a0 + 2 * n + 2)
                        for j, tile in enumerate(blocks[n]):
                            src = ps[banks[n][j]][:, :]
                            if tile < 2:
                                scale = 1.0 if n == 0 else DK ** -0.5
                                dve.tensor_scalar(dst[:, tile, :], src, scale, None, ALU.mult).then_inc(out, 1)
                            else:
                                rope(dve, dst[:, tile, :], src, tile, table, RH, tmp, False).then_inc(out, 1)
                                dve.wait_ge(out, (done[n - 1] if n else 0) + j + 1)

                @block.tensor
                def _(pe):
                    for n in range(4):
                        if n >= 2:
                            pe.wait_ge(out, done[n - 2])
                        project(pe, a0 + 2 * n, banks[n], blocks[n])
                    pe.wait_ge(out, done[3])
                    for i in range(2 * RH):
                        src, h, tiles = (qtok, i, q_tiles) if i < RH else (ktok, i - RH, ALL_TILES)
                        for j, tile in enumerate(tiles):
                            last = pe.transpose(ps[i][:, j * P:(j + 1) * P], src[:, tile, h * DK:(h + 1) * DK], ident)
                        last.then_inc(turned, 1)
            end_stage()

        def ret_mix(l, tiles):
            ktok, qT, kT, o, qtok, v = ret_tensors()
            base = outT_at + 16384
            decay = at("ret_decays", [P, RH, P], F32, base)
            state = at("ret_state", [P, 2, RH, DV], F32, base + 2048)
            kw = at("k_weighted", [P, RH * DK], F32, base + 10240)
            part = at("ret_part", [P, 2, 512], F32, base + 12288)
            mix = at("ret_mix", [P, 2, RH * P], F32, work + 40960)
            logs, t1, t2 = small[:, 20:28], small[:, 28:36], small[:, 36:44]
            wts, gam = small[:, 48:80], small[:, 80:88]
            names = ("lg_dve", "lg_act", "exps_done", "decay_done", "scores", "mixed", "intra", "intra_out",
                     "weighted", "update", "update_out", "inter", "inter_out")
            (lg_dve, lg_act, exps_done, decay_done, scores, mixed, intra, intra_out,
             weighted, update, update_out, inter, inter_out) = (stage_sem(s) for s in names)
            n = len(tiles)
            steps = [(s, d) for s in range(NT) for d in range(2)]
            tmp = at("decay_exps", [P, 8, P], F32, work + 45056)

            def w_of(kind, d):
                return wts[:, kind * 8 + d * 4:kind * 8 + d * 4 + 4]

            with nc.Block() as block:
                @block.scalar
                def _(act):
                    act.wait_ge(lg_dve, 1)
                    act.activation(t2, t1, ACT.Exp, scale=-1.0).then_inc(lg_act, 1)
                    act.wait_ge(lg_dve, 2)
                    act.activation(t2, t2, ACT.Ln).then_inc(lg_act, 1)
                    act.wait_ge(lg_dve, 3)
                    for d in range(2):
                        for h in range(RH):
                            act.activation(tmp[:, 4 * d + h, :], const("dist_f" if d == 0 else "dist_b"), ACT.Exp,
                                           scale=logs[:, 4 * d + h:4 * d + h + 1])
                    for kind in range(4):
                        act.activation(wts[:, kind * 8:kind * 8 + 8], logs, ACT.Exp,
                                       scale=const("ret_w")[:, kind:kind + 1])
                    act.activation(gam, logs, ACT.Exp, scale=float(P)).then_inc(exps_done, 1)
                    for j, tile in enumerate(tiles):
                        for b in range(2):
                            act.wait_ge(intra, 2 * j + b + 1)
                            act.activation(o[:, tile, b * 512:(b + 1) * 512], ps[2 + b][:, :], ACT.Copy).then_inc(intra_out, 1)

                @block.vector
                def _(dve):
                    r = heads[l][:, 0:8]
                    dve.scalar_tensor_tensor(t1, r, -1.0, r, ALU.mult, ALU.max).then_inc(lg_dve, 1)
                    dve.wait_ge(lg_act, 1)
                    dve.tensor_scalar(t2, t2, 1.0, None, ALU.add).then_inc(lg_dve, 1)
                    dve.wait_ge(lg_act, 2)
                    dve.scalar_tensor_tensor(logs, r, 0.0, t2, ALU.min, ALU.subtract).then_inc(lg_dve, 1)
                    dve.wait_ge(exps_done, 1)
                    for d in range(2):
                        tri = const("tri_f" if d == 0 else "tri_b").unsqueeze(1).to_broadcast([P, RH, P])
                        dve_step(dve, dve.tensor_tensor(tmp[:, 4 * d:4 * d + 4, :], tmp[:, 4 * d:4 * d + 4, :], tri, ALU.mult))
                    dve.tensor_tensor(decay[:, :, :], tmp[:, 0:4, :], tmp[:, 4:8, :], ALU.add).then_inc(decay_done, 1)
                    dve.wait_ge(decay_done, 1)
                    for j, tile in enumerate(tiles):
                        dve.wait_ge(scores, j + 1)
                        dve.tensor_tensor(mix[:, j % 2, :], ps[j % 2][:, :], decay[:, :, :].rearrange("p h i -> p (h i)"),
                                          ALU.mult).then_inc(mixed, 1)
                    n_in = n_up = 0
                    for s, d in steps:
                        tile = ORDER[d][s]
                        if s < NT - 1:
                            if n_up:
                                dve.wait_ge(update, n_up)
                            dve.tensor_tensor(kw[:, :].rearrange("p (h e) -> p h e", h=RH),
                                              ktok[:, tile, :].rearrange("p (h e) -> p h e", h=RH),
                                              spread(w_of(d, d), RH, DK), ALU.mult).then_inc(weighted, 1)
                        if s > 0 and tile in tiles:
                            if n_in == 0:
                                dve.wait_ge(intra_out, 2 * n)
                            for b in range(2):
                                dve.wait_ge(inter, n_in + 1)
                                pt = part[:, b, :]
                                dve_step(dve, dve.tensor_tensor(pt.rearrange("p (h e) -> p h e", h=2),
                                                                ps[4 + b][:, :].rearrange("p (h e) -> p h e", h=2),
                                                                spread(w_of(2 + d, d)[:, 2 * b:2 * b + 2], 2, DV), ALU.mult))
                                oo = o[:, tile, b * 512:(b + 1) * 512]
                                dve.tensor_tensor(oo, oo, pt, ALU.add).then_inc(inter_out, 1)
                                n_in += 1
                        if s < NT - 1:
                            dve.wait_ge(update, n_up + 1)
                            for h in range(RH):
                                st = state[:, d, h, :]
                                u = ps[6 + h // 2][:, (h % 2) * DV:(h % 2 + 1) * DV]
                                if s:
                                    ins = dve.scalar_tensor_tensor(st, st, gam[:, 4 * d + h:4 * d + h + 1], u, ALU.mult, ALU.add)
                                else:
                                    ins = dve.tensor_copy(st, u)
                            ins.then_inc(update_out, 1)
                            n_up += 1

                @block.tensor
                def _(pe):
                    for j in range(n + 1):
                        if j < n:
                            tok = slice(tiles[j] * P, (tiles[j] + 1) * P)
                            if j >= 2:
                                pe.wait_ge(mixed, j - 1)
                            for h in range(RH):
                                last = pe.matmul(ps[j % 2][:, h * P:(h + 1) * P], kT[:, h, tok], qT[:, h, tok], start=True, stop=True)
                            last.then_inc(scores, 1)
                        if j >= 1:
                            tile = tiles[j - 1]
                            pe.wait_ge(mixed, j)
                            for b in range(2):
                                if j >= 2:
                                    pe.wait_ge(intra_out, 2 * (j - 2) + b + 1)
                                for h in (2 * b, 2 * b + 1):
                                    last = pe.matmul(ps[2 + b][:, (h % 2) * DV:(h % 2 + 1) * DV],
                                                     mix[:, (j - 1) % 2, h * P:(h + 1) * P],
                                                     v[:, tile, h * DV:(h + 1) * DV], start=True, stop=True)
                                last.then_inc(intra, 1)
                    n_in = n_up = 0
                    for s, d in steps:
                        tile = ORDER[d][s]
                        if s > 0 and tile in tiles:
                            pe.wait_ge(update_out, 2 * (s - 1) + d + 1)
                            for b in range(2):
                                if n_in >= 2:
                                    pe.wait_ge(inter_out, n_in - 1)
                                for h in (2 * b, 2 * b + 1):
                                    last = pe.matmul(ps[4 + b][:, (h % 2) * DV:(h % 2 + 1) * DV],
                                                     qT[:, h, tile * P:(tile + 1) * P], state[:, d, h, :], start=True, stop=True)
                                last.then_inc(inter, 1)
                                n_in += 1
                        if s < NT - 1:
                            pe.wait_ge(weighted, n_up + 1)
                            if n_up:
                                pe.wait_ge(update_out, n_up)
                            for h in range(RH):
                                last = pe.matmul(ps[6 + h // 2][:, (h % 2) * DV:(h % 2 + 1) * DV],
                                                 kw[:, h * DK:(h + 1) * DK], v[:, tile, h * DV:(h + 1) * DV], start=True, stop=True)
                            last.then_inc(update, 1)
                            n_up += 1
            end_stage()

        def ret_gate(l, tiles):
            a0, b0 = span[f"g{l}"]
            o = ret_tensors()[3]
            gate = at("ret_silu", [P, NT, 512], F32, work)
            junk = at("ret_junk", [P, DV], F32, work + 8192)
            squared, roots, silu_out, gated, turned, hi_out, parts = (
                stage_sem(s) for s in ("squared", "roots", "silu_out", "gated", "turned", "hi_out", "parts"))
            ssq = small[:, 0:16]
            n, lo = len(tiles), 4 * tiles[0]
            with nc.Block() as block:
                @block.sync
                def _(sp):
                    loads(sp, f"g{l}")

                @block.gpsimd
                def _(pool):
                    splits_lo(pool, f"g{l}")

                @block.scalar
                def _(act):
                    for tile in tiles:
                        for h in range(RH):
                            ins = act.activation(junk[:, :], o[:, tile, h * DV:(h + 1) * DV], ACT.Square,
                                                 accum_out=ssq[:, 4 * tile + h:4 * tile + h + 1])
                            act_step(act, ins)
                    act.activation(small[:, 16:17], small[:, lo:lo + 1], ACT.Copy).then_inc(squared, 1)
                    act.wait_ge(roots, 1)
                    act.activation(ssq[:, lo:16], ssq[:, lo:16], ACT.Sqrt).then_inc(roots, 1)
                    for b in range(2):
                        for u in range(2):
                            split_hi(act, a0 + 2 * b + u + 2)
                        act.wait_ge(unit_used, a0 + 2 * b + 2)
                        if b:
                            act.wait_ge(gated, n)
                        for j in range(n):
                            act.activation(gate[:, j, :], ps[4 * b + j][:, :], ACT.Silu).then_inc(silu_out, 1)
                    for f in range(KD):
                        outT_hi(act, tiles, f, turned, hi_out)

                @block.vector
                def _(dve):
                    dve.wait_ge(squared, 1)
                    dve.tensor_scalar(ssq[:, lo:16], ssq[:, lo:16], 1.0 / DV, EPS, ALU.mult, ALU.add).then_inc(roots, 1)
                    dve.wait_ge(roots, 2)
                    dve_step(dve, dve.reciprocal(ssq[:, lo:16], ssq[:, lo:16]))
                    for b in range(2):
                        for j, tile in enumerate(tiles):
                            dve.wait_ge(silu_out, n * b + j + 1)
                            for h in range(2):
                                hh = 2 * b + h
                                oo = o[:, tile, hh * DV:(hh + 1) * DV]
                                ins = dve.scalar_tensor_tensor(oo, oo, ssq[:, 4 * tile + hh:4 * tile + hh + 1],
                                                               gate[:, j, h * DV:(h + 1) * DV], ALU.mult, ALU.mult)
                            ins.then_inc(gated, 1)
                    for f in range(KD):
                        outT_lo(dve, tiles, f, hi_out, parts)

                @block.tensor
                def _(pe):
                    for b in range(2):
                        project(pe, a0 + 2 * b, [4 * b + j for j in range(n)], tiles)
                    turn_to_outT(pe, o, tiles, range(KD), lambda f: (gated, n * (f // 4 + 1)), turned, parts)
            end_stage()

        def att_tensors():
            qT = at("att_qT", [P, AH, TOK], F32, work)
            kT = at("att_kT", [P, KVH, TOK], F32, work + 16384)
            v = at("att_v", [P, NT, KVH * AD], F32, work + 20480)
            tok = at("att_tok", [P, NT, 512], F32, work + 24576)
            return qT, kT, v, tok

        def att_project(l, q_tiles):
            a0, b0 = span[f"att{l}"]
            qT, kT, v, tok = att_tensors()
            tmp = at("att_rope_tmp", [P, 4, 256], F32, work + 32768)
            out, turned, turned_out = stage_sem("out"), stage_sem("turned"), stage_sem("turned_out")
            blocks = [q_tiles, q_tiles, ALL_TILES]
            heads_of = [4, 4, 2]
            done = np.cumsum([len(b) for b in blocks]).tolist()
            turns = [0, 4, 8, 10]
            bank0 = [0, 4, 0]
            with nc.Block() as block:
                @block.sync
                def _(sp):
                    loads(sp, f"att{l}")

                @block.gpsimd
                def _(pool):
                    splits_lo(pool, f"att{l}")

                @block.scalar
                def _(act):
                    for n in range(3):
                        for u in range(2):
                            split_hi(act, a0 + 2 * n + u + 2)
                        for i in range(turns[n], turns[n + 1]):
                            m = i - turns[n]
                            act.wait_ge(turned, i + 1)
                            dst = qT[:, i, :] if n < 2 else kT[:, m, :]
                            lo = q_tiles[0] * P if n < 2 else 0
                            act.activation(dst[:, lo:TOK], ps[bank0[n] + m][:, 0:TOK - lo], ACT.Copy).then_inc(turned_out, 1)

                @block.vector
                def _(dve):
                    for n in range(3):
                        w = heads_of[n] * AD
                        dve.wait_ge(unit_used, a0 + 2 * n + 2)
                        if n:
                            dve.wait_ge(turned, turns[n])
                        for j, tile in enumerate(blocks[n]):
                            src = ps[bank0[n] + j]
                            if n == 2:
                                dve.tensor_copy(v[:, tile, :], src[:, 256:512])
                            if tile < 2:
                                dve.tensor_scalar(tok[:, tile, 0:w], src[:, 0:w], AD ** -0.5 if n < 2 else 1.0, None,
                                                  ALU.mult).then_inc(out, 1)
                            else:
                                rope(dve, tok[:, tile, 0:w], src[:, 0:w], tile, "aq" if n < 2 else "ak", heads_of[n],
                                     tmp, True).then_inc(out, 1)
                                dve.wait_ge(out, (done[n - 1] if n else 0) + j + 1)

                @block.tensor
                def _(pe):
                    for n in range(3):
                        if n == 2:
                            pe.wait_ge(turned_out, turns[1])
                        project(pe, a0 + 2 * n, [bank0[n] + j for j in range(len(blocks[n]))], blocks[n])
                        pe.wait_ge(out, done[n])
                        for i in range(turns[n], turns[n + 1]):
                            m = i - turns[n]
                            for j, tile in enumerate(blocks[n]):
                                last = pe.transpose(ps[bank0[n] + m][:, j * P:(j + 1) * P], tok[:, tile, m * AD:(m + 1) * AD], ident)
                            last.then_inc(turned, 1)
            end_stage()

        def att_mix(l, tiles):
            qT, kT, v, tok = att_tensors()
            pr = at("att_probs", [P, 2, AG, 512], F32, work + 24576)
            pT = at("att_probs_T", [P, NT, AG * P], F32, work + 40960)
            scores, maxed, summed, normed, turned, turned_out, summed_v, hi_out, parts = (
                stage_sem(s) for s in ("scores", "maxed", "summed", "normed", "turned", "turned_out", "summed_v", "hi_out", "parts"))
            sink = heads[l][:, 104:112]
            jobs = [(tile, kv) for tile in tiles for kv in range(KVH)]

            def sc(i, job):
                a = 32 + 16 * (job % 2) + 4 * i
                return small[:, a:a + 4]

            def keys(tile):
                return 2 if tile < 2 else NT

            with nc.Block() as block:
                @block.scalar
                def _(act):
                    for n in range(len(jobs) + 1):
                        if n < len(jobs):
                            w = keys(jobs[n][0]) * P
                            act.wait_ge(maxed, n + 1)
                            for h in range(AG):
                                act.activation(pr[:, n % 2, h, 0:w], ps[h][:, 0:w], ACT.Exp, bias=sc(0, n)[:, h:h + 1],
                                               accum_out=sc(2, n)[:, h:h + 1])
                            act.activation(sc(1, n), sc(1, n), ACT.Exp).then_inc(summed, 1)
                        if n:
                            tile, kv = jobs[n - 1]
                            act.wait_ge(summed_v, n)
                            act.activation(outT[0][:, 4 * kv:4 * kv + 4, tile * P:(tile + 1) * P],
                                           ps[6 + (n - 1) % 2][:, :].rearrange("p (h t) -> p h t", h=AG), ACT.Copy).then_inc(hi_out, 1)

                @block.vector
                def _(dve):
                    def maxima(n):
                        tile, kv = jobs[n]
                        w = keys(tile) * P
                        dve.wait_ge(scores, n + 1)
                        if tile >= 2:
                            other = 5 - tile
                            for h in range(AG):
                                s = ps[h][:, other * P:(other + 1) * P]
                                ins = dve.tensor_tensor(s, s, const("neg_up" if tile == 2 else "neg_low"), ALU.add)
                            dve_step(dve, ins)
                        mx = sc(0, n)
                        for h in range(AG):
                            ins = dve.tensor_reduce(mx[:, h:h + 1], ps[h][:, 0:w], AX.X, ALU.max)
                        dve_step(dve, ins)
                        sk = sink[:, 4 * kv:4 * kv + 4]
                        dve_step(dve, dve.tensor_tensor(mx, mx, sk, ALU.max))
                        dve_step(dve, dve.tensor_tensor(sc(1, n), sk, mx, ALU.subtract))
                        dve.tensor_scalar(mx, mx, -1.0, None, ALU.mult).then_inc(maxed, 1)

                    def normalize(n):
                        w = keys(jobs[n][0]) * P
                        dve.wait_ge(summed, n + 1)
                        dve_step(dve, dve.tensor_tensor(sc(2, n), sc(2, n), sc(1, n), ALU.add))
                        dve_step(dve, dve.reciprocal(sc(2, n), sc(2, n)))
                        for h in range(AG):
                            ins = dve.tensor_scalar(pr[:, n % 2, h, 0:w], pr[:, n % 2, h, 0:w], sc(2, n)[:, h:h + 1], None, ALU.mult)
                        ins.then_inc(normed, 1)

                    def tail(n):
                        tile, kv = jobs[n]
                        dve.wait_ge(hi_out, n + 1)
                        s = slice(tile * P, (tile + 1) * P)
                        dve.tensor_tensor(outT[1][:, 4 * kv:4 * kv + 4, s], ps[6 + n % 2][:, :].rearrange("p (h t) -> p h t", h=AG),
                                          outT[0][:, 4 * kv:4 * kv + 4, s].bitcast(F32), ALU.subtract).then_inc(parts, 1)

                    maxima(0)
                    normalize(0)
                    n_turn = 0
                    for n, (tile, kv) in enumerate(jobs):
                        if n + 1 < len(jobs):
                            maxima(n + 1)
                        if n:
                            dve.wait_ge(summed_v, n)
                        for k in range(keys(tile)):
                            dve.wait_ge(turned, n_turn + 1)
                            dve.tensor_copy(pT[:, k, :], ps[4 + k % 2][:, :]).then_inc(turned_out, 1)
                            n_turn += 1
                        if n + 1 < len(jobs):
                            normalize(n + 1)
                        if n:
                            tail(n - 1)
                    tail(len(jobs) - 1)

                @block.tensor
                def _(pe):
                    def score(n):
                        tile, kv = jobs[n]
                        if n:
                            pe.wait_ge(summed, n)
                        w = keys(tile) * P
                        for h in range(AG):
                            last = pe.matmul(ps[h][:, 0:w], qT[:, AG * kv + h, tile * P:(tile + 1) * P],
                                             kT[:, kv, 0:w], start=True, stop=True)
                        last.then_inc(scores, 1)

                    score(0)
                    n_turn = 0
                    for n, (tile, kv) in enumerate(jobs):
                        nk = keys(tile)
                        if n + 1 < len(jobs):
                            score(n + 1)
                        pe.wait_ge(normed, n + 1)
                        for k in range(nk):
                            if n_turn >= 2:
                                pe.wait_ge(turned_out, n_turn - 1)
                            for h in range(AG):
                                last = pe.transpose(ps[4 + k % 2][:, h * P:(h + 1) * P], pr[:, n % 2, h, k * P:(k + 1) * P], ident)
                            last.then_inc(turned, 1)
                            n_turn += 1
                        if n >= 2:
                            pe.wait_ge(parts, n - 1)
                        pe.wait_ge(turned_out, n_turn)
                        for k in range(nk):
                            last = pe.matmul(ps[6 + n % 2][:, :], v[:, k, kv * AD:(kv + 1) * AD], pT[:, k, :],
                                             start=k == 0, stop=k == nk - 1)
                        last.then_inc(summed_v, 1)
            end_stage()

        def post_rows_pe(pe, l, which, conds, rows_sum, rows_out, banks):
            for i, c in enumerate(conds):
                for half in range(2):
                    m = 2 * i + half
                    if m >= len(banks):
                        pe.wait_ge(rows_out, m - len(banks) + 1)
                    for d in range(4):
                        w = gains[l][:, 2 + which, 4 * half + d, c:c + 1].to_broadcast([P, P])
                        last = pe.matmul(ps[banks[m % len(banks)]][:, d * P:(d + 1) * P], w, ident, start=True, stop=True)
                    last.then_inc(rows_sum, 1)

        def post_rows_act(act, rows, conds, rows_sum, rows_out, banks):
            for i, c in enumerate(conds):
                for half in range(2):
                    m = 2 * i + half
                    act.wait_ge(rows_sum, m + 1)
                    act.activation(rows[:, c, half * 512:(half + 1) * 512], ps[banks[m % len(banks)]][:, :],
                                   ACT.Copy).then_inc(rows_out, 1)

        def post_norm_act(act, yb, tiles, ssq, junk, y_out, squared, roots):
            for j, tile in enumerate(tiles):
                act.wait_ge(y_out, 2 * j + 2)
                act_step(act, act.activation(junk[:, :], yb[:, tile, :], ACT.Square, accum_out=ssq[:, tile:tile + 1]))
            act.activation(small[:, 126:127], small[:, 125:126], ACT.Copy).then_inc(squared, 1)
            act.wait_ge(roots, 1)
            lo = tiles[0]
            act.activation(ssq[:, lo:NT], ssq[:, lo:NT], ACT.Sqrt).then_inc(roots, 1)

        def post_norm_dve(dve, yb, rows, tiles, ssq, squared, roots, rows_out, n_rows, x_out):
            lo = tiles[0]
            dve.wait_ge(squared, 1)
            dve.tensor_scalar(ssq[:, lo:NT], ssq[:, lo:NT], 1.0 / D, EPS, ALU.mult, ALU.add).then_inc(roots, 1)
            dve.wait_ge(roots, 2)
            dve_step(dve, dve.reciprocal(ssq[:, lo:NT], ssq[:, lo:NT]))
            dve.wait_ge(rows_out, n_rows)
            for tile in tiles:
                yt = yb[:, tile, :]
                dve_step(dve, dve.scalar_tensor_tensor(yt, yt, ssq[:, tile:tile + 1], rows[:, 1 if tile < 2 else 0, :],
                                                       ALU.mult, ALU.mult))
                dve.tensor_tensor(xres[:, tile, :], xres[:, tile, :], yt, ALU.add).then_inc(x_out, 1)

        def out_project(l, tiles):
            a0, b0 = span[f"out{l}"]
            yb = at("y_out", [P, NT, D], F32, work)
            rows = at("post_rows", [P, 2, D], F32, work + 16384)
            junk = at("post_junk", [P, D], F32, work + 24576)
            conds = [1, 0] if len(tiles) == NT else [0]
            n = len(tiles)
            rows_sum, rows_out, turned, hi_out, parts, y_out, squared, roots, x_out = (
                stage_sem(s) for s in ("rows_sum", "rows_out", "turned", "hi_out", "parts", "y_out", "squared", "roots", "x_out"))
            ssq = small[:, 0:4]
            with nc.Block() as block:
                @block.sync
                def _(sp):
                    loads(sp, f"out{l}")

                @block.gpsimd
                def _(pool):
                    splits_lo(pool, f"out{l}")

                @block.scalar
                def _(act):
                    post_rows_act(act, rows, conds, rows_sum, rows_out, [0, 1, 2, 3])
                    for f in range(KD):
                        outT_hi(act, tiles, f, turned, hi_out)
                    for g in range(a0 + 2, b0 + 2):
                        split_hi(act, g)
                    post_norm_act(act, yb, tiles, ssq, junk, y_out, squared, roots)

                @block.vector
                def _(dve):
                    dve_step(dve, dve.memset(small[:, 125:126], 0.0))
                    for f in range(KD):
                        outT_lo(dve, tiles, f, hi_out, parts)
                    dve.wait_ge(unit_used, a0 + 4)
                    for j, tile in enumerate(tiles):
                        for b in range(2):
                            dve.tensor_copy(yb[:, tile, b * 512:(b + 1) * 512], ps[4 * b + j][:, :]).then_inc(y_out, 1)
                    post_norm_dve(dve, yb, rows, tiles, ssq, squared, roots, rows_out, 2 * len(conds), x_out)

                @block.tensor
                def _(pe):
                    post_rows_pe(pe, l, 0, conds, rows_sum, rows_out, [0, 1, 2, 3])
                    pe.wait_ge(rows_out, 2 * len(conds))
                    turn_to_outT(pe, merged, tiles, range(KD), None, turned, parts)
                    pe.wait_ge(parts, KD)
                    for b in range(2):
                        project(pe, a0 + 2 * b, [4 * b + j for j in range(n)], tiles, outT)
            end_stage()

        def ffn_tensors():
            gT = [at(f"ffn_gT_{n}", [P, FT, TOK], F32R, outT_at + i * FT * TOK * 4) for i, n in enumerate(("hi", "lo"))]
            return gT, outT_at + 2 * FT * TOK * 4

        def ffn_up():
            a0, b0 = span["ffn_up"]
            gT, free = ffn_tensors()
            silu = at("ffn_silu", [P, 2, TOK], F32, free)
            prod = at("ffn_prod", [P, 2, TOK], F32, free + 4096)
            rounds = FF // 256
            silu_out, g_done, chain = stage_sem("silu_out"), stage_sem("g_done"), stage_sem("chain")
            w1, w3, w2 = (t[f"ffn_w{i}"][0].rearrange("(k p) n -> p k n", p=P) for i in (1, 3, 2))

            def flat(buf, g):
                return buf[:, g % 2, :]

            with nc.Block() as block:
                @block.sync
                def _(sp):
                    with sp.Fori(0, rounds - 2) as i:
                        for u, w in enumerate((w1, w3)):
                            g = a0 + 4 + u
                            sp.wait_ge(lo_ready, 2 * i + g - 1)
                            sp.dma_start(view(raw, g), w[:, :, bass.ds((i + 2) * 256, 256)]).then_inc(raw_loaded[g % 2], 16)
                    for g in range(b0, b0 + 4):
                        load_unit(sp, g)

                @block.gpsimd
                def _(pool):
                    with pool.Fori(0, rounds) as i:
                        for g in (a0 + 2, a0 + 3):
                            pool.wait_ge(hi_ready, 2 * i + g + 1)
                            pool.tensor_tensor(flat(wlo, g), flat(raw, g), flat(whi, g).bitcast(F32), ALU.subtract).then_inc(lo_ready, 1)

                @block.scalar
                def _(act):
                    act.sem_inc(silu_out, 2)
                    with act.Fori(0, rounds) as i:
                        for u in range(2):
                            g = a0 + 2 + u
                            act.wait_ge(raw_loaded[g % 2], 16 * (g // 2 + 1) + 16 * i)
                            act.wait_ge(unit_used, 2 * i + g - 1)
                            act.activation(flat(whi, g), flat(raw, g), ACT.Copy).then_inc(hi_ready, 1)
                            if u == 0:
                                for j in range(2):
                                    act.wait_ge(g_done, 2 * i + j + 1)
                                    act.activation(silu[:, j, :], ps[j][:, :], ACT.Silu).then_inc(silu_out, 1)

                @block.vector
                def _(dve):
                    dve.sem_inc(g_done, 2)
                    with dve.Fori(0, rounds) as i:
                        dve.wait_ge(unit_used, 2 * i + a0 + 2)
                        for j in range(2):
                            dve.wait_ge(silu_out, 2 * i + j + 3)
                            dve.tensor_tensor(prod[:, j, :], silu[:, j, :], ps[2 + j][:, :], ALU.mult).then_inc(chain, 1)
                            dve.wait_ge(chain, 4 * i + 2 * j + 1)
                            hi, lo = (g[:, bass.ds(2 * i + j, 1), :].rearrange("p a t -> p (a t)") for g in gT)
                            dve.tensor_copy(hi, prod[:, j, :]).then_inc(chain, 1)
                            dve.wait_ge(chain, 4 * i + 2 * j + 2)
                            dve.tensor_tensor(lo, prod[:, j, :], hi.bitcast(F32), ALU.subtract).then_inc(g_done, 1)

                @block.tensor
                def _(pe):
                    with pe.Fori(0, rounds) as i:
                        for u in range(2):
                            g = a0 + u
                            pe.wait_ge(lo_ready, 2 * i + g + 1)
                            pe.wait_ge(silu_out if u == 0 else g_done, 2 * i + 2)
                            wh, wl = view(whi, g), view(wlo, g)
                            for j in range(2):
                                for k in range(KD):
                                    a = [wh[:, k, j * P:(j + 1) * P], wl[:, k, j * P:(j + 1) * P]]
                                    last = three(pe, ps[2 * u + j][:, :], a, [h[:, k, :] for h in hT], k == 0, k == KD - 1)
                            last.then_inc(unit_used, 1)
            end_stage()

        def ffn_down(l):
            a0, b0 = span["ffn_down"]
            gT, free = ffn_tensors()
            yb = at("ffn_y", [P, NT, D], F32, hT_at)
            rows = at("ffn_rows", [P, 2, D], F32, hT_at + 16384)
            junk = at("ffn_junk", [P, D], F32, hT_at + 24576)
            rows_sum, rows_out, y_out, squared, roots, x_out = (
                stage_sem(s) for s in ("rows_sum", "rows_out", "y_out", "squared", "roots", "x_out"))
            ssq = small[:, 0:4]
            with nc.Block() as block:
                @block.sync
                def _(sp):
                    loads(sp, "ffn_down")

                @block.gpsimd
                def _(pool):
                    splits_lo(pool, "ffn_down")

                @block.scalar
                def _(act):
                    post_rows_act(act, rows, [1, 0], rows_sum, rows_out, [0, 1, 2, 3])
                    for g in range(a0 + 2, b0 + 2):
                        split_hi(act, g)
                    post_norm_act(act, yb, ALL_TILES, ssq, junk, y_out, squared, roots)

                @block.vector
                def _(dve):
                    dve.wait_ge(unit_used, b0)
                    for tile in ALL_TILES:
                        for b in range(2):
                            dve.tensor_copy(yb[:, tile, b * 512:(b + 1) * 512], ps[2 * tile + b][:, :]).then_inc(y_out, 1)
                    post_norm_dve(dve, yb, rows, ALL_TILES, ssq, squared, roots, rows_out, 4, x_out)

                @block.tensor
                def _(pe):
                    post_rows_pe(pe, l, 1, [1, 0], rows_sum, rows_out, [0, 1, 2, 3])
                    pe.wait_ge(rows_out, 4)
                    for g in range(a0, b0):
                        pe.wait_ge(lo_ready, g + 1)
                        wh, wl = view(whi, g), view(wlo, g)
                        for k in range(2):
                            kk = 2 * (g - a0) + k
                            for tile in ALL_TILES:
                                a = [x[:, kk, tile * P:(tile + 1) * P] for x in gT]
                                for b in range(2):
                                    s = slice(b * 512, (b + 1) * 512)
                                    last = three(pe, ps[2 * tile + b][:, :], a, [wh[:, k, s], wl[:, k, s]],
                                                 kk == 0, kk == FT - 1)
                        last.then_inc(unit_used, 1)
            end_stage()

        R0 = ring_at
        RAW_RING, RING, AHEAD = 6, 3, 2
        moe_raw = at("moe_raw", [P, RAW_RING, 2048], F32, R0)
        moe_hi = at("moe_unit_hi", [P, RING, 2048], F32R, R0 + RAW_RING * 8192)
        moe_lo = at("moe_unit_lo", [P, RING, 2048], F32R, R0 + (RAW_RING + RING) * 8192)
        M0 = R0 + (RAW_RING + 2 * RING) * 8192
        htok = [at(f"moe_h_{n}", [P, 2, D], F32R, M0 + 8192 * i) for i, n in enumerate(("hi", "lo"))]
        route = at("moe_route", [P, 3, 2, 2 * NE + 1], F32, M0 + 16384)
        n_pass = at("moe_passes", [P, 1], mybir.dt.int32, M0 + 16384 + 448)
        slot_of, chosen, weight = route[:, 0, :, :], route[:, 1, :, :], route[:, 2, :, :]

        w1, w3 = (t[f"moe_w{i}"][0].rearrange("e (k p) n -> p e k n", p=P) for i in (1, 3))
        w2 = t["moe_w2"][0].rearrange("e (k p) n -> p e k n", p=P)
        NB = 6
        plan = []
        for _b in range(NB - 1):
            plan += [(w, 4 * half, 4, _b * 512, 512) for w in (w1, w3) for half in range(2)]
        plan += [(w, 0, KD, (NB - 1) * 512, 256) for w in (w1, w3)]
        up = len(plan)
        plan += [(w2, 2 * j, 2, 0, D) for j in range(FT // 2)]
        U = len(plan)
        assert U % RING == 0 and 2 * U % RAW_RING == 0
        raw_m = [sem(f"moe_raw_loaded{i}") for i in range(RAW_RING)]

        def unit_part(buf, slot, v):
            _, _, a, _, b = plan[v % U]
            return buf[:, slot, 0:a * b].rearrange("p (a b) -> p a b", b=b)

        def load_moe(sp, expert, x, v):
            w, k, a, c, b = plan[v % U]
            slot = (U * x + v) % RAW_RING
            src = w[:, bass.ds(expert, 1), k:k + a, c:c + b].rearrange("p e k n -> p (e k) n")
            sp.dma_start(unit_part(moe_raw, slot, v), src).then_inc(raw_m[slot], 16)

        def moe_route(l):
            rows = at("moe_rows", [P, 2, D], F32, work)
            xn = at("moe_xn", [P, 2, D], F32, work + 8192)
            wr = at("router", [P, KD, NE], F32, work + 16384)
            wr2 = [at(f"router_{n}", [P, KD, NE], F32R, work + 16640 + 256 * i) for i, n in enumerate(("hi", "lo"))]
            lg = at("logits", [P, 2, NE], F32, work + 17152)
            cmp = at("compare", [P, 2, 2, NE * NE], F32, work + 17280)
            sc = at("route_scratch", [P, 64], F32, work + 18304)
            names = ("router_in", "squares", "roots", "rows_sum", "rows_out", "h_done", "turned", "hi_out", "parts",
                     "logits_sum", "logits_out", "exps", "sel_done", "counted")
            (router_in, squares, roots, rows_sum, rows_out, h_done, turned, hi_out, parts,
             logits_sum, logits_out, exps, sel_done, counted) = (stage_sem(s) for s in names)
            ssq = small[:, 0:2]
            negm, ssum, most = sc[:, 0:2], sc[:, 2:4], sc[:, 4:5]
            ex = sc[:, 16:32].rearrange("p (j e) -> p j e", j=2)
            sel = sc[:, 32:48].rearrange("p (j e) -> p j e", j=2)
            gain, shift = gains[l][:, 1, :, 0:1], mods[l][:, 24:32, 0:1]
            with nc.Block() as block:
                @block.sync
                def _(sp):
                    sp.dma_start(wr[:, :, :], t["moe_router"][0].rearrange("(k p) n -> p k n", p=P)).then_inc(router_in, 16)
                    for v in range(RAW_RING):
                        load_moe(sp, 0, 0, v)
                    sp.wait_ge(router_in, 16)

                @block.scalar
                def _(act):
                    for j in range(2):
                        act.activation(xn[:, j, :], xres[:, 2 + j, :], ACT.Square, accum_out=ssq[:, j:j + 1]).then_inc(squares, 1)
                    act.wait_ge(roots, 1)
                    act.activation(ssq, ssq, ACT.Sqrt).then_inc(roots, 1)
                    for m in range(4):
                        act.wait_ge(rows_sum, m + 1)
                        act.activation(rows[:, m // 2, (m % 2) * 512:(m % 2 + 1) * 512], ps[m][:, :], ACT.Copy).then_inc(rows_out, 1)
                    for f in range(KD):
                        act.wait_ge(turned, f + 1)
                        act.activation(hT[0][:, f, 2 * P:TOK], ps[f][:, 0:2 * P], ACT.Copy).then_inc(hi_out, 1)
                    act.wait_ge(logits_out, 2)
                    for j in range(2):
                        ins = act.activation(ex[:, j, :], lg[:, j, :], ACT.Exp, bias=negm[:, j:j + 1])
                    ins.then_inc(exps, 1)

                @block.vector
                def _(dve):
                    dve.wait_ge(router_in, 16)
                    dve_step(dve, dve.tensor_copy(wr2[0][:, :, :], wr[:, :, :]))
                    dve_step(dve, dve.tensor_tensor(wr2[1][:, :, :], wr[:, :, :], wr2[0][:, :, :].bitcast(F32), ALU.subtract))
                    dve.wait_ge(squares, 2)
                    dve.tensor_scalar(ssq, ssq, 1.0 / D, EPS, ALU.mult, ALU.add).then_inc(roots, 1)
                    dve.wait_ge(roots, 2)
                    dve_step(dve, dve.reciprocal(ssq, ssq))
                    dve.wait_ge(rows_out, 4)
                    for j in range(2):
                        h = xn[:, j, :]
                        dve_step(dve, dve.scalar_tensor_tensor(h, xres[:, 2 + j, :], ssq[:, j:j + 1], rows[:, 0, :], ALU.mult, ALU.mult))
                        dve.tensor_tensor(h, h, rows[:, 1, :], ALU.add).then_inc(h_done, 1)
                        dve.wait_ge(h_done, j + 1)
                        dve_step(dve, dve.tensor_copy(htok[0][:, j, :], h))
                        dve_step(dve, dve.tensor_tensor(htok[1][:, j, :], h, htok[0][:, j, :].bitcast(F32), ALU.subtract))
                    for f in range(KD):
                        dve.wait_ge(hi_out, f + 1)
                        dve.tensor_tensor(hT[1][:, f, 2 * P:TOK], ps[f][:, 0:2 * P], hT[0][:, f, 2 * P:TOK].bitcast(F32),
                                          ALU.subtract).then_inc(parts, 1)
                    dve.wait_ge(logits_sum, 1)
                    dve_step(dve, dve.tensor_copy(lg[:, :, :], ps[0][:, 0:2 * NE].rearrange("p (j e) -> p j e", j=2)))
                    dve.tensor_reduce(negm, lg[:, :, :], AX.X, ALU.max).then_inc(logits_out, 1)
                    dve.wait_ge(logits_out, 1)
                    dve.tensor_scalar(negm, negm, -1.0, None, ALU.mult).then_inc(logits_out, 1)
                    for j in range(2):
                        shape = [P, NE, NE]
                        inner, outer = lg[:, j, :].unsqueeze(1).to_broadcast(shape), lg[:, j, :].unsqueeze(2).to_broadcast(shape)
                        gt, eq = (cmp[:, j, i, :].rearrange("p (a b) -> p a b", a=NE) for i in range(2))
                        dve.tensor_tensor(gt, inner, outer, ALU.is_gt)
                        dve_step(dve, dve.tensor_tensor(eq, inner, outer, ALU.is_equal))
                        dve_step(dve, dve.tensor_tensor(cmp[:, j, 1, :], cmp[:, j, 1, :], const("before"), ALU.mult))
                        dve_step(dve, dve.tensor_tensor(cmp[:, j, 0, :], cmp[:, j, 0, :], cmp[:, j, 1, :], ALU.add))
                        dve_step(dve, dve.tensor_reduce(sel[:, j, :], gt, AX.X, ALU.add))
                    dve.tensor_scalar(sc[:, 32:48], sc[:, 32:48], 2.0, None, ALU.is_lt).then_inc(sel_done, 1)
                    dve.wait_ge(exps, 1)
                    dve.wait_ge(sel_done, 1)
                    dve_step(dve, dve.tensor_tensor(ex, ex, sel, ALU.mult))
                    dve_step(dve, dve.tensor_reduce(ssum, ex, AX.X, ALU.add))
                    dve_step(dve, dve.reciprocal(ssum, ssum))
                    dve_step(dve, dve.tensor_tensor(ex, ex, spread(ssum, 2, NE), ALU.mult))
                    dve.wait_ge(counted, 1)
                    pos = ps[1][:, 0:2 * NE].rearrange("p (j e) -> p j e", j=2)
                    for r in range(2):
                        s = slice(r * NE, (r + 1) * NE)
                        dve.tensor_copy(chosen[:, :, s], sel)
                        dve.tensor_copy(weight[:, :, s], ex)
                        dve.scalar_tensor_tensor(slot_of[:, :, s], pos, -float(r * P), sel, ALU.add, ALU.subtract)
                    for a in (slot_of, chosen, weight):
                        dve.memset(a[:, :, 2 * NE:2 * NE + 1], -1.0)
                    dve_step(dve, dve.tensor_reduce(most, ps[1][:, 2 * NE:3 * NE], AX.X, ALU.max))
                    dve_step(dve, dve.tensor_scalar(n_pass[:, :], most, float(P), 1.0, ALU.is_gt, ALU.add))

                @block.tensor
                def _(pe):
                    for i, cols_of_row in enumerate((gain, shift)):
                        for half in range(2):
                            for d in range(4):
                                last = pe.matmul(ps[2 * i + half][:, d * P:(d + 1) * P],
                                                 cols_of_row[:, 4 * half + d, :].to_broadcast([P, P]), ident, start=True, stop=True)
                            last.then_inc(rows_sum, 1)
                    pe.wait_ge(h_done, 2)
                    for f in range(KD):
                        for j in range(2):
                            last = pe.transpose(ps[f][:, j * P:(j + 1) * P], xn[:, j, f * P:(f + 1) * P], ident)
                        last.then_inc(turned, 1)
                    pe.wait_ge(parts, KD)
                    for j in range(2):
                        for k in range(KD):
                            a = [h[:, k, (2 + j) * P:(3 + j) * P] for h in hT]
                            last = three(pe, ps[0][:, j * NE:(j + 1) * NE], a, [w[:, k, :] for w in wr2], k == 0, k == KD - 1)
                    last.then_inc(logits_sum, 1)
                    pe.wait_ge(sel_done, 1)
                    pe.matmul(ps[1][:, 0:NE], const("tri_f"), sel[:, 0, :], start=True, stop=True)
                    pe.matmul(ps[1][:, NE:2 * NE], const("tri_f"), sel[:, 1, :], start=True, stop=False)
                    pe.matmul(ps[1][:, NE:2 * NE], const("ones"), sel[:, 0, :], start=False, stop=True)
                    for j in range(2):
                        last = pe.matmul(ps[1][:, 2 * NE:3 * NE], const("ones"), sel[:, j, :], start=j == 0, stop=j == 1)
                    last.then_inc(counted, 1)
            end_stage()

        yacc = at("moe_y", [P, NT, D], F32, M0 + 17408 - 2 * D * 4)

        def moe_experts():
            m = M0 + 17408 + 2 * D * 4
            xeT = [at(f"xe_T_{n}", [P, KD, P], F32R, m + 4096 * i) for i, n in enumerate(("hi", "lo"))]
            m += 8192
            gT = [at(f"moe_gT_{n}", [P, FT, P], F32R, m + FT * P * 4 * i) for i, n in enumerate(("hi", "lo"))]
            m += 2 * FT * P * 4
            pick = at("pick", [P, 2, P], F32, m)
            pick_r = at("pick_r", [P, 2, P], F32R, m + 1024)
            put = at("put", [P, 2 * P], F32R, m + 2048)
            w_slot = at("w_slot", [P, 1], F32, m + 3072)
            m += 3136
            silu = at("moe_silu", [P, 2, 512], F32, m)
            prod = at("moe_prod", [P, 2, 512], F32, m + 4096)
            ytmp = at("moe_ytmp", [P, D], F32, m + 8192)
            ye = [at(f"moe_ye_{n}", [P, D], F32R, m + 12288 + 4096 * i) for i, n in enumerate(("hi", "lo"))]

            CUT = 1408
            h1_end = [4 * b + 1 for b in range(NB - 1)] + [up - 2]
            h3_end = [4 * b + 3 for b in range(NB - 1)] + [up - 1]
            turn_after = [h1_end[b + 1] for b in range(NB - 1)] + [up + 1]
            gather_after = up + 4
            names = ("hi_m", "lo_dve", "lo_pool", "used", "pick_ready", "gathered", "xe_act", "xe_dve", "put_sum",
                     "put_out", "ws_out", "silu_out", "g_done", "turned", "hi_out", "lo_done", "ye_out", "ye_ready",
                     "combined", "added", "dve_loop", "slot_free")
            (hi_m, lo_dve, lo_pool, used, pick_ready, gathered, xe_act, xe_dve, put_sum,
             put_out, ws_out, silu_out, g_done, turned, hi_out, lo_done, ye_out, ye_ready,
             combined, added, dve_loop, slot_free) = (stage_sem(s) for s in names)

            def part(buf, v):
                return unit_part(buf, v % RING, v)

            def raw_slot(x, v):
                return (U * x + v) % RAW_RING

            def hi(act, i, x, v):
                act.wait_ge(raw_m[raw_slot(x, v)], 16 * (2 * U // RAW_RING) * i + 16 * ((U * x + v) // RAW_RING + 1))
                act.activation(moe_hi[:, v % RING, :], moe_raw[:, raw_slot(x, v), :], ACT.Copy).then_inc(hi_m, 1)

            def lo(eng, i, x, v, a, b, done):
                eng.wait_ge(hi_m, 2 * U * i + U * x + v + 1)
                s = v % RING
                eng.tensor_tensor(moe_lo[:, s, a:b], moe_raw[:, raw_slot(x, v), a:b], moe_hi[:, s, a:b].bitcast(F32), ALU.subtract).then_inc(done, 1)

            class LoopSteps:

                def __init__(self, sem, per, n):
                    self.sem, self.per, self.n, self.k = sem, per, n, 0

                def __call__(self, eng, ins):
                    self.k += 1
                    ins.then_inc(self.sem, 1)
                    eng.wait_ge(self.sem, self.per * self.n + self.k)

                def end(self):
                    assert self.k == self.per, self.k

            def build_pick(dve, step, nn):
                for j in range(2):
                    dve.tensor_scalar(pick[:, j, :], const("iota"), slot_of[:, j, bass.ds(nn, 1)], chosen[:, j, bass.ds(nn, 1)],
                                      ALU.is_equal, ALU.mult).then_inc(pick_ready, 1)
                dve.wait_ge(pick_ready, 3 * nn + 2)
                dve.tensor_copy(pick_r[:, :, :], pick[:, :, :]).then_inc(pick_ready, 1)

            def gather(pe, nn):
                pe.wait_ge(pick_ready, 3 * nn + 3)
                for i in range(4):
                    src, half = htok[i // 2], i % 2
                    if i >= 2:
                        pe.wait_ge(xe_act if half == 0 else xe_dve, 2 * nn + 1)
                    for d in range(4):
                        dd = 4 * half + d
                        for j in range(2):
                            last = pe.matmul(ps[4 + half][:, d * P:(d + 1) * P], src[:, j, dd * P:(dd + 1) * P], pick_r[:, j, :],
                                             start=j == 0, stop=j == 1)
                    last.then_inc(gathered, 1)

            def xe_out(copy, nn, half, done, eng):
                for i in range(2):
                    eng.wait_ge(gathered, 4 * nn + 2 * i + half + 1)
                    copy(xeT[i][:, 4 * half:4 * half + 4, :], ps[4 + half][:, :].rearrange("p (d s) -> p d s", d=4)).then_inc(done, 1)

            def combine(pe, n, c):
                if c >= 2:
                    pe.wait_ge(added, 4 * n + c - 1)
                j, half = divmod(c, 2)
                for p, a in enumerate(ye):
                    last = pe.matmul(ps[4 + half][:, :], put[:, j * P:(j + 1) * P], a[:, half * 512:(half + 1) * 512],
                                     start=p == 0, stop=p == 1)
                last.then_inc(combined, 1)

            def add_combined(dve, n, c):
                dve.wait_ge(combined, 4 * n + c + 1)
                a = yacc[:, 2 + c // 2, (c % 2) * 512:(c % 2 + 1) * 512]
                dve.tensor_tensor(a, a, ps[4 + c % 2][:, :], ALU.add).then_inc(added, 1)

            with nc.Block() as block:
                @block.sync
                def _(sp):
                    passes = sp.value_load(n_pass[0:1, 0:1], min_val=1, max_val=2)
                    with sp.Fori(0, passes * (NE // 2)) as i:
                        experts = [sp.snap((2 * i + x) % NE) for x in range(3)]
                        for x in range(2):
                            for v in range(RAW_RING, U + RAW_RING):
                                split = sp.snap(2 * U * i + (U * x + v - RAW_RING + 1))
                                sp.wait_ge(lo_dve, split)
                                sp.wait_ge(lo_pool, split)
                                sp.sem_inc(slot_free, 1)
                                load_moe(sp, experts[x + v // U], x, v)
                    for s in range(RAW_RING):
                        sp.wait_ge(raw_m[s], passes * (NE // 2 * (2 * U // RAW_RING) * 16) + 16)
                        sp.sem_inc(slot_free, 1)

                @block.gpsimd
                def _(pool):
                    passes = pool.value_load(n_pass[0:1, 0:1], min_val=1, max_val=2)
                    for v in range(AHEAD):
                        lo(pool, 0, 0, v, CUT, 2048, lo_pool)
                    with pool.Fori(0, passes * (NE // 2)) as i:
                        for x in range(2):
                            for v in range(AHEAD, U + AHEAD):
                                lo(pool, i, x, v, CUT, 2048, lo_pool)

                @block.scalar
                def _(act):
                    passes = act.value_load(n_pass[0:1, 0:1], min_val=1, max_val=2)

                    def copy(out, in_):
                        return act.activation(out, in_, ACT.Copy)

                    act.sem_inc(silu_out, 2)
                    act.sem_inc(ye_out, 1)
                    for v in range(AHEAD):
                        hi(act, 0, 0, v)
                    xe_out(copy, 0, 0, xe_act, act)
                    with act.Fori(0, passes * (NE // 2)) as i:
                        for x in range(2):
                            n = 2 * i + x
                            for u in range(U):
                                act.wait_ge(used, U * n + u + 1)
                                hi(act, i, x, u + AHEAD)
                                if u == 3:
                                    act.wait_ge(put_sum, n + 1)
                                    act.activation(put[:, :], ps[4][:, 0:2 * P], ACT.Copy).then_inc(put_out, 1)
                                for b in range(NB):
                                    if u == h1_end[b] + 1:
                                        w = plan[h1_end[b]][4]
                                        act.wait_ge(g_done, NB * n + b + 1)
                                        act.activation(silu[:, b % 2, 0:w], ps[b % 2][:, 0:w], ACT.Silu).then_inc(silu_out, 1)
                                    if u == turn_after[b] + 1:
                                        k = 4 if b < NB - 1 else 2
                                        act.wait_ge(turned, NB * n + b + 1)
                                        act.activation(gT[0][:, 4 * b:4 * b + k, :],
                                                       ps[4 + b % 2][:, 0:k * P].rearrange("p (k s) -> p k s", k=k),
                                                       ACT.Copy).then_inc(hi_out, 1)
                                if u == gather_after + 1:
                                    xe_out(copy, n + 1, 0, xe_act, act)
                            act.wait_ge(used, U * n + U + 1)
                            act.wait_ge(ws_out, n + 1)
                            act.activation(ytmp[:, 0:512], ps[6][:, :], ACT.Copy, scale=w_slot[:, 0:1])
                            act.activation(ytmp[:, 512:D], ps[7][:, :], ACT.Copy, scale=w_slot[:, 0:1]).then_inc(ye_out, 1)

                @block.vector
                def _(dve):
                    passes = dve.value_load(n_pass[0:1, 0:1], min_val=1, max_val=2)
                    dve.sem_inc(g_done, 2)
                    dve.sem_inc(lo_done, 2)
                    build_pick(dve, None, 0)
                    dve_step(dve, dve.memset(yacc[:, 2:4, :], 0.0))
                    dve_step(dve, dve.tensor_copy(put[:, :], yacc[:, 2, 0:2 * P]))
                    for a in ye:
                        dve_step(dve, dve.tensor_copy(a[:, :], yacc[:, 2, :]))
                    dve.sem_inc(ye_ready, 1)
                    for v in range(AHEAD):
                        lo(dve, 0, 0, v, 0, CUT, lo_dve)
                    xe_out(dve.tensor_copy, 0, 1, xe_dve, dve)
                    with dve.Fori(0, passes * (NE // 2)) as i:
                        for x in range(2):
                            n = 2 * i + x
                            step = LoopSteps(dve_loop, 1, n)
                            for u in range(U):
                                lo(dve, i, x, u + AHEAD, 0, CUT, lo_dve)
                                if u in (1, 2):
                                    for c in (2 * u - 2, 2 * u - 1):
                                        add_combined(dve, n, c)
                                if u == 3:
                                    dve.wait_ge(put_sum, n + 1)
                                    dve.tensor_copy(w_slot[:, :], ps[5][:, 0:1]).then_inc(ws_out, 1)
                                for b in range(NB):
                                    if u == h3_end[b] + 1:
                                        w = plan[h3_end[b]][4]
                                        dve.wait_ge(silu_out, NB * n + b + 3)
                                        dve.wait_ge(used, U * n + h3_end[b] + 2)
                                        dve.tensor_tensor(prod[:, b % 2, 0:w], silu[:, b % 2, 0:w], ps[2 + b % 2][:, 0:w],
                                                          ALU.mult).then_inc(g_done, 1)
                                    if u == turn_after[b] + 2:
                                        k = 4 if b < NB - 1 else 2
                                        dve.wait_ge(hi_out, NB * n + b + 1)
                                        dve.tensor_tensor(gT[1][:, 4 * b:4 * b + k, :],
                                                          ps[4 + b % 2][:, 0:k * P].rearrange("p (k s) -> p k s", k=k),
                                                          gT[0][:, 4 * b:4 * b + k, :].bitcast(F32), ALU.subtract).then_inc(lo_done, 1)
                                if u == up + 1:
                                    build_pick(dve, None, n + 1)
                                if u == gather_after + 1:
                                    xe_out(dve.tensor_copy, n + 1, 1, xe_dve, dve)
                            dve.wait_ge(ye_out, n + 2)
                            step(dve, dve.tensor_copy(ye[0][:, :], ytmp[:, :]))
                            dve.tensor_tensor(ye[1][:, :], ytmp[:, :], ye[0][:, :].bitcast(F32), ALU.subtract).then_inc(ye_ready, 1)
                            step.end()
                    for c in range(4):
                        add_combined(dve, passes * NE, c)

                @block.tensor
                def _(pe):
                    passes = pe.value_load(n_pass[0:1, 0:1], min_val=1, max_val=2)
                    pe.sem_inc(used, 1)
                    gather(pe, 0)
                    with pe.Fori(0, passes * (NE // 2)) as i:
                        for x in range(2):
                            n = 2 * i + x
                            pe.wait_ge(xe_act, 2 * n + 2)
                            pe.wait_ge(xe_dve, 2 * n + 2)
                            for u in range(U):
                                pe.wait_ge(lo_dve, U * n + u + 1)
                                pe.wait_ge(lo_pool, U * n + u + 1)
                                _, k0, a, _, w = plan[u]
                                wh, wl = part(moe_hi, u), part(moe_lo, u)
                                if u < up:
                                    b = min(u // 4, NB - 1)
                                    is_h3 = plan[u][0] is w3
                                    if u in (4 * b, 4 * b + 2) or b == NB - 1:
                                        pe.wait_ge(g_done if is_h3 else silu_out, NB * n + b + 1)
                                    bank = ps[2 * is_h3 + b % 2]
                                    for k in range(a):
                                        kk = k0 + k
                                        last = three(pe, bank[:, 0:w], [a_[:, kk, :] for a_ in xeT], [wh[:, k, :], wl[:, k, :]],
                                                     kk == 0, kk == KD - 1)
                                else:
                                    if u == up:
                                        pe.wait_ge(ye_out, n + 1)
                                    for k in range(a):
                                        kk = k0 + k
                                        if kk % 4 == 0:
                                            pe.wait_ge(lo_done, NB * n + kk // 4 + 3)
                                        for half in range(2):
                                            c = slice(half * 512, (half + 1) * 512)
                                            last = three(pe, ps[6 + half][:, :], [a_[:, kk, :] for a_ in gT], [wh[:, k, c], wl[:, k, c]],
                                                         kk == 0, kk == FT - 1)
                                last.then_inc(used, 1)
                                if u < 2:
                                    if u == 0:
                                        pe.wait_ge(ye_ready, n + 1)
                                    for c in (2 * u, 2 * u + 1):
                                        combine(pe, n, c)
                                if u == 2:
                                    pe.wait_ge(added, 4 * n + 4)
                                    for j in range(2):
                                        pe.transpose(ps[4][:, j * P:(j + 1) * P], pick[:, j, :], ident)
                                    for j in range(2):
                                        last = pe.matmul(ps[5][:, 0:1], pick[:, j, :], weight[:, j, bass.ds(n, 1)], start=j == 0, stop=j == 1)
                                    last.then_inc(put_sum, 1)
                                for b in range(NB):
                                    if u == turn_after[b]:
                                        if b < 2:
                                            pe.wait_ge(put_out if b == 0 else ws_out, n + 1)
                                        pe.wait_ge(g_done, NB * n + b + 3)
                                        pe.wait_ge(lo_done, NB * n + b + 1)
                                        for k in range(4 if b < NB - 1 else 2):
                                            last = pe.transpose(ps[4 + b % 2][:, k * P:(k + 1) * P], prod[:, b % 2, k * P:(k + 1) * P], ident)
                                        last.then_inc(turned, 1)
                                if u == gather_after:
                                    pe.wait_ge(lo_done, NB * n + NB + 2)
                                    gather(pe, n + 1)
                    pe.wait_ge(xe_act, passes * (2 * NE) + 2)
                    pe.wait_ge(xe_dve, passes * (2 * NE) + 2)
                    pe.wait_ge(ye_ready, passes * NE + 1)
                    for c in range(4):
                        combine(pe, passes * NE, c)
            end_stage()

        def finish(l):
            rows = at("last_rows", [P, 2, D], F32, R0)
            junk = at("last_junk", [P, D], F32, R0 + 8192)
            rows_sum, rows_out, y_out, squared, roots, x_out, stored = (
                stage_sem(s) for s in ("rows_sum", "rows_out", "y_out", "squared", "roots", "x_out", "stored"))
            ssq = small[:, 0:4]
            with nc.Block() as block:
                @block.sync
                def _(sp):
                    for j in range(2):
                        sp.wait_ge(x_out, j + 1)
                        sp.dma_start(t["out"][0, j * P:(j + 1) * P, :], xres[:, 2 + j, :]).then_inc(stored, 16)
                    sp.wait_ge(stored, 32)

                @block.scalar
                def _(act):
                    post_rows_act(act, rows, [0], rows_sum, rows_out, [0, 1, 2, 3])
                    post_norm_act(act, yacc, X_TILES, ssq, junk, y_out, squared, roots)

                @block.vector
                def _(dve):
                    dve.sem_inc(y_out, 4)
                    post_norm_dve(dve, yacc, rows, X_TILES, ssq, squared, roots, rows_out, 2, x_out)

                @block.tensor
                def _(pe):
                    post_rows_pe(pe, l, 1, [0], rows_sum, rows_out, [0, 1, 2, 3])
            end_stage()

        setup()
        for l in range(DEPTH):
            tiles = ALL_TILES if l == 0 else X_TILES
            norm(l, ALL_TILES, 0)
            if l == 0:
                other_params()
            ssm_project(l)
            ssm_mix(l, tiles, [(0, c) for c in range(2, 6)] + [(1, 0), (1, 1)] if l == 0 else [(1, c) for c in range(2, 6)])
            ssm_gate(l, tiles)
            merge(l, 1, tiles, True)
            ret_project(l, tiles)
            ret_mix(l, tiles)
            ret_gate(l, tiles)
            merge(l, 0, tiles, False)
            att_project(l, tiles)
            att_mix(l, tiles)
            merge(l, 2, tiles, False)
            out_project(l, tiles)
            if l == 0:
                norm(l, ALL_TILES, 1)
                ffn_up()
                ffn_down(l)
            else:
                moe_route(l)
                moe_experts()
                finish(l)


INPUTS = ["x", "c", "ctx", "c_ctx", "ada_w", "ada_b", "mix_norm_pre", "mix_norm_post", "ffn_norm_pre",
          "ffn_norm_post", "w_in", "ret_decay", "ssm_conv_w", "ssm_conv_b", "ssm_dt_bias", "ssm_a_log", "ssm_d",
          "ssm_norm_w", "att_sink", "w_branch", "w_out", "ffn_w1", "ffn_w3", "ffn_w2", "moe_router", "moe_w1",
          "moe_w3", "moe_w2"]


def kernel(**inputs):
    import concourse.bacc as bacc
    from concourse.bass_utils import run_bass_kernel_spmd

    nc = bacc.Bacc("TRN2", target_bir_lowering=False, num_devices=1)
    arrays = {name: np.ascontiguousarray(inputs[name]) for name in INPUTS}
    arrays["consts"] = constants()
    t = {name: nc.dram_tensor(f"in_{name}", a.shape, F32, kind="ExternalInput").ap() for name, a in arrays.items()}
    t["out"] = nc.dram_tensor("out", (1, SEQ, D), F32, kind="ExternalOutput").ap()
    program(nc, t)
    r = run_bass_kernel_spmd(nc, [{f"in_{name}": a for name, a in arrays.items()}], core_ids=[0])
    return r.results[0]["out"]
```

```python
from contextlib import ExitStack

import numpy as np

import concourse.bass as bass
from concourse import mybir

F32 = mybir.dt.float32
F32R = mybir.dt.float32r
ACT = mybir.ActivationFunctionType
ALU = mybir.AluOpType
AX = mybir.AxisListType

P = 128
D = 1024
KD = D // P
SEQ, CTX = 256, 256
NT = (SEQ + CTX) // P
TOK = NT * P
X_TILES, ALL_TILES = [2, 3], [0, 1, 2, 3]
DEPTH = 2
EPS = 1e-6
GRID_W = 64
BLK = 512
RH, DK, DV = 4, 128, 256
SH, HD, SG, ST = 16, 64, 2, 128
HG = SH // SG
XBC = SH * HD + 2 * SG * ST
AH, KVH, AD = 8, 2, 128
AG = AH // KVH
FF = 2816
FT = FF // P
NE = 8
NEG = -1e30

SPLITS = dict(rq=RH * DK, rk=RH * DK, rv=RH * DV, rg=RH * DV, sz=SH * HD, xbc=XBC, dt=SH,
              aq=AH * AD, akv=2 * KVH * AD, gate=3 * D)
COL = {}
_at = 0
for _name, _width in SPLITS.items():
    COL[_name] = _at
    _at += _width
IN_W = _at

CONSTS = dict(ident=P, tri_f=P, tri_b=P, neg_up=P, neg_low=P, ones=P, dist_f=P, dist_b=P, iota=P,
              ret_w=4, sel=2, before=NE * NE,
              rq_cos=128, rq_sin=128, rk_cos=128, rk_sin=128, aq_cos=128, aq_sin=128, ak_cos=128, ak_sin=128)
CAT = {}
_at = 0
for _name, _width in CONSTS.items():
    CAT[_name] = _at
    _at += _width
N_CONST = _at

ROWS = dict(ada_b=48, mix_pre=8, ffn_pre=8, conv_w=36, conv_b=12)
ROW = {}
_at = 0
for _name, _width in ROWS.items():
    ROW[_name] = _at
    _at += _width
N_ROWS = _at


def constants():
    a = np.zeros((P, N_CONST), np.float32)
    i = np.arange(P, dtype=np.float32)
    row, col = i[:, None], i[None, :]

    def put(name, v):
        a[:, CAT[name]:CAT[name] + v.shape[1]] = v

    put("ident", np.eye(P, dtype=np.float32))
    put("tri_f", (row <= col).astype(np.float32))
    put("tri_b", (row >= col).astype(np.float32))
    put("neg_up", np.where(col > row, NEG, 0.0).astype(np.float32))
    put("neg_low", np.where(col < row, NEG, 0.0).astype(np.float32))
    put("ones", np.ones((P, P), np.float32))
    put("dist_f", np.maximum(col - row, 0.0))
    put("dist_b", np.maximum(row - col, 0.0))
    put("iota", np.broadcast_to(col, (P, P)))
    put("ret_w", np.stack([P - 1 - i, i, i + 1, P - i], 1))
    put("sel", (np.arange(P)[:, None] % 2 == np.arange(2)[None, :]).astype(np.float32))
    e = np.arange(NE)
    put("before", np.broadcast_to((e[None, :] < e[:, None]).astype(np.float32).reshape(1, NE * NE), (P, NE * NE)))
    pos = np.arange(SEQ, dtype=np.float32)

    def angles(p, dim):
        inv = np.float32(10000.0) ** (-np.arange(0, dim, 2, dtype=np.float32) / np.float32(dim))
        return p[:, None] * inv[None, :].astype(np.float32)

    grid_row, grid_col = np.floor(pos / GRID_W), pos % GRID_W
    ret = angles(pos, DK)
    att = np.concatenate([angles(grid_row, AD // 2), angles(grid_col, AD // 2)], 1)
    for name, ang, scale in (("rq", ret, 1.0), ("rk", ret, DK ** -0.5), ("aq", att, AD ** -0.5), ("ak", att, 1.0)):
        for part, fn in (("cos", np.cos), ("sin", np.sin)):
            t = (fn(ang).astype(np.float32) * np.float32(scale)).reshape(2, P, 64).transpose(1, 0, 2)
            put(f"{name}_{part}", t.reshape(P, 128))
    return a


class Steps:

    def __init__(self, sem):
        self.sem, self.n = sem, 0

    def __call__(self, eng, ins):
        self.n += 1
        ins.then_inc(self.sem, 1)
        eng.wait_ge(self.sem, self.n)


def program(nc, t):
    ctx = ExitStack()
    with ctx:
        top = [nc.sbuf_base + (-nc.sbuf_base) % 64]

        placed = {}

        def at(name, shape, dt, offset):
            if name not in placed:
                placed[name] = nc.alloc_sbuf_tensor_at(name, shape, dt, offset=offset)
            return placed[name]

        def size(shape):
            return int(np.prod(shape[1:])) * 4

        def sb(name, shape, dt=F32):
            offset = top[0]
            top[0] += size(shape) + (-size(shape)) % 64
            return at(name, shape, dt, offset)

        def sem(name):
            return ctx.enter_context(nc.semaphore(name))

        ps = [ctx.enter_context(nc.psum_tensor(f"bank{i}", [P, BLK], F32)) for i in range(8)]

        cst = sb("constants", [P, N_CONST])

        def const(name):
            return cst[:, CAT[name]:CAT[name] + CONSTS[name]]

        ident = const("ident")
        cols = [sb(f"param_cols{l}", [P, P]) for l in range(DEPTH)]
        norm_cols = [sb(f"norm_cols{l}", [P, 24]) for l in range(DEPTH)]
        cond = sb("cond", [P, KD, 2])
        mods = [sb(f"mods{l}", [P, 48, 2]) for l in range(DEPTH)]
        gains = [sb(f"gains{l}", [P, 4, KD, 2]) for l in range(DEPTH)]
        heads = [sb(f"head_params{l}", [P, 8 + 32 + 32 + 32 + 8]) for l in range(DEPTH)]
        xres = sb("xres", [P, NT, D])
        small = sb("small", [P, 128])
        ring_at = top[0]
        raw = sb("raw_units", [P, 2, 2048])
        whi = sb("unit_hi", [P, 2, 2048], F32R)
        wlo = sb("unit_lo", [P, 2, 2048], F32R)
        hT_at = top[0]
        hT = [sb(f"hT_{n}", [P, KD, TOK], F32R) for n in ("hi", "lo")]
        outT_at = top[0]
        outT = [sb(f"outT_{n}", [P, KD, TOK], F32R) for n in ("hi", "lo")]
        merged_at = top[0]
        merged = sb("merged", [P, NT, D])
        work = top[0]
        limit = nc.sbuf_usable_end - 64

        raw_loaded = [[sem(f"raw_loaded{slot}_{half}") for half in range(2)] for slot in range(2)]
        hi_ready, lo_ready, unit_used = sem("hi_ready"), sem("lo_ready"), sem("unit_used")
        x_in = [sem("ctx_in"), sem("x_in")]
        params_in = sem("params_in")
        dve_step, act_step, pool_step = Steps(sem("dve_step")), Steps(sem("act_step")), Steps(sem("pool_step"))
        units, span = [], {}

        def unit_block(w, col, width=BLK):
            v = w.rearrange("(k p) n -> p k n", p=P)
            for half in range(2):
                units.append(v[:, 4 * half:4 * half + 4, col:col + width])

        def stage_units(name, add):
            a = len(units)
            add()
            span[name] = (a, len(units))

        for l in range(DEPTH):
            w_in, wb, wo = t["w_in"][l], t["w_branch"][l], t["w_out"][l]

            def cols_of(name, n):
                for b in range(n):
                    unit_block(w_in, COL[name] + b * BLK)

            def add_ssm():
                units.append(w_in.rearrange("(k p) n -> p k n", p=P)[:, :, COL["dt"]:COL["dt"] + SH])
                cols_of("xbc", 3)

            def add_gate(n, b):
                unit_block(w_in, COL["gate"] + n * D + b * BLK)

            def add_merge(n, early):
                for b in range(2):
                    if b or not early:
                        add_gate(n, b)
                    unit_block(wb[n], b * BLK)

            stage_units(f"ssm{l}", add_ssm)
            stage_units(f"z{l}", lambda: [cols_of("sz", 2), add_gate(1, 0)])
            stage_units(f"merge1_{l}", lambda: add_merge(1, True))
            stage_units(f"ret{l}", lambda: [cols_of("rq", 1), cols_of("rk", 1), cols_of("rv", 2)])
            stage_units(f"g{l}", lambda: [cols_of("rg", 2), add_gate(0, 0)])
            stage_units(f"merge0_{l}", lambda: add_merge(0, True))
            stage_units(f"att{l}", lambda: [cols_of("aq", 2), cols_of("akv", 1)])
            stage_units(f"merge2_{l}", lambda: add_merge(2, False))
            stage_units(f"out{l}", lambda: [unit_block(wo, b * BLK) for b in range(2)])
            if l == 0:
                w1, w3, w2 = t["ffn_w1"][0], t["ffn_w3"][0], t["ffn_w2"][0]

                def add_ffn():
                    for f in range(FF // 256):
                        for w in (w1, w3):
                            units.append(w.rearrange("(k p) n -> p k n", p=P)[:, :, f * 256:f * 256 + 256])

                stage_units("ffn_up", add_ffn)
                stage_units("ffn_down", lambda: [
                    units.append(w2.rearrange("(k p) n -> p k n", p=P)[:, 2 * u:2 * u + 2, :]) for u in range(FT // 2)])
        n_units = len(units)

        def view(buf, g):
            a, b = units[g].shape[1], units[g].shape[2]
            return buf[:, g % 2, 0:a * b].rearrange("p (a b) -> p a b", b=b)

        def half_of(v, half):
            n = v.shape[1] // 2
            return v[:, half * n:(half + 1) * n, :]

        def load_unit(sp, g):
            if g >= n_units:
                return
            for half in range(2):
                if g >= 2:
                    alike = np.prod(units[g].shape) == np.prod(units[g - 2].shape)
                    sp.wait_ge(lo_ready, 2 * (g - 2) + (half if alike else 1) + 1)
                sp.dma_start(half_of(view(raw, g), half), half_of(units[g], half)).then_inc(raw_loaded[g % 2][half], 16)

        def split_hi(act, g):
            if g >= n_units or g > stage_units_end[0]:
                return
            for half in range(2):
                act.wait_ge(raw_loaded[g % 2][half], 16 * (g // 2 + 1))
                if g >= 2 and half == 0:
                    act.wait_ge(unit_used, g - 1)
                act.activation(half_of(view(whi, g), half), half_of(view(raw, g), half), ACT.Copy).then_inc(hi_ready, 1)

        def split_lo(eng, g):
            if g >= n_units:
                return
            for half in range(2):
                eng.wait_ge(hi_ready, 2 * g + half + 1)
                lo, whole, hi = (half_of(view(buf, g), half) for buf in (wlo, raw, whi))
                eng.tensor_tensor(lo, whole, hi.bitcast(F32), ALU.subtract).then_inc(lo_ready, 1)

        stage_units_end = [0]

        def loads(sp, name):
            a, b = span[name]
            stage_units_end[0] = b
            for g in range(a + 3, b + 3):
                load_unit(sp, g)

        def splits_lo(eng, name, first=1):
            a, b = span[name]
            for g in range(a + first, b + 1):
                split_lo(eng, g)

        def three(pe, out, a, w, first, last):
            pe.matmul(out, a[0], w[0], start=first, stop=False)
            pe.matmul(out, a[0], w[1], start=False, stop=False)
            return pe.matmul(out, a[1], w[0], start=False, stop=last)

        def project(pe, g, banks, tiles, src=None):
            for u in range(2):
                project_half(pe, g, u, banks, tiles, src)

        def project_half(pe, g, u, banks, tiles, src=None):
            pe.wait_ge(lo_ready, 2 * (g + u + 1))
            w = [view(whi, g + u), view(wlo, g + u)]
            for k in range(4):
                kk = 4 * u + k
                for j, tile in enumerate(tiles):
                    a = [h[:, kk, tile * P:(tile + 1) * P] for h in (src or hT)]
                    last = three(pe, ps[banks[j]][:, :], a, [w[0][:, k, :], w[1][:, k, :]], kk == 0, kk == KD - 1)
            last.then_inc(unit_used, 1)

        def spread(col, n, m):
            return col.unsqueeze(2).to_broadcast([P, n, m])

        stage_no, in_use, cleared = [0], [], []

        def stage_sem(name):
            guard = nc.semaphore(f"{name}_{stage_no[0]}")
            in_use.append((guard, guard.__enter__()))
            return in_use[-1][1]

        def end_stage():
            for guard, handle in cleared:
                guard.__exit__(None, None, None)
            cleared[:] = in_use
            in_use.clear()
            for guard, handle in cleared:
                nc.sync.sem_clear(handle)
            stage_no[0] += 1

        ADA_U = 4

        def ada_unit(l, chunk, u):
            c = chunk * D + u * 256
            return t["ada_w"][l].rearrange("(k p) n -> p k n", p=P)[:, :, c:c + 256]

        def ada_rows(pe, out, buf):
            for k in range(KD):
                last = pe.matmul(out, cond[:, k, :], buf[:, k, :], start=k == 0, stop=k == KD - 1)
            return last

        def ada_turn(pe, out, rows, u):
            for m in range(2):
                f = 2 * u + m
                last = pe.matmul(out[:, 2 * f:2 * f + 2], rows[:, m * P:(m + 1) * P], ident[0:2, 0:2], start=True, stop=True)
            return last

        def ada_finish(dve, l, chunk, out):
            m = mods[l][:, 8 * chunk:8 * chunk + 8, :]
            dve_step(dve, dve.tensor_tensor(m, out.rearrange("p (f c) -> p f c", c=2),
                                            spread(col(l, "ada_b")[:, 8 * chunk:8 * chunk + 8], KD, 2), ALU.add))
            if chunk in (1, 4):
                gn = gains[l][:, chunk // 4, :, :]
                dve_step(dve, dve.tensor_scalar(gn, m, 1.0, None, ALU.add))
                dve_step(dve, dve.tensor_tensor(gn, gn, spread(col(l, "mix_pre" if chunk == 1 else "ffn_pre"), KD, 2), ALU.mult))
            if chunk in (2, 5):
                j = (chunk - 2) // 3
                dve_step(dve, dve.tensor_tensor(gains[l][:, 2 + j, :, :], m, spread(norm_cols[l][:, 8 * j:8 * j + 8], KD, 2), ALU.mult))

        def param_rows(eng, l, done):
            rows, nrows = row_bufs(l)
            for name, src in (("ada_b", t["ada_b"][l]), ("mix_pre", t["mix_norm_pre"][l]), ("ffn_pre", t["ffn_norm_pre"][l]),
                              ("conv_w", t["ssm_conv_w"][l].rearrange("w n -> (w n)")), ("conv_b", t["ssm_conv_b"][l])):
                eng.dma_start(rows[ROW[name]:ROW[name] + ROWS[name], :], src.rearrange("(a p) -> a p", p=P)).then_inc(done, 16)
            for j, name in enumerate(("mix_norm_post", "ffn_norm_post", "ssm_norm_w")):
                eng.dma_start(nrows[8 * j:8 * j + 8, :], t[name][l].rearrange("(a p) -> a p", p=P)).then_inc(done, 16)

        def row_bufs(l):
            return (at(f"param_rows{l}", [N_ROWS, P], F32, merged_at + 512 * (l + 1)),
                    at(f"norm_rows{l}", [24, P], F32, merged_at + 1536 + 512 * l))

        def turn_params(pe, l, turned):
            rows, nrows = row_bufs(l)
            pe.transpose(ps[l][:, 0:N_ROWS], rows[:, :], ident[0:N_ROWS, 0:N_ROWS])
            pe.transpose(ps[l][:, N_ROWS:N_ROWS + 24], nrows[:, :], ident[0:24, 0:24]).then_inc(turned, 1)

        def take_params(dve, l, turned):
            dve.wait_ge(turned, l + 1)
            dve_step(dve, dve.tensor_copy(cols[l][:, 0:N_ROWS], ps[l][:, 0:N_ROWS]))
            dve_step(dve, dve.tensor_copy(norm_cols[l][:, :], ps[l][:, N_ROWS:N_ROWS + 24]))

        def setup():
            cond_rows = at("cond_rows", [16, P], F32, merged_at)
            bufs = [at(f"ada_first{i}", [P, KD, 256], F32, hT_at + 8192 * i) for i in range(8)]
            row_buf = at("mod_rows", [2, 2, 256], F32, work)
            const_in, cond_in, row_in = (stage_sem(n) for n in ("const_in", "cond_in", "row_in"))
            turned, cond_turned, cond_out, summed, rows_out, ada_done = (
                stage_sem(n) for n in ("turned", "cond_turned", "cond_out", "summed", "rows_out", "ada_done"))
            unit_in = [stage_sem(f"ada_unit_in{i}") for i in range(8)]
            with nc.Block() as block:
                @block.sync
                def _(sp):
                    sp.dma_start(cond_rows[0:8, :], t["c"][0].rearrange("(a p) -> a p", p=P)).then_inc(cond_in, 16)
                    sp.dma_start(cond_rows[8:16, :], t["c_ctx"].rearrange("(a p) -> a p", p=P)).then_inc(cond_in, 16)
                    sp.dma_start(cst[:, :], t["consts"]).then_inc(const_in, 16)
                    for i in range(8):
                        sp.dma_start(bufs[i][:, :, :], ada_unit(0, i // 4, i % 4)).then_inc(unit_in[i], 16)
                    for j, src in enumerate((t["ctx"], t["x"])):
                        sp.dma_start(xres[:, 2 * j:2 * j + 2, :], src[0].rearrange("(t p) d -> p t d", p=P)).then_inc(x_in[j], 16)
                    param_rows(sp, 1, params_in)
                    for l in range(DEPTH):
                        for a, b, src in ((0, 8, t["ret_decay"][l].rearrange("a b -> (a b)")),
                                          (8, 40, t["ssm_dt_bias"][l].rearrange("a b -> (a b)")),
                                          (40, 72, t["ssm_a_log"][l].rearrange("a b -> (a b)")),
                                          (72, 104, t["ssm_d"][l].rearrange("a b -> (a b)")),
                                          (104, 112, t["att_sink"][l])):
                            sp.dma_start(heads[l][:, a:b], src.partition_broadcast(P)).then_inc(params_in, 16)
                    for g in range(3):
                        load_unit(sp, g)

                @block.scalar
                def _(act):
                    param_rows(act, 0, row_in)
                    act.wait_ge(cond_turned, 1)
                    act.activation(cond[:, :, :], ps[4][:, 0:16].rearrange("p (c k) -> p k c", c=2), ACT.Silu).then_inc(cond_out, 1)
                    for i in range(8):
                        act.wait_ge(summed, i + 1)
                        act.activation(row_buf[:, i % 2, :], ps[6 + i % 2][0:2, 0:256], ACT.Copy).then_inc(rows_out, 1)
                    split_hi(act, 0)

                @block.tensor
                def _(pe):
                    pe.wait_ge(const_in, 16)
                    pe.wait_ge(cond_in, 32)
                    pe.transpose(ps[4][:, 0:16], cond_rows[:, :], ident[0:16, 0:16]).then_inc(cond_turned, 1)
                    pe.wait_ge(cond_out, 1)
                    for i in range(9):
                        if i < 8:
                            pe.wait_ge(unit_in[i], 16)
                            ada_rows(pe, ps[6 + i % 2][0:2, 0:256], bufs[i]).then_inc(summed, 1)
                        if i:
                            n = i - 1
                            pe.wait_ge(rows_out, n + 1)
                            last = ada_turn(pe, ps[5][:, 16 * (n // 4):16 * (n // 4) + 16], row_buf[:, n % 2, :], n % 4)
                    last.then_inc(ada_done, 1)
                    pe.wait_ge(row_in, 16 * 8)
                    turn_params(pe, 0, turned)
                    pe.wait_ge(params_in, 16 * (8 + 5 * DEPTH))
                    turn_params(pe, 1, turned)

                @block.vector
                def _(dve):
                    take_params(dve, 0, turned)
                    dve.wait_ge(ada_done, 1)
                    for chunk in range(2):
                        ada_finish(dve, 0, chunk, ps[5][:, 16 * chunk:16 * chunk + 16])
                    take_params(dve, 1, turned)
                    split_lo(dve, 0)
            end_stage()

        def col(l, name, n=None):
            a = ROW[name]
            return cols[l][:, a:a + (n or ROWS[name])]

        def norm(l, tiles, which):
            A, B = gains[l][:, which, :, :], mods[l][:, 24 * which:24 * which + 8, :]
            n = len(tiles)
            xn = at("normed", [P, NT, D], F32, work)
            tmp = at("affine", [P, 2, TOK], F32, work + NT * D * 4)
            squares, roots, normed, turned, affine, parts = (
                stage_sem(s) for s in ("squares", "roots", "normed", "turned", "affine", "parts"))
            ssq, rstd = small[:, 8:12], small[:, 4:8]
            early_unit = span[f"ssm{l}"][0] + 1
            with nc.Block() as block:
                if which == 0:
                    stage_units_end[0] = early_unit

                    @block.gpsimd
                    def _(pool):
                        split_lo(pool, early_unit)

                @block.scalar
                def _(act):
                    if l == 0 and which == 0:
                        for tile in tiles:
                            act.wait_ge(x_in[tile // 2], 16)
                            act.activation(xn[:, tile, :], xres[:, tile, :], ACT.Square,
                                           accum_out=ssq[:, tile:tile + 1]).then_inc(squares, 1)
                    act.wait_ge(roots, 1)
                    act.activation(rstd[:, :], rstd[:, :], ACT.Sqrt).then_inc(roots, 1)
                    if which == 0:
                        split_hi(act, early_unit)
                    for d in range(KD):
                        act.wait_ge(turned, d + 1)
                        if d >= 2:
                            act.wait_ge(parts, d - 1)
                        segs = [(0, 2 * P, 1), (2 * P, TOK, 0)] if n == NT else [(0, 2 * P, 0)]
                        for s, (a, b, c) in enumerate(segs):
                            ins = act.activation(tmp[:, d % 2, a:b], ps[d][:, a:b], ACT.Identity,
                                                 scale=A[:, d, c:c + 1], bias=B[:, d, c:c + 1])
                        ins.then_inc(affine, 1)

                @block.vector
                def _(dve):
                    lo, hi = tiles[0], tiles[-1] + 1
                    if l == 0 and which == 0:
                        dve.wait_ge(squares, n)
                    dve_step(dve, dve.memset(rstd[:, :], 1.0))
                    dve.tensor_scalar(rstd[:, lo:hi], ssq[:, lo:hi], 1.0 / D, EPS, ALU.mult, ALU.add).then_inc(roots, 1)
                    dve.wait_ge(roots, 2)
                    dve_step(dve, dve.reciprocal(rstd[:, :], rstd[:, :]))
                    for tile in tiles:
                        dve.tensor_scalar(xn[:, tile, :], xres[:, tile, :], rstd[:, tile:tile + 1], None,
                                          ALU.mult).then_inc(normed, 1)
                    for d in range(KD):
                        dve.wait_ge(affine, d + 1)
                        w = n * P
                        dve_step(dve, dve.tensor_copy(hT[0][:, d, lo * P:hi * P], tmp[:, d % 2, 0:w]))
                        dve.tensor_tensor(hT[1][:, d, lo * P:hi * P], tmp[:, d % 2, 0:w],
                                          hT[0][:, d, lo * P:hi * P].bitcast(F32), ALU.subtract).then_inc(parts, 1)

                @block.tensor
                def _(pe):
                    pe.wait_ge(normed, n)
                    for d in range(KD):
                        for j, tile in enumerate(tiles):
                            last = pe.transpose(ps[d][:, j * P:(j + 1) * P], xn[:, tile, d * P:(d + 1) * P], ident)
                        last.then_inc(turned, 1)
            end_stage()

        def ssm_project(l):
            a0, b0 = span[f"ssm{l}"]
            a1 = a0 + 1
            ux = at("u_x", [P, 8, TOK], F32, work)
            bT, cT, btok, xtok = ssm_tensors()[:4]
            dtv, dta, tmp1, cums, exps, ecum, wst, dec, skip = decay_tensors()
            acc = at("conv_acc", [P, 4, TOK], F32, work + 34816)
            dtT = at("dt_T", [SH, TOK], F32, outT_at + 16384)
            names = ("acc_set", "conv_done", "u_ready", "turned", "turned_out", "dt_copied", "dt_turned", "dt_act",
                     "dt_dve", "cum_sum", "cum_out", "exps_done")
            (acc_set, conv_done, u_ready, turned, turned_out, dt_copied, dt_turned, dt_act,
             dt_dve, cum_sum, cum_out, exps_done) = (stage_sem(s) for s in names)
            cw, cb, hp = col(l, "conv_w"), col(l, "conv_b"), heads[l]

            def u_of(i):
                return ux[:, i, :] if i < 8 else (bT if i < 10 else cT)[:, i % 2, :]

            def d4(a, d):
                return a[:, d * 64:(d + 1) * 64].rearrange("p (t h) -> p t h", h=SH)

            with nc.Block() as block:
                @block.sync
                def _(sp):
                    loads(sp, f"ssm{l}")

                @block.gpsimd
                def _(pool):
                    splits_lo(pool, f"ssm{l}", 2)

                @block.scalar
                def _(act):
                    split_hi(act, a1 + 1)
                    for n in range(3):
                        if n == 0:
                            act.wait_ge(dt_dve, 1)
                            act_step(act, act.activation(dta[:, :], tmp1[:, :], ACT.Exp, scale=-1.0))
                            act.activation(exps[:, :], hp[:, 40:72], ACT.Exp).then_inc(dt_act, 1)
                            act.wait_ge(dt_dve, 2)
                            act.activation(cums[:, 0:128], tmp1[:, :], ACT.Ln).then_inc(dt_act, 1)
                        split_hi(act, a1 + 2 * n + 2)
                        act.wait_ge(unit_used, a1 + 2 * n + 2)
                        for m in range(4):
                            i = 4 * n + m
                            act.activation(acc[:, m, :], ps[4 * (n % 2) + m][:, :], ACT.Identity,
                                           scale=cw[:, 12 + i:13 + i], bias=cb[:, i:i + 1]).then_inc(acc_set, 1)
                        split_hi(act, a1 + 2 * n + 3)
                        for m in range(4):
                            i = 4 * n + m
                            act.wait_ge(conv_done, i + 1)
                            act.activation(u_of(i), acc[:, m, :], ACT.Silu).then_inc(u_ready, 1)
                        act.wait_ge(u_ready, 4 * n + 4)
                        if n == 0:
                            act.wait_ge(cum_out, 1)
                            act.activation(ecum[:, :], cums[:, 0:128], ACT.Exp)
                            act.activation(dec[:, :], cums[:, 128:256], ACT.Exp)
                            act.activation(wst[:, :], wst[:, :], ACT.Exp).then_inc(exps_done, 1)

                @block.vector
                def _(dve):
                    def conv(n):
                        for i in range(4 * n, 4 * n + 4):
                            m = i - 4 * n
                            s = ps[4 * (n % 2) + m][:, :].rearrange("p (s t) -> p s t", s=2)
                            o = acc[:, m, :].rearrange("p (s t) -> p s t", s=2)
                            dve.wait_ge(acc_set, i + 1)
                            dve_step(dve, dve.scalar_tensor_tensor(o[:, :, 1:], s[:, :, :-1], cw[:, i:i + 1], o[:, :, 1:],
                                                                   ALU.mult, ALU.add))
                            dve.scalar_tensor_tensor(o[:, :, :-1], s[:, :, 1:], cw[:, 24 + i:25 + i], o[:, :, :-1],
                                                     ALU.mult, ALU.add).then_inc(conv_done, 1)

                    def take_turned(i):
                        dve.wait_ge(turned, i + 1)
                        out = xtok[:, :, i * P:(i + 1) * P] if i < 8 else btok[:, :, (i - 8) * P:(i - 7) * P]
                        dve.tensor_copy(out, ps[5 + i % 3][:, :].rearrange("p (t f) -> p t f", t=NT)).then_inc(turned_out, 1)

                    dve.wait_ge(unit_used, a0 + 1)
                    dve.tensor_copy(dtT[:, :], ps[7][0:SH, :]).then_inc(dt_copied, 1)
                    dve.wait_ge(dt_turned, 1)
                    dtraw = ps[6][:, 0:NT * SH].rearrange("p (t h) -> p t h", h=SH)
                    for d in range(2):
                        bias = hp[:, 8 + 16 * d:24 + 16 * d].unsqueeze(1).to_broadcast([P, NT, SH])
                        dve_step(dve, dve.tensor_tensor(d4(dtv, d), dtraw, bias, ALU.add))
                    dve.scalar_tensor_tensor(tmp1[:, :], dtv[:, :], -1.0, dtv[:, :], ALU.mult, ALU.max).then_inc(dt_dve, 1)
                    dve.wait_ge(dt_act, 1)
                    dve.tensor_scalar(tmp1[:, :], dta[:, :], 1.0, None, ALU.add).then_inc(dt_dve, 1)
                    dve.wait_ge(dt_dve, 2)
                    dve_step(dve, dve.tensor_scalar(ecum[:, :], tmp1[:, :], -1.0, 1e-30, ALU.add, ALU.max))
                    dve_step(dve, dve.reciprocal(ecum[:, :], ecum[:, :]))
                    dve_step(dve, dve.tensor_tensor(ecum[:, :], ecum[:, :], dta[:, :], ALU.mult))
                    dve.wait_ge(dt_act, 2)
                    dve_step(dve, dve.tensor_tensor(ecum[:, :], ecum[:, :], cums[:, 0:128], ALU.mult))
                    dve_step(dve, dve.scalar_tensor_tensor(dtv[:, :], dtv[:, :], 0.0, ecum[:, :], ALU.max, ALU.add))
                    for d in range(2):
                        ea = exps[:, 16 * d:16 * d + 16].unsqueeze(1).to_broadcast([P, NT, SH])
                        ins = dve.scalar_tensor_tensor(d4(dta, d), d4(dtv, d), -1.0, ea, ALU.mult, ALU.mult)
                    ins.then_inc(dt_dve, 1)
                    dve.wait_ge(cum_sum, 1)
                    dve_step(dve, dve.tensor_copy(cums[:, :], ps[5][:, 0:256]))
                    dve.tensor_tensor(wst[:, :], cums[:, 128:256], cums[:, 0:128], ALU.subtract).then_inc(cum_out, 1)
                    conv(0)
                    dve.wait_ge(exps_done, 1)
                    dve_step(dve, dve.tensor_tensor(wst[:, :], wst[:, :], dtv[:, :], ALU.mult))
                    conv(1)
                    for i in range(4):
                        take_turned(i)
                    conv(2)
                    for i in range(4, 10):
                        take_turned(i)

                @block.tensor
                def _(pe):
                    def turn(i):
                        pe.wait_ge(u_ready, i + 1)
                        if i >= 3:
                            pe.wait_ge(turned_out, i - 2)
                        for tile in range(NT):
                            last = pe.transpose(ps[5 + i % 3][:, tile * P:(tile + 1) * P],
                                                u_of(i)[:, tile * P:(tile + 1) * P], ident)
                        last.then_inc(turned, 1)

                    pe.wait_ge(lo_ready, 2 * (a0 + 1))
                    for k in range(KD):
                        last = three(pe, ps[7][0:SH, :], [view(whi, a0)[:, k, :], view(wlo, a0)[:, k, :]],
                                     [h[:, k, :] for h in hT], k == 0, k == KD - 1)
                    last.then_inc(unit_used, 1)
                    for n in range(3):
                        if n == 1:
                            pe.wait_ge(cum_out, 1)
                        if n == 2:
                            pe.wait_ge(conv_done, 4)
                        for u in range(2):
                            g = a1 + 2 * n + u
                            pe.wait_ge(lo_ready, 2 * (g + 1))
                            wh, wl = view(whi, g), view(wlo, g)
                            for k in range(4):
                                kk = 4 * u + k
                                for m in range(4):
                                    a = [wh[:, k, m * P:(m + 1) * P], wl[:, k, m * P:(m + 1) * P]]
                                    last = three(pe, ps[4 * (n % 2) + m][:, :], a, [h[:, kk, :] for h in hT],
                                                 kk == 0, kk == KD - 1)
                            last.then_inc(unit_used, 1)
                            if n == 0 and u == 0:
                                pe.wait_ge(dt_copied, 1)
                                for tile in range(NT):
                                    last = pe.transpose(ps[6][:, tile * SH:(tile + 1) * SH], dtT[:, tile * P:(tile + 1) * P],
                                                        ident[0:SH, 0:SH])
                                last.then_inc(dt_turned, 1)
                            if n == 2 and u == 0:
                                pe.wait_ge(conv_done, 8)
                                for i in range(4):
                                    turn(i)
                        if n == 0:
                            pe.wait_ge(dt_dve, 3)
                            for d, tri in enumerate(("tri_f", "tri_b")):
                                pe.matmul(ps[5][:, 64 * d:64 * d + 64], const(tri), dta[:, 64 * d:64 * d + 64], start=True, stop=True)
                                last = pe.matmul(ps[5][:, 128 + 64 * d:192 + 64 * d], const("ones"), dta[:, 64 * d:64 * d + 64],
                                                 start=True, stop=True)
                            last.then_inc(cum_sum, 1)
                    for i in range(4, 10):
                        turn(i)
            end_stage()

        def decay_tensors():
            p0 = work + 28672 + 256
            dtv, dta, tmp1, cums, exps = (at(f"ssm_{n}", [P, w], F32, p0 + o) for n, w, o in (
                ("dt", 128, 0), ("dta", 128, 512), ("tmp", 128, 1024), ("cum_tot", 256, 1536), ("expa", 32, 2560)))
            ecum, wst, dec, skip = (at(f"ssm_{n}", [P, w], F32, p0 + 2688 + o) for n, w, o in (
                ("ecum", 128, 0), ("w_state", 128, 512), ("decay", 128, 1024), ("skip", 16, 1536)))
            return dtv, dta, tmp1, cums, exps, ecum, wst, dec, skip

        def ssm_tensors():
            bT = at("B_T", [P, SG, TOK], F32, work + 16384)
            cT = at("C_T", [P, SG, TOK], F32, work + 20480)
            btok = at("B_tok", [P, NT, SG * ST], F32, work + 24576)
            xtok = at("x_tok", [P, NT, D], F32, outT_at)
            y = at("y_ssm", [P, NT, D], F32, work)
            return bT, cT, btok, xtok, y

        ORDER = ([0, 1, 2, 3], [1, 0, 3, 2])

        def ssm_mix(l, tiles, ada_chunks):
            ada_buf = [at(f"ada_unit{i}", [P, KD, 256], F32, merged_at + 8192 * i) for i in range(2)]
            ada_in = [stage_sem(f"ada_in{i}") for i in range(2)]
            ada_used, ada_out, ada_turned = stage_sem("ada_used"), stage_sem("ada_out"), stage_sem("ada_turned")
            ada_row = at("ada_row", [2, 256], F32, work + 51200)
            ada_units = [(la, c, u) for la, c in ada_chunks for u in range(ADA_U)]

            def ada_cols(i):
                return ps[6][:, 256 + 16 * i:272 + 16 * i]

            bT, cT, btok, xtok, y = ssm_tensors()
            dtv, dta, tmp1, cums, exps, ecum, wst, dec, skip = decay_tensors()
            cbs = at("CB", [P, 2, P], F32, work + 34816)
            state = at("ssm_state", [P, 2, SG, 512], F32, work + 36864)
            xw = at("x_weighted", [P, 512], F32, work + 45056)
            part = at("y_part", [P, 2, 512], F32, work + 47104)
            seg = at("segments", [P, 2, 2, HG, P], F32, outT_at + 16384)
            hp = heads[l]

            def hg(a, d, tile, g):
                b = d * 64 + tile * SH + g * HG
                return a[:, b:b + HG]

            def wide(a):
                return spread(a, HG, HD)

            def by_head(a):
                return a.rearrange("p (h e) -> p h e", h=HG)

            names = ("skipped", "backward", "seg_sum", "seg_out", "seg_exp", "mixed",
                     "intra", "intra_out", "weighted", "update", "update_out", "inter", "inter_out")
            (skipped, backward, seg_sum, seg_out, seg_exp, mixed,
             intra, intra_out, weighted, update, update_out, inter, inter_out) = (stage_sem(s) for s in names)
            jobs = [(tile, g) for tile in tiles for g in range(SG)]
            steps = [(s, d, g) for s in range(NT) for d in range(2) for g in range(SG)]
            inters = [x for x in steps if x[0] > 0 and ORDER[x[1]][x[0]] in tiles]
            def skips(pool):
                pool_step(pool, pool.tensor_tensor(skip[:, :], hp[:, 72:88], hp[:, 88:104], ALU.add))
                for tile, g in jobs:
                    pool.tensor_tensor(by_head(y[:, tile, g * 512:(g + 1) * 512]), by_head(xtok[:, tile, g * 512:(g + 1) * 512]),
                                       wide(skip[:, g * HG:(g + 1) * HG]), ALU.mult).then_inc(skipped, 1)

            def ada_copy(act, i):
                act.wait_ge(ada_used, i + 1)
                if i:
                    act.wait_ge(ada_turned, i)
                act.activation(ada_row[:, :], ps[6][0:2, 0:256], ACT.Copy).then_inc(ada_out, 1)

            with nc.Block() as block:
                @block.sync
                def _(sp):
                    for i, (la, c, u) in enumerate(ada_units):
                        if i >= 2:
                            sp.wait_ge(ada_used, i - 1)
                        sp.dma_start(ada_buf[i % 2][:, :, :], ada_unit(la, c, u)).then_inc(ada_in[i % 2], 16)

                @block.gpsimd
                def _(pool):
                    skips(pool)
                    for n, (tile, g) in enumerate(jobs):
                        pool.wait_ge(seg_exp, n + 1)
                        s = seg[:, n % 2, 1, :, :]
                        pool.tensor_tensor(s, s, spread(hg(dtv, 1, tile, g), HG, P), ALU.mult).then_inc(backward, 1)

                @block.scalar
                def _(act):
                    for n in range(len(jobs)):
                        act.wait_ge(seg_out, n + 1)
                        for d in range(2):
                            ins = act.activation(seg[:, n % 2, d, :, :], seg[:, n % 2, d, :, :], ACT.Exp)
                        ins.then_inc(seg_exp, 1)
                        ada_copy(act, n)
                    for i in range(len(jobs), len(ada_units)):
                        ada_copy(act, i)

                @block.vector
                def _(dve):
                    def segments(n):
                        tile, g = jobs[n]
                        s = seg[:, n % 2, :, :, :]
                        dve.wait_ge(seg_sum, n + 1)
                        for d in (1, 0):
                            if n >= 2 and d == 0:
                                dve.wait_ge(intra, n - 1)
                            for h in range(HG):
                                bank = ps[2 * d + h // 4]
                                cum = hg(cums, d, tile, g)[:, h:h + 1]
                                dve.scalar_tensor_tensor(s[:, d, h, :], bank[:, (h % 4) * P:(h % 4 + 1) * P], cum,
                                                         const("neg_low" if d == 0 else "neg_up"), ALU.subtract, ALU.add)
                        dve.tensor_copy(cbs[:, n % 2, :], ps[4][:, 0:P]).then_inc(seg_out, 1)

                    def mix(n):
                        tile, g = jobs[n]
                        s = seg[:, n % 2, :, :, :]
                        dve.wait_ge(seg_exp, n + 1)
                        dt = spread(hg(dtv, 0, tile, g), HG, P)
                        dve_step(dve, dve.tensor_tensor(s[:, 0, :, :], s[:, 0, :, :], dt, ALU.mult))
                        dve.wait_ge(backward, n + 1)
                        dve_step(dve, dve.tensor_tensor(s[:, 0, :, :], s[:, 0, :, :], s[:, 1, :, :], ALU.add))
                        dve.tensor_tensor(s[:, 0, :, :], s[:, 0, :, :], cbs[:, n % 2, :].unsqueeze(1).to_broadcast([P, HG, P]),
                                          ALU.mult).then_inc(mixed, 1)

                    def add_intra(n):
                        tile, g = jobs[n]
                        yo = y[:, tile, g * 512:(g + 1) * 512]
                        dve.wait_ge(skipped, n + 1)
                        dve.wait_ge(intra, n + 1)
                        dve.tensor_tensor(yo, yo, ps[5 + 2 * (n % 2)][:, :], ALU.add).then_inc(intra_out, 1)

                    segments(0)
                    for n in range(len(jobs)):
                        if n + 1 < len(jobs):
                            segments(n + 1)
                        if n:
                            add_intra(n - 1)
                        mix(n)
                    add_intra(len(jobs) - 1)
                    n_up = n_in = 0
                    for s, d, g in steps:
                        tile = ORDER[d][s]
                        if s < NT - 1:
                            if n_up:
                                dve.wait_ge(update, n_up)
                            dve.tensor_tensor(by_head(xw[:, :]), by_head(xtok[:, tile, g * 512:(g + 1) * 512]),
                                              wide(hg(wst, d, tile, g)), ALU.mult).then_inc(weighted, 1)
                        if (s, d, g) in inters:
                            dve.wait_ge(inter, n_in + 1)
                            yo = y[:, tile, g * 512:(g + 1) * 512]
                            pt = part[:, n_in % 2, :]
                            dve_step(dve, dve.tensor_tensor(by_head(pt), by_head(ps[2 + n_in % 2][:, :]),
                                                            wide(hg(ecum, d, tile, g)), ALU.mult))
                            dve.tensor_tensor(yo, yo, pt, ALU.add).then_inc(inter_out, 1)
                            n_in += 1
                        if s < NT - 1:
                            st = state[:, d, g, :]
                            if s:
                                dve_step(dve, dve.tensor_tensor(by_head(st), by_head(st), wide(hg(dec, d, tile, g)), ALU.mult))
                            dve.wait_ge(update, n_up + 1)
                            if s:
                                dve.tensor_tensor(st, st, ps[n_up % 2][:, :], ALU.add).then_inc(update_out, 1)
                            else:
                                dve.tensor_copy(st, ps[n_up % 2][:, :]).then_inc(update_out, 1)
                            n_up += 1
                    dve.wait_ge(ada_turned, len(ada_units))
                    for i, (la, c) in enumerate(ada_chunks):
                        ada_finish(dve, la, c, ada_cols(i))

                @block.tensor
                def _(pe):
                    todo = list(enumerate(ada_units))

                    def turn_row(i):
                        pe.wait_ge(ada_out, i + 1)
                        ada_turn(pe, ada_cols(i // ADA_U), ada_row, ada_units[i][2]).then_inc(ada_turned, 1)

                    def modulation():
                        if todo:
                            i, _ = todo.pop(0)
                            if i:
                                turn_row(i - 1)
                            pe.wait_ge(ada_in[i % 2], 16 * (i // 2 + 1))
                            ada_rows(pe, ps[6][0:2, 0:256], ada_buf[i % 2]).then_inc(ada_used, 1)

                    for n in range(len(jobs) + 2):
                        if n < len(jobs):
                            tile, g = jobs[n]
                            tok = slice(tile * P, (tile + 1) * P)
                            if n:
                                pe.wait_ge(seg_out, n)
                            pe.matmul(ps[4][:, 0:P], bT[:, g, tok], cT[:, g, tok], start=True, stop=True)
                            for d, tri in enumerate(("tri_f", "tri_b")):
                                for h in range(HG):
                                    w = hg(dta, d, tile, g)[:, h:h + 1].to_broadcast([P, P])
                                    last = pe.matmul(ps[2 * d + h // 4][:, (h % 4) * P:(h % 4 + 1) * P], w, const(tri),
                                                     start=True, stop=True)
                            last.then_inc(seg_sum, 1)
                        if n >= 2:
                            tile, g = jobs[n - 2]
                            pe.wait_ge(mixed, n - 1)
                            if n >= 4:
                                pe.wait_ge(intra_out, n - 3)
                            for h in range(HG):
                                c = (g * HG + h) * HD
                                last = pe.matmul(ps[5 + 2 * (n % 2)][:, h * HD:(h + 1) * HD],
                                                 seg[:, n % 2, 0, h, :], xtok[:, tile, c:c + HD], start=True, stop=True)
                            last.then_inc(intra, 1)
                        if n < len(jobs):
                            modulation()
                    n_up = n_in = 0
                    for s, d, g in steps:
                        modulation()
                        tile = ORDER[d][s]
                        if (s, d, g) in inters:
                            pe.wait_ge(update_out, 4 * (s - 1) + 2 * d + g + 1)
                            if n_in >= 2:
                                pe.wait_ge(inter_out, n_in - 1)
                            pe.matmul(ps[2 + n_in % 2][:, :], cT[:, g, tile * P:(tile + 1) * P], state[:, d, g, :],
                                      start=True, stop=True).then_inc(inter, 1)
                            n_in += 1
                        if s < NT - 1:
                            pe.wait_ge(weighted, n_up + 1)
                            if n_up >= 2:
                                pe.wait_ge(update_out, n_up - 1)
                            pe.matmul(ps[n_up % 2][:, :], btok[:, tile, g * ST:(g + 1) * ST], xw[:, :],
                                      start=True, stop=True).then_inc(update, 1)
                            n_up += 1
                    while todo:
                        modulation()
                    turn_row(len(ada_units) - 1)
            end_stage()

        def turn_to_outT(pe, src, tiles, f_range, ready, turned, parts, banks=range(8)):
            nb = len(banks)
            for f in f_range:
                if ready is not None:
                    pe.wait_ge(*ready(f))
                if f >= nb:
                    pe.wait_ge(parts, f - nb + 1)
                for j, tile in enumerate(tiles):
                    last = pe.transpose(ps[banks[f % nb]][:, j * P:(j + 1) * P], src[:, tile, f * P:(f + 1) * P], ident)
                last.then_inc(turned, 1)

        def outT_hi(act, tiles, f, turned, hi_out, scale=1.0, banks=range(8)):
            lo, n = tiles[0] * P, len(tiles) * P
            act.wait_ge(turned, f + 1)
            act.activation(outT[0][:, f, lo:lo + n], ps[banks[f % len(banks)]][:, 0:n], ACT.Identity if not isinstance(scale, float) else ACT.Copy,
                           scale=scale).then_inc(hi_out, 1)

        def outT_lo(dve, tiles, f, hi_out, parts, scale=1.0, banks=range(8)):
            lo, n = tiles[0] * P, len(tiles) * P
            dve.wait_ge(hi_out, f + 1)
            dve.scalar_tensor_tensor(outT[1][:, f, lo:lo + n], ps[banks[f % len(banks)]][:, 0:n], scale,
                                     outT[0][:, f, lo:lo + n].bitcast(F32), ALU.mult, ALU.subtract).then_inc(parts, 1)

        LATE_BANKS = [4, 5, 6, 7]

        def ssm_gate(l, tiles):
            a0, b0 = span[f"z{l}"]
            y = ssm_tensors()[4]
            gate = at("z_gate", [P, NT, 512], F32, work + 16384)
            junk = at("squares_junk", [P, 512], F32, work + 24576)
            gated, silu_out, squared, roots, scaled, turned, hi_out, parts = (
                stage_sem(s) for s in ("gated", "silu_out", "squared", "roots", "scaled", "turned", "hi_out", "parts"))
            ssq = small[:, 8:16]
            n = len(tiles)
            lo = 2 * tiles[0]
            with nc.Block() as block:
                @block.sync
                def _(sp):
                    loads(sp, f"z{l}")

                @block.gpsimd
                def _(pool):
                    splits_lo(pool, f"z{l}")

                @block.scalar
                def _(act):
                    split_hi(act, a0 + 1)
                    for g in range(SG):
                        for u in range(2):
                            split_hi(act, a0 + 2 * g + u + 2)
                        act.wait_ge(unit_used, a0 + 2 * g + 2)
                        if g:
                            act.wait_ge(gated, n)
                        for j in range(n):
                            act.activation(gate[:, j, :], ps[4 * g + j][:, :], ACT.Silu).then_inc(silu_out, 1)
                        for j, tile in enumerate(tiles):
                            act.wait_ge(gated, n * g + j + 1)
                            act_step(act, act.activation(junk[:, :], y[:, tile, g * 512:(g + 1) * 512], ACT.Square,
                                                         accum_out=ssq[:, 2 * tile + g:2 * tile + g + 1]))
                    act.activation(small[:, 16:17], ssq[:, lo:lo + 1], ACT.Copy).then_inc(squared, 1)
                    act.wait_ge(roots, 1)
                    act.activation(ssq[:, lo:8], ssq[:, lo:8], ACT.Sqrt).then_inc(roots, 1)
                    for u in range(2):
                        split_hi(act, a0 + 2 * SG + u + 2)
                    for f in range(KD):
                        outT_hi(act, tiles, f, turned, hi_out, norm_cols[l][:, 16 + f:17 + f], LATE_BANKS)

                @block.vector
                def _(dve):
                    for g in range(SG):
                        for j, tile in enumerate(tiles):
                            dve.wait_ge(silu_out, n * g + j + 1)
                            yo = y[:, tile, g * 512:(g + 1) * 512]
                            dve.tensor_tensor(yo, yo, gate[:, j, :], ALU.mult).then_inc(gated, 1)
                    dve.wait_ge(squared, 1)
                    dve.tensor_scalar(ssq[:, lo:8], ssq[:, lo:8], 1.0 / 512, EPS, ALU.mult, ALU.add).then_inc(roots, 1)
                    dve.wait_ge(roots, 2)
                    dve_step(dve, dve.reciprocal(ssq[:, lo:8], ssq[:, lo:8]))
                    for g in range(SG):
                        for tile in tiles:
                            yo = y[:, tile, g * 512:(g + 1) * 512]
                            ins = dve.tensor_scalar(yo, yo, ssq[:, 2 * tile + g:2 * tile + g + 1], None, ALU.mult)
                        ins.then_inc(scaled, 1)
                    for f in range(KD):
                        outT_lo(dve, tiles, f, hi_out, parts, norm_cols[l][:, 16 + f:17 + f], LATE_BANKS)

                @block.tensor
                def _(pe):
                    for g in range(SG):
                        project(pe, a0 + 2 * g, [4 * g + j for j in range(n)], tiles)
                    pe.wait_ge(silu_out, n)
                    project(pe, a0 + 2 * SG, range(n), tiles)
                    pe.wait_ge(silu_out, 2 * n)
                    turn_to_outT(pe, y, tiles, range(KD), lambda f: (scaled, f // 4 + 1), turned, parts, LATE_BANKS)
            end_stage()

        def merge(l, branch, tiles, first):
            a0, b0 = span[f"merge{branch}_{l}"]
            gate = at("merge_gate", [P, 2, NT, 512], F32, work)
            part = at("merge_part", [P, 2, 512], F32, work + 16384)
            gate_out, merged_out = stage_sem("gate_out"), stage_sem("merged_out")
            n = len(tiles)
            early = branch != 2
            a0 -= 2 * early
            with nc.Block() as block:
                @block.sync
                def _(sp):
                    loads(sp, f"merge{branch}_{l}")

                @block.gpsimd
                def _(pool):
                    splits_lo(pool, f"merge{branch}_{l}")

                @block.scalar
                def _(act):
                    split_hi(act, span[f"merge{branch}_{l}"][0] + 1)
                    for b in range(2):
                        if b or not early:
                            for u in range(2):
                                split_hi(act, a0 + 4 * b + u + 2)
                        act.wait_ge(unit_used, a0 + 4 * b + 2)
                        for j in range(n):
                            act.activation(gate[:, b, j, :], ps[j][:, :], ACT.Sigmoid).then_inc(gate_out, 1)
                        for u in range(2, 4):
                            split_hi(act, a0 + 4 * b + u + 2)

                @block.vector
                def _(dve):
                    for b in range(2):
                        dve.wait_ge(unit_used, a0 + 4 * b + 4)
                        for j, tile in enumerate(tiles):
                            dve.wait_ge(gate_out, n * b + j + 1)
                            out = merged[:, tile, b * 512:(b + 1) * 512]
                            if first:
                                dve.tensor_tensor(out, gate[:, b, j, :], ps[4 + j][:, :], ALU.mult).then_inc(merged_out, 1)
                            else:
                                pt = part[:, j % 2, :]
                                dve_step(dve, dve.tensor_tensor(pt, gate[:, b, j, :], ps[4 + j][:, :], ALU.mult))
                                dve.tensor_tensor(out, out, pt, ALU.add).then_inc(merged_out, 1)

                @block.tensor
                def _(pe):
                    for b in range(2):
                        if b:
                            pe.wait_ge(gate_out, n)
                        if b or not early:
                            project(pe, a0 + 4 * b, range(n), tiles)
                        if b:
                            pe.wait_ge(merged_out, n)
                        project(pe, a0 + 4 * b + 2, [4 + j for j in range(n)], tiles, outT)
            end_stage()

        def rope(dve, out, src, tile, table, n_heads, tmp, axial):
            half = 32 if axial else 64
            pairs = n_heads * (2 if axial else 1)

            def parts(a):
                v = a.rearrange("p (h e w) -> p h e w", e=2, w=half)
                return v[:, :, 0, :], v[:, :, 1, :]

            def angle(kind):
                a = const(f"{table}_{kind}")[:, 64 * (tile - 2):64 * (tile - 1)]
                if axial:
                    return a.rearrange("p (e w) -> p e w", w=half).unsqueeze(1).to_broadcast([P, n_heads, 2, half])
                return a.unsqueeze(1).to_broadcast([P, n_heads, half])

            def shaped(a):
                return a.rearrange("p (h e) w -> p h e w", e=2) if axial else a

            w = pairs * half
            s1, s2 = (shaped(v) for v in parts(src))
            o1, o2 = (shaped(v) for v in parts(out))
            m = [shaped(tmp[:, i, 0:w].rearrange("p (h w) -> p h w", w=half)) for i in range(4)]
            cos, sin = angle("cos"), angle("sin")
            dve.tensor_tensor(m[0], s1, cos, ALU.mult)
            dve.tensor_tensor(m[1], s2, sin, ALU.mult)
            dve.tensor_tensor(m[2], s1, sin, ALU.mult)
            dve_step(dve, dve.tensor_tensor(m[3], s2, cos, ALU.mult))
            dve.tensor_tensor(o1, m[0], m[1], ALU.subtract)
            return dve.tensor_tensor(o2, m[2], m[3], ALU.add)

        def ret_tensors():
            ktok = at("k_tok", [P, NT, RH * DK], F32, work)
            qT = at("ret_qT", [P, RH, TOK], F32, work + 8192)
            kT = at("ret_kT", [P, RH, TOK], F32, work + 16384)
            o = at("ret_o", [P, NT, D], F32, work + 24576)
            qtok = at("q_tok", [P, NT, RH * DK], F32, work + 40960)
            v = at("ret_v", [P, NT, D], F32, outT_at)
            return ktok, qT, kT, o, qtok, v

        def ret_decays():
            decay = at("ret_decays", [P, RH, P], F32, outT_at + 16384)
            wts, gam = small[:, 48:80], small[:, 80:88]
            logs, t1, t2 = small[:, 20:28], small[:, 28:36], small[:, 36:44]
            tmp = at("decay_exps", [P, 8, P], F32, work + 24576)
            return decay, wts, gam, logs, t1, t2, tmp

        def decays_act(act, lg_dve, lg_act, exps_done):
            decay, wts, gam, logs, t1, t2, tmp = ret_decays()
            act.wait_ge(lg_dve, 1)
            act.activation(t2, t1, ACT.Exp, scale=-1.0).then_inc(lg_act, 1)
            act.wait_ge(lg_dve, 2)
            act.activation(t2, t2, ACT.Ln).then_inc(lg_act, 1)
            act.wait_ge(lg_dve, 3)
            for d in range(2):
                for h in range(RH):
                    act.activation(tmp[:, 4 * d + h, :], const("dist_f" if d == 0 else "dist_b"), ACT.Exp,
                                   scale=logs[:, 4 * d + h:4 * d + h + 1])
            for kind in range(4):
                act.activation(wts[:, kind * 8:kind * 8 + 8], logs, ACT.Exp,
                               scale=const("ret_w")[:, kind:kind + 1])
            act.activation(gam, logs, ACT.Exp, scale=float(P)).then_inc(exps_done, 1)

        def decays_dve(dve, l, lg_dve, lg_act, exps_done, decay_done):
            decay, wts, gam, logs, t1, t2, tmp = ret_decays()
            r = heads[l][:, 0:8]
            dve.scalar_tensor_tensor(t1, r, -1.0, r, ALU.mult, ALU.max).then_inc(lg_dve, 1)
            dve.wait_ge(lg_act, 1)
            dve.tensor_scalar(t2, t2, 1.0, None, ALU.add).then_inc(lg_dve, 1)
            dve.wait_ge(lg_act, 2)
            dve.scalar_tensor_tensor(logs, r, 0.0, t2, ALU.min, ALU.subtract).then_inc(lg_dve, 1)
            dve.wait_ge(exps_done, 1)
            for d in range(2):
                tri = const("tri_f" if d == 0 else "tri_b").unsqueeze(1).to_broadcast([P, RH, P])
                dve_step(dve, dve.tensor_tensor(tmp[:, 4 * d:4 * d + 4, :], tmp[:, 4 * d:4 * d + 4, :], tri, ALU.mult))
            dve.tensor_tensor(decay[:, :, :], tmp[:, 0:4, :], tmp[:, 4:8, :], ALU.add).then_inc(decay_done, 1)
            dve.wait_ge(decay_done, 1)

        def ret_project(l, q_tiles):
            a0, b0 = span[f"ret{l}"]
            ktok, qT, kT, o, qtok, v = ret_tensors()
            tmp = at("rope_tmp", [P, 4, 256], F32, work + 28672)
            out, turned, turned_out = stage_sem("out"), stage_sem("turned"), stage_sem("turned_out")
            lg_dve, lg_act, exps_done, decay_done = (stage_sem(n) for n in ("lg_dve", "lg_act", "exps_done", "decay_done"))
            blocks = [q_tiles, ALL_TILES, ALL_TILES, ALL_TILES]
            done = np.cumsum([len(b) for b in blocks]).tolist()
            banks = [[4 * (n % 2) + j for j in range(len(b))] for n, b in enumerate(blocks)]
            with nc.Block() as block:
                @block.sync
                def _(sp):
                    loads(sp, f"ret{l}")

                @block.gpsimd
                def _(pool):
                    splits_lo(pool, f"ret{l}")

                @block.scalar
                def _(act):
                    split_hi(act, a0 + 1)
                    decays_act(act, lg_dve, lg_act, exps_done)
                    for n in range(4):
                        for u in range(2):
                            split_hi(act, a0 + 2 * n + u + 2)
                        if n >= 2:
                            act.wait_ge(unit_used, a0 + 2 * n + 2)
                            act.wait_ge(out, done[n - 1])
                            for j, tile in enumerate(blocks[n]):
                                act.activation(v[:, tile, (n - 2) * 512:(n - 1) * 512], ps[banks[n][j]][:, :],
                                               ACT.Copy).then_inc(out, 1)
                    for i in range(2 * RH):
                        act.wait_ge(turned, i + 1)
                        dst, h = (qT, i) if i < RH else (kT, i - RH)
                        lo = q_tiles[0] * P if i < RH else 0
                        act.activation(dst[:, h, lo:TOK], ps[i][:, 0:TOK - lo], ACT.Copy).then_inc(turned_out, 1)

                @block.vector
                def _(dve):
                    decays_dve(dve, l, lg_dve, lg_act, exps_done, decay_done)
                    for n, (dst, table) in enumerate(((qtok, "rq"), (ktok, "rk"))):
                        dve.wait_ge(unit_used, a0 + 2 * n + 2)
                        for j, tile in enumerate(blocks[n]):
                            src = ps[banks[n][j]][:, :]
                            if tile < 2:
                                scale = 1.0 if n == 0 else DK ** -0.5
                                dve.tensor_scalar(dst[:, tile, :], src, scale, None, ALU.mult).then_inc(out, 1)
                            else:
                                rope(dve, dst[:, tile, :], src, tile, table, RH, tmp, False).then_inc(out, 1)
                                dve.wait_ge(out, (done[n - 1] if n else 0) + j + 1)

                @block.tensor
                def _(pe):
                    for n in range(4):
                        if n >= 2:
                            pe.wait_ge(out, done[n - 2])
                        project(pe, a0 + 2 * n, banks[n], blocks[n])
                    pe.wait_ge(out, done[3])
                    for i in range(2 * RH):
                        src, h, tiles = (qtok, i, q_tiles) if i < RH else (ktok, i - RH, ALL_TILES)
                        for j, tile in enumerate(tiles):
                            last = pe.transpose(ps[i][:, j * P:(j + 1) * P], src[:, tile, h * DK:(h + 1) * DK], ident)
                        last.then_inc(turned, 1)
            end_stage()

        def ret_mix(l, tiles):
            ktok, qT, kT, o, qtok, v = ret_tensors()
            base = outT_at + 16384
            decay, wts, gam = ret_decays()[:3]
            state = at("ret_state", [P, 2, RH, DV], F32, base + 2048)
            kw = at("k_weighted", [P, RH * DK], F32, base + 10240)
            part = at("ret_part", [P, 2, 512], F32, base + 12288)
            mix = at("ret_mix", [P, 2, RH * P], F32, work + 40960)
            names = ("scores", "mixed", "intra", "intra_out",
                     "weighted", "update", "update_out", "inter", "inter_out")
            (scores, mixed, intra, intra_out,
             weighted, update, update_out, inter, inter_out) = (stage_sem(s) for s in names)
            n = len(tiles)
            steps = [(s, d) for s in range(NT) for d in range(2)]

            def w_of(kind, d):
                return wts[:, kind * 8 + d * 4:kind * 8 + d * 4 + 4]

            with nc.Block() as block:
                @block.scalar
                def _(act):
                    for j, tile in enumerate(tiles):
                        for b in range(2):
                            act.wait_ge(intra, 2 * j + b + 1)
                            act.activation(o[:, tile, b * 512:(b + 1) * 512], ps[2 + b][:, :], ACT.Copy).then_inc(intra_out, 1)

                @block.vector
                def _(dve):
                    for j, tile in enumerate(tiles):
                        dve.wait_ge(scores, j + 1)
                        dve.tensor_tensor(mix[:, j % 2, :], ps[j % 2][:, :], decay[:, :, :].rearrange("p h i -> p (h i)"),
                                          ALU.mult).then_inc(mixed, 1)
                    n_in = n_up = 0
                    for s, d in steps:
                        tile = ORDER[d][s]
                        if s < NT - 1:
                            if n_up:
                                dve.wait_ge(update, n_up)
                            dve.tensor_tensor(kw[:, :].rearrange("p (h e) -> p h e", h=RH),
                                              ktok[:, tile, :].rearrange("p (h e) -> p h e", h=RH),
                                              spread(w_of(d, d), RH, DK), ALU.mult).then_inc(weighted, 1)
                        if s > 0 and tile in tiles:
                            if n_in == 0:
                                dve.wait_ge(intra_out, 2 * n)
                            for b in range(2):
                                dve.wait_ge(inter, n_in + 1)
                                pt = part[:, b, :]
                                dve_step(dve, dve.tensor_tensor(pt.rearrange("p (h e) -> p h e", h=2),
                                                                ps[4 + b][:, :].rearrange("p (h e) -> p h e", h=2),
                                                                spread(w_of(2 + d, d)[:, 2 * b:2 * b + 2], 2, DV), ALU.mult))
                                oo = o[:, tile, b * 512:(b + 1) * 512]
                                dve.tensor_tensor(oo, oo, pt, ALU.add).then_inc(inter_out, 1)
                                n_in += 1
                        if s < NT - 1:
                            dve.wait_ge(update, n_up + 1)
                            for h in range(RH):
                                st = state[:, d, h, :]
                                u = ps[6 + h // 2][:, (h % 2) * DV:(h % 2 + 1) * DV]
                                if s:
                                    ins = dve.scalar_tensor_tensor(st, st, gam[:, 4 * d + h:4 * d + h + 1], u, ALU.mult, ALU.add)
                                else:
                                    ins = dve.tensor_copy(st, u)
                            ins.then_inc(update_out, 1)
                            n_up += 1

                @block.tensor
                def _(pe):
                    for j in range(n + 1):
                        if j < n:
                            tok = slice(tiles[j] * P, (tiles[j] + 1) * P)
                            if j >= 2:
                                pe.wait_ge(mixed, j - 1)
                            for h in range(RH):
                                last = pe.matmul(ps[j % 2][:, h * P:(h + 1) * P], kT[:, h, tok], qT[:, h, tok], start=True, stop=True)
                            last.then_inc(scores, 1)
                        if j >= 1:
                            tile = tiles[j - 1]
                            pe.wait_ge(mixed, j)
                            for b in range(2):
                                if j >= 2:
                                    pe.wait_ge(intra_out, 2 * (j - 2) + b + 1)
                                for h in (2 * b, 2 * b + 1):
                                    last = pe.matmul(ps[2 + b][:, (h % 2) * DV:(h % 2 + 1) * DV],
                                                     mix[:, (j - 1) % 2, h * P:(h + 1) * P],
                                                     v[:, tile, h * DV:(h + 1) * DV], start=True, stop=True)
                                last.then_inc(intra, 1)
                    n_in = n_up = 0
                    for s, d in steps:
                        tile = ORDER[d][s]
                        if s > 0 and tile in tiles:
                            pe.wait_ge(update_out, 2 * (s - 1) + d + 1)
                            for b in range(2):
                                if n_in >= 2:
                                    pe.wait_ge(inter_out, n_in - 1)
                                for h in (2 * b, 2 * b + 1):
                                    last = pe.matmul(ps[4 + b][:, (h % 2) * DV:(h % 2 + 1) * DV],
                                                     qT[:, h, tile * P:(tile + 1) * P], state[:, d, h, :], start=True, stop=True)
                                last.then_inc(inter, 1)
                                n_in += 1
                        if s < NT - 1:
                            pe.wait_ge(weighted, n_up + 1)
                            if n_up:
                                pe.wait_ge(update_out, n_up)
                            for h in range(RH):
                                last = pe.matmul(ps[6 + h // 2][:, (h % 2) * DV:(h % 2 + 1) * DV],
                                                 kw[:, h * DK:(h + 1) * DK], v[:, tile, h * DV:(h + 1) * DV], start=True, stop=True)
                            last.then_inc(update, 1)
                            n_up += 1
            end_stage()

        def ret_gate(l, tiles):
            a0, b0 = span[f"g{l}"]
            o = ret_tensors()[3]
            gate = at("ret_silu", [P, NT, 512], F32, work)
            junk = at("ret_junk", [P, DV], F32, work + 8192)
            squared, roots, silu_out, gated, turned, hi_out, parts = (
                stage_sem(s) for s in ("squared", "roots", "silu_out", "gated", "turned", "hi_out", "parts"))
            ssq = small[:, 0:16]
            n, lo = len(tiles), 4 * tiles[0]
            with nc.Block() as block:
                @block.sync
                def _(sp):
                    loads(sp, f"g{l}")

                @block.gpsimd
                def _(pool):
                    splits_lo(pool, f"g{l}")

                @block.scalar
                def _(act):
                    split_hi(act, a0 + 1)
                    for tile in tiles:
                        for h in range(RH):
                            ins = act.activation(junk[:, :], o[:, tile, h * DV:(h + 1) * DV], ACT.Square,
                                                 accum_out=ssq[:, 4 * tile + h:4 * tile + h + 1])
                            act_step(act, ins)
                    act.activation(small[:, 16:17], small[:, lo:lo + 1], ACT.Copy).then_inc(squared, 1)
                    act.wait_ge(roots, 1)
                    act.activation(ssq[:, lo:16], ssq[:, lo:16], ACT.Sqrt).then_inc(roots, 1)
                    for b in range(2):
                        for u in range(2):
                            split_hi(act, a0 + 2 * b + u + 2)
                        act.wait_ge(unit_used, a0 + 2 * b + 2)
                        if b:
                            act.wait_ge(gated, n)
                        for j in range(n):
                            act.activation(gate[:, j, :], ps[4 * b + j][:, :], ACT.Silu).then_inc(silu_out, 1)
                    for u in range(2):
                        split_hi(act, a0 + 4 + u + 2)
                    for f in range(KD):
                        outT_hi(act, tiles, f, turned, hi_out, banks=LATE_BANKS)

                @block.vector
                def _(dve):
                    dve.wait_ge(squared, 1)
                    dve.tensor_scalar(ssq[:, lo:16], ssq[:, lo:16], 1.0 / DV, EPS, ALU.mult, ALU.add).then_inc(roots, 1)
                    dve.wait_ge(roots, 2)
                    dve_step(dve, dve.reciprocal(ssq[:, lo:16], ssq[:, lo:16]))
                    for b in range(2):
                        for j, tile in enumerate(tiles):
                            dve.wait_ge(silu_out, n * b + j + 1)
                            for h in range(2):
                                hh = 2 * b + h
                                oo = o[:, tile, hh * DV:(hh + 1) * DV]
                                ins = dve.scalar_tensor_tensor(oo, oo, ssq[:, 4 * tile + hh:4 * tile + hh + 1],
                                                               gate[:, j, h * DV:(h + 1) * DV], ALU.mult, ALU.mult)
                            ins.then_inc(gated, 1)
                    for f in range(KD):
                        outT_lo(dve, tiles, f, hi_out, parts, banks=LATE_BANKS)

                @block.tensor
                def _(pe):
                    for b in range(2):
                        project(pe, a0 + 2 * b, [4 * b + j for j in range(n)], tiles)
                    pe.wait_ge(silu_out, n)
                    project(pe, a0 + 4, range(n), tiles)
                    pe.wait_ge(silu_out, 2 * n)
                    turn_to_outT(pe, o, tiles, range(KD), lambda f: (gated, n * (f // 4 + 1)), turned, parts, LATE_BANKS)
            end_stage()

        def att_tensors():
            qT = at("att_qT", [P, AH, TOK], F32, work)
            kT = at("att_kT", [P, KVH, TOK], F32, work + 16384)
            v = at("att_v", [P, NT, KVH * AD], F32, work + 20480)
            tok = at("att_tok", [P, NT, 512], F32, work + 24576)
            return qT, kT, v, tok

        def att_project(l, q_tiles):
            a0, b0 = span[f"att{l}"]
            qT, kT, v, tok = att_tensors()
            tmp = at("att_rope_tmp", [P, 4, 256], F32, work + 32768)
            out, turned, turned_out = stage_sem("out"), stage_sem("turned"), stage_sem("turned_out")
            blocks = [q_tiles, q_tiles, ALL_TILES]
            heads_of = [4, 4, 2]
            done = np.cumsum([len(b) for b in blocks]).tolist()
            turns = [0, 4, 8, 10]
            bank0 = [0, 4, 0]
            with nc.Block() as block:
                @block.sync
                def _(sp):
                    loads(sp, f"att{l}")

                @block.gpsimd
                def _(pool):
                    splits_lo(pool, f"att{l}")

                @block.scalar
                def _(act):
                    split_hi(act, a0 + 1)
                    for n in range(3):
                        for u in range(2):
                            split_hi(act, a0 + 2 * n + u + 2)
                        for i in range(turns[n], turns[n + 1]):
                            m = i - turns[n]
                            act.wait_ge(turned, i + 1)
                            dst = qT[:, i, :] if n < 2 else kT[:, m, :]
                            lo = q_tiles[0] * P if n < 2 else 0
                            act.activation(dst[:, lo:TOK], ps[bank0[n] + m][:, 0:TOK - lo], ACT.Copy).then_inc(turned_out, 1)

                @block.vector
                def _(dve):
                    for n in range(3):
                        w = heads_of[n] * AD
                        dve.wait_ge(unit_used, a0 + 2 * n + 2)
                        if n:
                            dve.wait_ge(turned, turns[n])
                        for j, tile in enumerate(blocks[n]):
                            src = ps[bank0[n] + j]
                            if n == 2:
                                dve.tensor_copy(v[:, tile, :], src[:, 256:512])
                            if tile < 2:
                                dve.tensor_scalar(tok[:, tile, 0:w], src[:, 0:w], AD ** -0.5 if n < 2 else 1.0, None,
                                                  ALU.mult).then_inc(out, 1)
                            else:
                                rope(dve, tok[:, tile, 0:w], src[:, 0:w], tile, "aq" if n < 2 else "ak", heads_of[n],
                                     tmp, True).then_inc(out, 1)
                                dve.wait_ge(out, (done[n - 1] if n else 0) + j + 1)

                @block.tensor
                def _(pe):
                    def turn(n):
                        pe.wait_ge(out, done[n])
                        for i in range(turns[n], turns[n + 1]):
                            m = i - turns[n]
                            for j, tile in enumerate(blocks[n]):
                                last = pe.transpose(ps[bank0[n] + m][:, j * P:(j + 1) * P], tok[:, tile, m * AD:(m + 1) * AD], ident)
                            last.then_inc(turned, 1)

                    for n in range(3):
                        if n == 2:
                            pe.wait_ge(turned_out, turns[1])
                        for u in range(2):
                            project_half(pe, a0 + 2 * n, u, [bank0[n] + j for j in range(len(blocks[n]))], blocks[n])
                            if n and u == 0:
                                turn(n - 1)
                    turn(2)
            end_stage()

        def att_mix(l, tiles):
            qT, kT, v, tok = att_tensors()
            pr = at("att_probs", [P, 2, AG, 512], F32, work + 24576)
            pT = at("att_probs_T", [P, NT, AG * P], F32, work + 40960)
            scores, maxed, exp_done, summed, normed, turned, turned_out, summed_v, hi_out, parts = (
                stage_sem(s) for s in ("scores", "maxed", "exp_done", "summed", "normed", "turned", "turned_out", "summed_v", "hi_out", "parts"))
            sink = heads[l][:, 104:112]
            jobs = [(tile, kv) for tile in tiles for kv in range(KVH)]

            def sc(i, job):
                a = 32 + 16 * (job % 2) + 4 * i
                return small[:, a:a + 4]

            def keys(tile):
                return 2 if tile < 2 else NT

            with nc.Block() as block:
                @block.scalar
                def _(act):
                    def exponentials(n):
                        w = keys(jobs[n][0]) * P
                        act.wait_ge(maxed, n + 1)
                        for h in range(AG):
                            act.activation(pr[:, n % 2, h, 0:w], ps[h][:, 0:w], ACT.Exp, bias=sc(0, n)[:, h:h + 1],
                                           accum_out=sc(2, n)[:, h:h + 1]).then_inc(exp_done, 1)
                        act.activation(sc(1, n), sc(1, n), ACT.Exp).then_inc(summed, 1)

                    exponentials(0)
                    n_turn = 0
                    for n, (tile, kv) in enumerate(jobs):
                        for k in range(keys(tile)):
                            act.wait_ge(turned, n_turn + 1)
                            act.activation(pT[:, k, :], ps[4 + k % 2][:, :], ACT.Copy).then_inc(turned_out, 1)
                            n_turn += 1
                        if n + 1 < len(jobs):
                            exponentials(n + 1)
                        act.wait_ge(summed_v, n + 1)
                        act.activation(outT[0][:, 4 * kv:4 * kv + 4, tile * P:(tile + 1) * P],
                                       ps[6 + n % 2][:, :].rearrange("p (h t) -> p h t", h=AG), ACT.Copy).then_inc(hi_out, 1)

                @block.vector
                def _(dve):
                    def maxima(n):
                        tile, kv = jobs[n]
                        w = keys(tile) * P
                        dve.wait_ge(scores, n + 1)
                        if tile >= 2:
                            other = 5 - tile
                            for h in range(AG):
                                s = ps[h][:, other * P:(other + 1) * P]
                                ins = dve.tensor_tensor(s, s, const("neg_up" if tile == 2 else "neg_low"), ALU.add)
                            dve_step(dve, ins)
                        mx = sc(0, n)
                        for h in range(AG):
                            ins = dve.tensor_reduce(mx[:, h:h + 1], ps[h][:, 0:w], AX.X, ALU.max)
                        dve_step(dve, ins)
                        sk = sink[:, 4 * kv:4 * kv + 4]
                        dve_step(dve, dve.tensor_tensor(mx, mx, sk, ALU.max))
                        dve_step(dve, dve.tensor_tensor(sc(1, n), sk, mx, ALU.subtract))
                        dve.tensor_scalar(mx, mx, -1.0, None, ALU.mult).then_inc(maxed, 1)

                    def normalize(n):
                        w = keys(jobs[n][0]) * P
                        dve.wait_ge(summed, n + 1)
                        dve_step(dve, dve.tensor_tensor(sc(2, n), sc(2, n), sc(1, n), ALU.add))
                        dve_step(dve, dve.reciprocal(sc(2, n), sc(2, n)))
                        for h in range(AG):
                            ins = dve.tensor_scalar(pr[:, n % 2, h, 0:w], pr[:, n % 2, h, 0:w], sc(2, n)[:, h:h + 1], None, ALU.mult)
                        ins.then_inc(normed, 1)

                    def tail(n):
                        tile, kv = jobs[n]
                        dve.wait_ge(hi_out, n + 1)
                        s = slice(tile * P, (tile + 1) * P)
                        dve.tensor_tensor(outT[1][:, 4 * kv:4 * kv + 4, s], ps[6 + n % 2][:, :].rearrange("p (h t) -> p h t", h=AG),
                                          outT[0][:, 4 * kv:4 * kv + 4, s].bitcast(F32), ALU.subtract).then_inc(parts, 1)

                    maxima(0)
                    normalize(0)
                    for n in range(len(jobs)):
                        if n + 1 < len(jobs):
                            maxima(n + 1)
                        if n:
                            tail(n - 1)
                        if n + 1 < len(jobs):
                            normalize(n + 1)
                    tail(len(jobs) - 1)

                @block.tensor
                def _(pe):
                    def score(n):
                        tile, kv = jobs[n]
                        w = keys(tile) * P
                        for h in range(AG):
                            if n:
                                pe.wait_ge(exp_done, AG * (n - 1) + h + 1)
                            last = pe.matmul(ps[h][:, 0:w], qT[:, AG * kv + h, tile * P:(tile + 1) * P],
                                             kT[:, kv, 0:w], start=True, stop=True)
                        last.then_inc(scores, 1)

                    score(0)
                    n_turn = 0
                    for n, (tile, kv) in enumerate(jobs):
                        nk = keys(tile)
                        if n + 1 < len(jobs):
                            score(n + 1)
                        pe.wait_ge(normed, n + 1)
                        for k in range(nk):
                            if n_turn >= 2:
                                pe.wait_ge(turned_out, n_turn - 1)
                            for h in range(AG):
                                last = pe.transpose(ps[4 + k % 2][:, h * P:(h + 1) * P], pr[:, n % 2, h, k * P:(k + 1) * P], ident)
                            last.then_inc(turned, 1)
                            n_turn += 1
                        if n >= 2:
                            pe.wait_ge(parts, n - 1)
                        pe.wait_ge(turned_out, n_turn)
                        for k in range(nk):
                            last = pe.matmul(ps[6 + n % 2][:, :], v[:, k, kv * AD:(kv + 1) * AD], pT[:, k, :],
                                             start=k == 0, stop=k == nk - 1)
                        last.then_inc(summed_v, 1)
            end_stage()

        def post_rows_pe(pe, l, which, conds, rows_sum, rows_out, banks):
            for i, c in enumerate(conds):
                for half in range(2):
                    m = 2 * i + half
                    if m >= len(banks):
                        pe.wait_ge(rows_out, m - len(banks) + 1)
                    for d in range(4):
                        w = gains[l][:, 2 + which, 4 * half + d, c:c + 1].to_broadcast([P, P])
                        last = pe.matmul(ps[banks[m % len(banks)]][:, d * P:(d + 1) * P], w, ident, start=True, stop=True)
                    last.then_inc(rows_sum, 1)

        def post_rows_act(act, rows, conds, rows_sum, rows_out, banks):
            for i, c in enumerate(conds):
                for half in range(2):
                    m = 2 * i + half
                    act.wait_ge(rows_sum, m + 1)
                    act.activation(rows[:, c, half * 512:(half + 1) * 512], ps[banks[m % len(banks)]][:, :],
                                   ACT.Copy).then_inc(rows_out, 1)

        post_sq, x_sq = small[:, 0:8], small[:, 8:12]

        def post_norm_act(act, yb, tiles, junk, y_out, squared, means, roots, x_out=None, x_squared=None, early=None):
            n = len(tiles)
            for b in {None: (0, 1), True: (0,), False: (1,)}[early]:
                for j in range(n + 1):
                    if j < n:
                        tile, m = tiles[j], n * b + j
                        act.wait_ge(y_out, m + 1)
                        if m >= 2:
                            act.wait_ge(squared, m - 1)
                        act.activation(junk[:, m % 2, :], yb[:, tile, b * 512:(b + 1) * 512], ACT.Square,
                                       accum_out=post_sq[:, 2 * tile + b:2 * tile + b + 1]).then_inc(squared, 1)
                    if b and j:
                        s = 2 * tiles[j - 1]
                        act.wait_ge(means, j)
                        act.activation(post_sq[:, s:s + 1], post_sq[:, s:s + 1], ACT.Sqrt).then_inc(roots, 1)
            if x_out is not None and not early:
                act.wait_ge(squared, 2 * n)
                for j, tile in enumerate(tiles):
                    act.wait_ge(x_out, j + 1)
                    if j:
                        act.wait_ge(x_squared, j)
                    act.activation(junk[:, :, :].rearrange("p a b -> p (a b)"), xres[:, tile, :], ACT.Square,
                                   accum_out=x_sq[:, tile:tile + 1]).then_inc(x_squared, 1)

        def post_norm_pool(pool, yb, tiles, scaled, x_out):
            for j, tile in enumerate(tiles):
                pool.wait_ge(scaled, j + 1)
                pool.tensor_tensor(xres[:, tile, :], xres[:, tile, :], yb[:, tile, :], ALU.add).then_inc(x_out, 1)

        def post_norm_dve(dve, yb, rows, tiles, squared, means, roots, rows_out, n_rows, scaled):
            n = len(tiles)
            dve.wait_ge(rows_out, n_rows)
            for j in range(n + 1):
                if j < n:
                    s = 2 * tiles[j]
                    dve.wait_ge(squared, n + j + 1)
                    dve_step(dve, dve.tensor_scalar(post_sq[:, s:s + 1], post_sq[:, s:s + 1], post_sq[:, s + 1:s + 2], 1.0 / D,
                                                    ALU.add, ALU.mult))
                    dve.tensor_scalar(post_sq[:, s:s + 1], post_sq[:, s:s + 1], EPS, None, ALU.add).then_inc(means, 1)
                if j:
                    tile = tiles[j - 1]
                    r = post_sq[:, 2 * tile:2 * tile + 1]
                    dve.wait_ge(roots, j)
                    dve_step(dve, dve.reciprocal(r, r))
                    yt = yb[:, tile, :]
                    dve.scalar_tensor_tensor(yt, yt, r, rows[:, 1 if tile < 2 else 0, :], ALU.mult, ALU.mult).then_inc(scaled, 1)

        def out_project(l, tiles):
            a0, b0 = span[f"out{l}"]
            yb = at("y_out", [P, NT, D], F32, work)
            rows = at("post_rows", [P, 2, D], F32, work + 16384)
            junk = at("post_junk", [P, 2, 512], F32, work + 24576)
            conds = [1, 0] if len(tiles) == NT else [0]
            n = len(tiles)
            names = ("rows_sum", "rows_out", "turned", "hi_out", "parts", "y_out", "squared", "means", "roots", "x_out", "x_squared", "scaled")
            (rows_sum, rows_out, turned, hi_out, parts, y_out, squared, means, roots, x_out, x_squared, scaled) = (
                stage_sem(s) for s in names)
            with nc.Block() as block:
                @block.sync
                def _(sp):
                    loads(sp, f"out{l}")

                @block.gpsimd
                def _(pool):
                    splits_lo(pool, f"out{l}")
                    post_norm_pool(pool, yb, tiles, scaled, x_out)

                @block.scalar
                def _(act):
                    split_hi(act, a0 + 1)
                    post_rows_act(act, rows, conds, rows_sum, rows_out, [0, 1, 2, 3])
                    for f in range(KD):
                        outT_hi(act, tiles, f, turned, hi_out)
                    for g in range(a0 + 2, b0):
                        split_hi(act, g)
                    post_norm_act(act, yb, tiles, junk, y_out, squared, means, roots, x_out, x_squared, early=True)
                    split_hi(act, b0)
                    post_norm_act(act, yb, tiles, junk, y_out, squared, means, roots, x_out, x_squared, early=False)

                @block.vector
                def _(dve):
                    for f in range(KD):
                        outT_lo(dve, tiles, f, hi_out, parts)
                    for b in range(2):
                        dve.wait_ge(unit_used, a0 + 2 * b + 2)
                        for j, tile in enumerate(tiles):
                            dve.tensor_copy(yb[:, tile, b * 512:(b + 1) * 512], ps[4 * b + j][:, :]).then_inc(y_out, 1)
                    post_norm_dve(dve, yb, rows, tiles, squared, means, roots, rows_out, 2 * len(conds), scaled)

                @block.tensor
                def _(pe):
                    post_rows_pe(pe, l, 0, conds, rows_sum, rows_out, [0, 1, 2, 3])
                    pe.wait_ge(rows_out, 2 * len(conds))
                    turn_to_outT(pe, merged, tiles, range(KD), None, turned, parts)
                    pe.wait_ge(parts, KD)
                    for b in range(2):
                        project(pe, a0 + 2 * b, [4 * b + j for j in range(n)], tiles, outT)
            end_stage()

        def ffn_tensors():
            gT = [at(f"ffn_gT_{n}", [P, FT, TOK], F32R, outT_at + i * FT * TOK * 4) for i, n in enumerate(("hi", "lo"))]
            return gT, outT_at + 2 * FT * TOK * 4

        def ffn_up():
            a0, b0 = span["ffn_up"]
            gT, free = ffn_tensors()
            silu = at("ffn_silu", [P, 2, TOK], F32, free)
            prod = at("ffn_prod", [P, 2, TOK], F32, free + 4096)
            rounds = FF // 256
            silu_out, g_done, chain = stage_sem("silu_out"), stage_sem("g_done"), stage_sem("chain")
            w1, w3, w2 = (t[f"ffn_w{i}"][0].rearrange("(k p) n -> p k n", p=P) for i in (1, 3, 2))

            def flat(buf, g, half):
                return buf[:, g % 2, half * 1024:(half + 1) * 1024]

            with nc.Block() as block:
                @block.sync
                def _(sp):
                    stage_units_end[0] = b0
                    load_unit(sp, a0 + 3)
                    with sp.Fori(0, rounds - 2) as i:
                        for u, w in enumerate((w1, w3)):
                            g = a0 + 4 + u
                            for half in range(2):
                                sp.wait_ge(lo_ready, 4 * i + 2 * (g - 2) + half + 1)
                                src = half_of(w, half)[:, :, bass.ds((i + 2) * 256, 256)]
                                sp.dma_start(half_of(view(raw, g), half), src).then_inc(raw_loaded[g % 2][half], 16)
                    for g in range(b0, b0 + 3):
                        load_unit(sp, g)

                @block.gpsimd
                def _(pool):
                    with pool.Fori(0, rounds) as i:
                        for g in (a0 + 1, a0 + 2):
                            for half in range(2):
                                pool.wait_ge(hi_ready, 4 * i + 2 * g + half + 1)
                                pool.tensor_tensor(flat(wlo, g, half), flat(raw, g, half), flat(whi, g, half).bitcast(F32),
                                                   ALU.subtract).then_inc(lo_ready, 1)

                @block.scalar
                def _(act):
                    act.sem_inc(silu_out, 2)
                    with act.Fori(0, rounds) as i:
                        for u in range(2):
                            g = a0 + 1 + u
                            for half in range(2):
                                act.wait_ge(raw_loaded[g % 2][half], 16 * (g // 2 + 1) + 16 * i)
                                if half == 0:
                                    act.wait_ge(unit_used, 2 * i + g - 1)
                                act.activation(flat(whi, g, half), flat(raw, g, half), ACT.Copy).then_inc(hi_ready, 1)
                            if u == 1:
                                for j in range(2):
                                    act.wait_ge(g_done, 2 * i + j + 1)
                                    act.activation(silu[:, j, :], ps[j][:, :], ACT.Silu).then_inc(silu_out, 1)

                @block.vector
                def _(dve):
                    dve.sem_inc(g_done, 2)
                    with dve.Fori(0, rounds) as i:
                        dve.wait_ge(unit_used, 2 * i + a0 + 2)
                        for j in range(2):
                            dve.wait_ge(silu_out, 2 * i + j + 3)
                            dve.tensor_tensor(prod[:, j, :], silu[:, j, :], ps[2 + j][:, :], ALU.mult).then_inc(chain, 1)
                            dve.wait_ge(chain, 4 * i + 2 * j + 1)
                            hi, lo = (g[:, bass.ds(2 * i + j, 1), :].rearrange("p a t -> p (a t)") for g in gT)
                            dve.tensor_copy(hi, prod[:, j, :]).then_inc(chain, 1)
                            dve.wait_ge(chain, 4 * i + 2 * j + 2)
                            dve.tensor_tensor(lo, prod[:, j, :], hi.bitcast(F32), ALU.subtract).then_inc(g_done, 1)

                @block.tensor
                def _(pe):
                    with pe.Fori(0, rounds) as i:
                        for u in range(2):
                            g = a0 + u
                            pe.wait_ge(lo_ready, 4 * i + 2 * (g + 1))
                            pe.wait_ge(silu_out if u == 0 else g_done, 2 * i + 2)
                            wh, wl = view(whi, g), view(wlo, g)
                            for j in range(2):
                                for k in range(KD):
                                    a = [wh[:, k, j * P:(j + 1) * P], wl[:, k, j * P:(j + 1) * P]]
                                    last = three(pe, ps[2 * u + j][:, :], a, [h[:, k, :] for h in hT], k == 0, k == KD - 1)
                            last.then_inc(unit_used, 1)
            end_stage()

        def ffn_down(l):
            a0, b0 = span["ffn_down"]
            gT, free = ffn_tensors()
            yb = at("ffn_y", [P, NT, D], F32, hT_at)
            rows = at("ffn_rows", [P, 2, D], F32, hT_at + 16384)
            junk = at("ffn_junk", [P, 2, 512], F32, hT_at + 24576)
            scaled, rows_sum, rows_out, y_out, squared, means, roots, x_out, x_squared = (
                stage_sem(s) for s in ("scaled", "rows_sum", "rows_out", "y_out", "squared", "means", "roots", "x_out", "x_squared"))
            with nc.Block() as block:
                @block.sync
                def _(sp):
                    loads(sp, "ffn_down")

                @block.gpsimd
                def _(pool):
                    splits_lo(pool, "ffn_down")
                    post_norm_pool(pool, yb, ALL_TILES, scaled, x_out)

                @block.scalar
                def _(act):
                    split_hi(act, a0 + 1)
                    post_rows_act(act, rows, [1, 0], rows_sum, rows_out, [0, 1, 2, 3])
                    for g in range(a0 + 2, b0 + 2):
                        split_hi(act, g)
                    post_norm_act(act, yb, ALL_TILES, junk, y_out, squared, means, roots, x_out, x_squared)

                @block.vector
                def _(dve):
                    dve.wait_ge(unit_used, b0)
                    for b in range(2):
                        for tile in ALL_TILES:
                            dve.tensor_copy(yb[:, tile, b * 512:(b + 1) * 512], ps[2 * tile + b][:, :]).then_inc(y_out, 1)
                    post_norm_dve(dve, yb, rows, ALL_TILES, squared, means, roots, rows_out, 4, scaled)

                @block.tensor
                def _(pe):
                    post_rows_pe(pe, l, 1, [1, 0], rows_sum, rows_out, [0, 1, 2, 3])
                    pe.wait_ge(rows_out, 4)
                    for g in range(a0, b0):
                        pe.wait_ge(lo_ready, 2 * (g + 1))
                        wh, wl = view(whi, g), view(wlo, g)
                        for k in range(2):
                            kk = 2 * (g - a0) + k
                            for tile in ALL_TILES:
                                a = [x[:, kk, tile * P:(tile + 1) * P] for x in gT]
                                for b in range(2):
                                    s = slice(b * 512, (b + 1) * 512)
                                    last = three(pe, ps[2 * tile + b][:, :], a, [wh[:, k, s], wl[:, k, s]],
                                                 kk == 0, kk == FT - 1)
                        last.then_inc(unit_used, 1)
            end_stage()

        R0 = ring_at
        RAW_RING, RING, AHEAD = 6, 3, 2
        moe_raw = at("moe_raw", [P, RAW_RING, 2048], F32, R0)
        moe_hi = at("moe_unit_hi", [P, RING, 2048], F32R, R0 + RAW_RING * 8192)
        moe_lo = at("moe_unit_lo", [P, RING, 2048], F32R, R0 + (RAW_RING + RING) * 8192)
        M0 = R0 + (RAW_RING + 2 * RING) * 8192
        htok = [at(f"moe_h_{n}", [P, 2, D], F32R, M0 + 8192 * i) for i, n in enumerate(("hi", "lo"))]
        route = at("moe_route", [P, 3, 2, 2 * NE + 1], F32, M0 + 16384)
        n_pass = at("moe_passes", [P, 1], mybir.dt.int32, M0 + 16384 + 448)
        slot_of, chosen, weight = route[:, 0, :, :], route[:, 1, :, :], route[:, 2, :, :]

        w1, w3 = (t[f"moe_w{i}"][0].rearrange("e (k p) n -> p e k n", p=P) for i in (1, 3))
        w2 = t["moe_w2"][0].rearrange("e (k p) n -> p e k n", p=P)
        NB = 6
        plan = []
        for _b in range(NB - 1):
            plan += [(w, 4 * half, 4, _b * 512, 512) for w in (w1, w3) for half in range(2)]
        plan += [(w, 0, KD, (NB - 1) * 512, 256) for w in (w1, w3)]
        up = len(plan)
        plan += [(w2, 2 * j, 2, 0, D) for j in range(FT // 2)]
        U = len(plan)
        assert U % RING == 0 and 2 * U % RAW_RING == 0
        raw_m = [sem(f"moe_raw_loaded{i}") for i in range(RAW_RING)]

        def unit_part(buf, slot, v):
            _, _, a, _, b = plan[v % U]
            return buf[:, slot, 0:a * b].rearrange("p (a b) -> p a b", b=b)

        def load_moe(sp, expert, x, v):
            w, k, a, c, b = plan[v % U]
            slot = (U * x + v) % RAW_RING
            src = w[:, bass.ds(expert, 1), k:k + a, c:c + b].rearrange("p e k n -> p (e k) n")
            sp.dma_start(unit_part(moe_raw, slot, v), src).then_inc(raw_m[slot], 16)

        def moe_route(l):
            rows = at("moe_rows", [P, 2, D], F32, work)
            xn = at("moe_xn", [P, 2, D], F32, work + 8192)
            wr = at("router", [P, KD, NE], F32, work + 16384)
            wr2 = [at(f"router_{n}", [P, KD, NE], F32R, work + 16640 + 256 * i) for i, n in enumerate(("hi", "lo"))]
            lg = at("logits", [P, 2, NE], F32, work + 17152)
            cmp = at("compare", [P, 2, 2, NE * NE], F32, work + 17280)
            sc = at("route_scratch", [P, 64], F32, work + 18304)
            names = ("router_in", "roots", "rows_sum", "rows_out", "h_done", "turned", "hi_out", "parts",
                     "logits_sum", "logits_out", "exps", "sel_done", "counted")
            (router_in, roots, rows_sum, rows_out, h_done, turned, hi_out, parts,
             logits_sum, logits_out, exps, sel_done, counted) = (stage_sem(s) for s in names)
            ssq = x_sq[:, 2:4]
            negm, ssum, most = sc[:, 0:2], sc[:, 2:4], sc[:, 4:5]
            ex = sc[:, 16:32].rearrange("p (j e) -> p j e", j=2)
            sel = sc[:, 32:48].rearrange("p (j e) -> p j e", j=2)
            gain, shift = gains[l][:, 1, :, 0:1], mods[l][:, 24:32, 0:1]
            with nc.Block() as block:
                @block.sync
                def _(sp):
                    sp.dma_start(wr[:, :, :], t["moe_router"][0].rearrange("(k p) n -> p k n", p=P)).then_inc(router_in, 16)
                    for v in range(RAW_RING):
                        load_moe(sp, 0, 0, v)
                    sp.wait_ge(router_in, 16)

                @block.scalar
                def _(act):
                    act.wait_ge(roots, 1)
                    act.activation(ssq, ssq, ACT.Sqrt).then_inc(roots, 1)
                    for m in range(4):
                        act.wait_ge(rows_sum, m + 1)
                        act.activation(rows[:, m // 2, (m % 2) * 512:(m % 2 + 1) * 512], ps[m][:, :], ACT.Copy).then_inc(rows_out, 1)
                    for f in range(KD):
                        act.wait_ge(turned, f + 1)
                        act.activation(hT[0][:, f, 2 * P:TOK], ps[f][:, 0:2 * P], ACT.Copy).then_inc(hi_out, 1)
                    act.wait_ge(logits_out, 2)
                    for j in range(2):
                        ins = act.activation(ex[:, j, :], lg[:, j, :], ACT.Exp, bias=negm[:, j:j + 1])
                    ins.then_inc(exps, 1)

                @block.vector
                def _(dve):
                    dve.wait_ge(router_in, 16)
                    dve_step(dve, dve.tensor_copy(wr2[0][:, :, :], wr[:, :, :]))
                    dve_step(dve, dve.tensor_tensor(wr2[1][:, :, :], wr[:, :, :], wr2[0][:, :, :].bitcast(F32), ALU.subtract))
                    dve.tensor_scalar(ssq, ssq, 1.0 / D, EPS, ALU.mult, ALU.add).then_inc(roots, 1)
                    dve.wait_ge(roots, 2)
                    dve_step(dve, dve.reciprocal(ssq, ssq))
                    dve.wait_ge(rows_out, 4)
                    for j in range(2):
                        h = xn[:, j, :]
                        dve_step(dve, dve.scalar_tensor_tensor(h, xres[:, 2 + j, :], ssq[:, j:j + 1], rows[:, 0, :], ALU.mult, ALU.mult))
                        dve.tensor_tensor(h, h, rows[:, 1, :], ALU.add).then_inc(h_done, 1)
                        dve.wait_ge(h_done, j + 1)
                        dve_step(dve, dve.tensor_copy(htok[0][:, j, :], h))
                        dve_step(dve, dve.tensor_tensor(htok[1][:, j, :], h, htok[0][:, j, :].bitcast(F32), ALU.subtract))
                    for f in range(KD):
                        dve.wait_ge(hi_out, f + 1)
                        dve.tensor_tensor(hT[1][:, f, 2 * P:TOK], ps[f][:, 0:2 * P], hT[0][:, f, 2 * P:TOK].bitcast(F32),
                                          ALU.subtract).then_inc(parts, 1)
                    dve.wait_ge(logits_sum, 1)
                    dve_step(dve, dve.tensor_copy(lg[:, :, :], ps[0][:, 0:2 * NE].rearrange("p (j e) -> p j e", j=2)))
                    dve.tensor_reduce(negm, lg[:, :, :], AX.X, ALU.max).then_inc(logits_out, 1)
                    dve.wait_ge(logits_out, 1)
                    dve.tensor_scalar(negm, negm, -1.0, None, ALU.mult).then_inc(logits_out, 1)
                    for j in range(2):
                        shape = [P, NE, NE]
                        inner, outer = lg[:, j, :].unsqueeze(1).to_broadcast(shape), lg[:, j, :].unsqueeze(2).to_broadcast(shape)
                        gt, eq = (cmp[:, j, i, :].rearrange("p (a b) -> p a b", a=NE) for i in range(2))
                        dve.tensor_tensor(gt, inner, outer, ALU.is_gt)
                        dve_step(dve, dve.tensor_tensor(eq, inner, outer, ALU.is_equal))
                        dve_step(dve, dve.tensor_tensor(cmp[:, j, 1, :], cmp[:, j, 1, :], const("before"), ALU.mult))
                        dve_step(dve, dve.tensor_tensor(cmp[:, j, 0, :], cmp[:, j, 0, :], cmp[:, j, 1, :], ALU.add))
                        dve_step(dve, dve.tensor_reduce(sel[:, j, :], gt, AX.X, ALU.add))
                    dve.tensor_scalar(sc[:, 32:48], sc[:, 32:48], 2.0, None, ALU.is_lt).then_inc(sel_done, 1)
                    dve.wait_ge(exps, 1)
                    dve.wait_ge(sel_done, 1)
                    dve_step(dve, dve.tensor_tensor(ex, ex, sel, ALU.mult))
                    dve_step(dve, dve.tensor_reduce(ssum, ex, AX.X, ALU.add))
                    dve_step(dve, dve.reciprocal(ssum, ssum))
                    dve_step(dve, dve.tensor_tensor(ex, ex, spread(ssum, 2, NE), ALU.mult))
                    dve.wait_ge(counted, 1)
                    pos = ps[1][:, 0:2 * NE].rearrange("p (j e) -> p j e", j=2)
                    for r in range(2):
                        s = slice(r * NE, (r + 1) * NE)
                        dve.tensor_copy(chosen[:, :, s], sel)
                        dve.tensor_copy(weight[:, :, s], ex)
                        dve.scalar_tensor_tensor(slot_of[:, :, s], pos, -float(r * P), sel, ALU.add, ALU.subtract)
                    for a in (slot_of, chosen, weight):
                        dve.memset(a[:, :, 2 * NE:2 * NE + 1], -1.0)
                    dve_step(dve, dve.tensor_reduce(most, ps[1][:, 2 * NE:3 * NE], AX.X, ALU.max))
                    dve_step(dve, dve.tensor_scalar(n_pass[:, :], most, float(P), 1.0, ALU.is_gt, ALU.add))

                @block.tensor
                def _(pe):
                    for i, cols_of_row in enumerate((gain, shift)):
                        for half in range(2):
                            for d in range(4):
                                last = pe.matmul(ps[2 * i + half][:, d * P:(d + 1) * P],
                                                 cols_of_row[:, 4 * half + d, :].to_broadcast([P, P]), ident, start=True, stop=True)
                            last.then_inc(rows_sum, 1)
                    pe.wait_ge(h_done, 2)
                    for f in range(KD):
                        for j in range(2):
                            last = pe.transpose(ps[f][:, j * P:(j + 1) * P], xn[:, j, f * P:(f + 1) * P], ident)
                        last.then_inc(turned, 1)
                    pe.wait_ge(parts, KD)
                    for j in range(2):
                        for k in range(KD):
                            a = [h[:, k, (2 + j) * P:(3 + j) * P] for h in hT]
                            last = three(pe, ps[0][:, j * NE:(j + 1) * NE], a, [w[:, k, :] for w in wr2], k == 0, k == KD - 1)
                    last.then_inc(logits_sum, 1)
                    pe.wait_ge(sel_done, 1)
                    pe.matmul(ps[1][:, 0:NE], const("tri_f"), sel[:, 0, :], start=True, stop=True)
                    pe.matmul(ps[1][:, NE:2 * NE], const("tri_f"), sel[:, 1, :], start=True, stop=False)
                    pe.matmul(ps[1][:, NE:2 * NE], const("ones"), sel[:, 0, :], start=False, stop=True)
                    for j in range(2):
                        last = pe.matmul(ps[1][:, 2 * NE:3 * NE], const("ones"), sel[:, j, :], start=j == 0, stop=j == 1)
                    last.then_inc(counted, 1)
            end_stage()

        yacc = at("moe_y", [P, NT, D], F32, M0 + 17408 - 2 * D * 4)

        def moe_experts():
            m = M0 + 17408 + 2 * D * 4
            xeT = [at(f"xe_T_{n}", [P, KD, P], F32R, m + 4096 * i) for i, n in enumerate(("hi", "lo"))]
            m += 8192
            gT = [at(f"moe_gT_{n}", [P, FT, P], F32R, m + FT * P * 4 * i) for i, n in enumerate(("hi", "lo"))]
            m += 2 * FT * P * 4
            pick = at("pick", [P, 2, P], F32, m)
            pick_r = at("pick_r", [P, 2, P], F32R, m + 1024)
            put = at("put", [P, 2 * P], F32R, m + 2048)
            w_slot = at("w_slot", [P, 1], F32, m + 3072)
            m += 3136
            silu = at("moe_silu", [P, 2, 512], F32, m)
            prod = at("moe_prod", [P, 2, 512], F32, m + 4096)
            ytmp = at("moe_ytmp", [P, D], F32, m + 8192)
            ye = [at(f"moe_ye_{n}", [P, D], F32R, m + 12288 + 4096 * i) for i, n in enumerate(("hi", "lo"))]

            CUT = 1408
            h1_end = [4 * b + 1 for b in range(NB - 1)] + [up - 2]
            h3_end = [4 * b + 3 for b in range(NB - 1)] + [up - 1]
            turn_after = [h1_end[b + 1] for b in range(NB - 2)] + [up - 1, up + 1]
            gather_after = up + 4
            names = ("hi_m", "lo_dve", "lo_pool", "used", "pick_ready", "gathered", "xe_act", "xe_dve", "put_sum",
                     "put_out", "ws_out", "silu_out", "g_done", "turned", "hi_out", "lo_done", "ye_out", "ye_ready",
                     "combined", "added", "dve_loop", "slot_free")
            (hi_m, lo_dve, lo_pool, used, pick_ready, gathered, xe_act, xe_dve, put_sum,
             put_out, ws_out, silu_out, g_done, turned, hi_out, lo_done, ye_out, ye_ready,
             combined, added, dve_loop, slot_free) = (stage_sem(s) for s in names)

            def part(buf, v):
                return unit_part(buf, v % RING, v)

            def raw_slot(x, v):
                return (U * x + v) % RAW_RING

            def hi(act, i, x, v):
                act.wait_ge(raw_m[raw_slot(x, v)], 16 * (2 * U // RAW_RING) * i + 16 * ((U * x + v) // RAW_RING + 1))
                act.activation(moe_hi[:, v % RING, :], moe_raw[:, raw_slot(x, v), :], ACT.Copy).then_inc(hi_m, 1)

            def lo(eng, i, x, v, a, b, done):
                eng.wait_ge(hi_m, 2 * U * i + U * x + v + 1)
                s = v % RING
                eng.tensor_tensor(moe_lo[:, s, a:b], moe_raw[:, raw_slot(x, v), a:b], moe_hi[:, s, a:b].bitcast(F32), ALU.subtract).then_inc(done, 1)

            class LoopSteps:

                def __init__(self, sem, per, n):
                    self.sem, self.per, self.n, self.k = sem, per, n, 0

                def __call__(self, eng, ins):
                    self.k += 1
                    ins.then_inc(self.sem, 1)
                    eng.wait_ge(self.sem, self.per * self.n + self.k)

                def end(self):
                    assert self.k == self.per, self.k

            def build_pick(dve, nn):
                for j in range(2):
                    dve.tensor_scalar(pick[:, j, :], const("iota"), slot_of[:, j, bass.ds(nn, 1)], chosen[:, j, bass.ds(nn, 1)],
                                      ALU.is_equal, ALU.mult).then_inc(pick_ready, 1)
                dve.wait_ge(pick_ready, 3 * nn + 2)
                dve.tensor_copy(pick_r[:, :, :], pick[:, :, :]).then_inc(pick_ready, 1)

            def gather(pe, nn, which):
                pe.wait_ge(pick_ready, 3 * nn + 3)
                for half in range(2):
                    src = htok[which]
                    if which:
                        pe.wait_ge(xe_act if half == 0 else xe_dve, 2 * nn + 1)
                    for d in range(4):
                        dd = 4 * half + d
                        for j in range(2):
                            last = pe.matmul(ps[4 + half][:, d * P:(d + 1) * P], src[:, j, dd * P:(dd + 1) * P], pick_r[:, j, :],
                                             start=j == 0, stop=j == 1)
                    last.then_inc(gathered, 1)

            def xe_out(copy, nn, which, half, done, eng):
                eng.wait_ge(gathered, 4 * nn + 2 * which + half + 1)
                copy(xeT[which][:, 4 * half:4 * half + 4, :], ps[4 + half][:, :].rearrange("p (d s) -> p d s", d=4)).then_inc(done, 1)

            def combine(pe, n, c):
                if c >= 2:
                    pe.wait_ge(added, 4 * n + c - 1)
                j, half = divmod(c, 2)
                for p, a in enumerate(ye):
                    last = pe.matmul(ps[4 + half][:, :], put[:, j * P:(j + 1) * P], a[:, half * 512:(half + 1) * 512],
                                     start=p == 0, stop=p == 1)
                last.then_inc(combined, 1)

            def add_combined(dve, n, c):
                dve.wait_ge(combined, 4 * n + c + 1)
                a = yacc[:, 2 + c // 2, (c % 2) * 512:(c % 2 + 1) * 512]
                dve.tensor_tensor(a, a, ps[4 + c % 2][:, :], ALU.add).then_inc(added, 1)

            with nc.Block() as block:
                @block.sync
                def _(sp):
                    passes = sp.value_load(n_pass[0:1, 0:1], min_val=1, max_val=2)
                    with sp.Fori(0, passes * (NE // 2)) as i:
                        experts = [sp.snap((2 * i + x) % NE) for x in range(3)]
                        for x in range(2):
                            for v in range(RAW_RING, U + RAW_RING):
                                split = sp.snap(2 * U * i + (U * x + v - RAW_RING + 1))
                                sp.wait_ge(lo_dve, split)
                                sp.wait_ge(lo_pool, split)
                                sp.sem_inc(slot_free, 1)
                                load_moe(sp, experts[x + v // U], x, v)
                    for s in range(RAW_RING):
                        sp.wait_ge(raw_m[s], passes * (NE // 2 * (2 * U // RAW_RING) * 16) + 16)
                        sp.sem_inc(slot_free, 1)

                @block.gpsimd
                def _(pool):
                    passes = pool.value_load(n_pass[0:1, 0:1], min_val=1, max_val=2)
                    for v in range(AHEAD):
                        lo(pool, 0, 0, v, CUT, 2048, lo_pool)
                    with pool.Fori(0, passes * (NE // 2)) as i:
                        for x in range(2):
                            for v in range(AHEAD, U + AHEAD):
                                lo(pool, i, x, v, CUT, 2048, lo_pool)

                @block.scalar
                def _(act):
                    passes = act.value_load(n_pass[0:1, 0:1], min_val=1, max_val=2)

                    def copy(out, in_):
                        return act.activation(out, in_, ACT.Copy)

                    act.sem_inc(silu_out, 2)
                    act.sem_inc(ye_out, 1)
                    for v in range(AHEAD):
                        hi(act, 0, 0, v)
                    for p in range(2):
                        xe_out(copy, 0, p, 0, xe_act, act)
                    with act.Fori(0, passes * (NE // 2)) as i:
                        for x in range(2):
                            n = 2 * i + x
                            for u in range(U):
                                act.wait_ge(used, U * n + u + 1)
                                hi(act, i, x, u + AHEAD)
                                if u == 4:
                                    act.wait_ge(put_sum, n + 1)
                                    act.activation(put[:, :], ps[4][:, 0:2 * P], ACT.Copy).then_inc(put_out, 1)
                                for b in range(NB):
                                    if u == h1_end[b] + 1:
                                        w = plan[h1_end[b]][4]
                                        act.wait_ge(g_done, NB * n + b + 1)
                                        act.activation(silu[:, b % 2, 0:w], ps[b % 2][:, 0:w], ACT.Silu).then_inc(silu_out, 1)
                                    if u == turn_after[b] + 1:
                                        k = 4 if b < NB - 1 else 2
                                        act.wait_ge(turned, NB * n + b + 1)
                                        act.activation(gT[0][:, 4 * b:4 * b + k, :],
                                                       ps[4 + b % 2][:, 0:k * P].rearrange("p (k s) -> p k s", k=k),
                                                       ACT.Copy).then_inc(hi_out, 1)
                                for p in range(2):
                                    if u == gather_after + 2 * p + 1:
                                        xe_out(copy, n + 1, p, 0, xe_act, act)
                            act.wait_ge(used, U * n + U + 1)
                            act.wait_ge(ws_out, n + 1)
                            act.activation(ytmp[:, 0:512], ps[6][:, :], ACT.Copy, scale=w_slot[:, 0:1])
                            act.activation(ytmp[:, 512:D], ps[7][:, :], ACT.Copy, scale=w_slot[:, 0:1]).then_inc(ye_out, 1)

                @block.vector
                def _(dve):
                    passes = dve.value_load(n_pass[0:1, 0:1], min_val=1, max_val=2)
                    dve.sem_inc(g_done, 2)
                    dve.sem_inc(lo_done, 2)
                    build_pick(dve, 0)
                    dve_step(dve, dve.memset(yacc[:, 2:4, :], 0.0))
                    dve_step(dve, dve.tensor_copy(put[:, :], yacc[:, 2, 0:2 * P]))
                    for a in ye:
                        dve_step(dve, dve.tensor_copy(a[:, :], yacc[:, 2, :]))
                    dve.sem_inc(ye_ready, 1)
                    for v in range(AHEAD):
                        lo(dve, 0, 0, v, 0, CUT, lo_dve)
                    for p in range(2):
                        xe_out(dve.tensor_copy, 0, p, 1, xe_dve, dve)
                    with dve.Fori(0, passes * (NE // 2)) as i:
                        for x in range(2):
                            n = 2 * i + x
                            step = LoopSteps(dve_loop, 1, n)
                            for u in range(U):
                                lo(dve, i, x, u + AHEAD, 0, CUT, lo_dve)
                                if u in (2, 3):
                                    for c in (2 * u - 4, 2 * u - 3):
                                        add_combined(dve, n, c)
                                if u == 4:
                                    dve.wait_ge(put_sum, n + 1)
                                    dve.tensor_copy(w_slot[:, :], ps[5][:, 0:1]).then_inc(ws_out, 1)
                                for b in range(NB):
                                    if u == h3_end[b] + 1:
                                        w = plan[h3_end[b]][4]
                                        dve.wait_ge(silu_out, NB * n + b + 3)
                                        dve.wait_ge(used, U * n + h3_end[b] + 2)
                                        dve.tensor_tensor(prod[:, b % 2, 0:w], silu[:, b % 2, 0:w], ps[2 + b % 2][:, 0:w],
                                                          ALU.mult).then_inc(g_done, 1)
                                    if u == turn_after[b] + 2:
                                        k = 4 if b < NB - 1 else 2
                                        dve.wait_ge(hi_out, NB * n + b + 1)
                                        dve.tensor_tensor(gT[1][:, 4 * b:4 * b + k, :],
                                                          ps[4 + b % 2][:, 0:k * P].rearrange("p (k s) -> p k s", k=k),
                                                          gT[0][:, 4 * b:4 * b + k, :].bitcast(F32), ALU.subtract).then_inc(lo_done, 1)
                                if u == up + 1:
                                    build_pick(dve, n + 1)
                                for p in range(2):
                                    if u == gather_after + 2 * p + 1:
                                        xe_out(dve.tensor_copy, n + 1, p, 1, xe_dve, dve)
                            dve.wait_ge(ye_out, n + 2)
                            step(dve, dve.tensor_copy(ye[0][:, :], ytmp[:, :]))
                            dve.tensor_tensor(ye[1][:, :], ytmp[:, :], ye[0][:, :].bitcast(F32), ALU.subtract).then_inc(ye_ready, 1)
                            step.end()
                    for c in range(4):
                        add_combined(dve, passes * NE, c)

                @block.tensor
                def _(pe):
                    passes = pe.value_load(n_pass[0:1, 0:1], min_val=1, max_val=2)
                    pe.sem_inc(used, 1)
                    for p in range(2):
                        gather(pe, 0, p)
                    with pe.Fori(0, passes * (NE // 2)) as i:
                        for x in range(2):
                            n = 2 * i + x
                            pe.wait_ge(xe_act, 2 * n + 2)
                            pe.wait_ge(xe_dve, 2 * n + 2)
                            for u in range(U):
                                pe.wait_ge(lo_dve, U * n + u + 1)
                                pe.wait_ge(lo_pool, U * n + u + 1)
                                _, k0, a, _, w = plan[u]
                                wh, wl = part(moe_hi, u), part(moe_lo, u)
                                if u < up:
                                    b = min(u // 4, NB - 1)
                                    is_h3 = plan[u][0] is w3
                                    if u in (4 * b, 4 * b + 2) or b == NB - 1:
                                        pe.wait_ge(g_done if is_h3 else silu_out, NB * n + b + 1)
                                    bank = ps[2 * is_h3 + b % 2]
                                    for k in range(a):
                                        kk = k0 + k
                                        last = three(pe, bank[:, 0:w], [a_[:, kk, :] for a_ in xeT], [wh[:, k, :], wl[:, k, :]],
                                                     kk == 0, kk == KD - 1)
                                else:
                                    if u == up:
                                        pe.wait_ge(ye_out, n + 1)
                                    for k in range(a):
                                        kk = k0 + k
                                        if kk % 4 == 0:
                                            pe.wait_ge(lo_done, NB * n + kk // 4 + 3)
                                        for half in range(2):
                                            c = slice(half * 512, (half + 1) * 512)
                                            last = three(pe, ps[6 + half][:, :], [a_[:, kk, :] for a_ in gT], [wh[:, k, c], wl[:, k, c]],
                                                         kk == 0, kk == FT - 1)
                                last.then_inc(used, 1)
                                if u in (1, 2):
                                    if u == 1:
                                        pe.wait_ge(ye_ready, n + 1)
                                    for c in (2 * u - 2, 2 * u - 1):
                                        combine(pe, n, c)
                                if u == 3:
                                    pe.wait_ge(added, 4 * n + 4)
                                    for j in range(2):
                                        pe.transpose(ps[4][:, j * P:(j + 1) * P], pick[:, j, :], ident)
                                    for j in range(2):
                                        last = pe.matmul(ps[5][:, 0:1], pick[:, j, :], weight[:, j, bass.ds(n, 1)], start=j == 0, stop=j == 1)
                                    last.then_inc(put_sum, 1)
                                for b in range(NB):
                                    if u == turn_after[b]:
                                        if b < 2:
                                            pe.wait_ge(put_out if b == 0 else ws_out, n + 1)
                                        pe.wait_ge(g_done, NB * n + b + 3)
                                        pe.wait_ge(lo_done, NB * n + b + 1)
                                        for k in range(4 if b < NB - 1 else 2):
                                            last = pe.transpose(ps[4 + b % 2][:, k * P:(k + 1) * P], prod[:, b % 2, k * P:(k + 1) * P], ident)
                                        last.then_inc(turned, 1)
                                if u == gather_after:
                                    pe.wait_ge(lo_done, NB * n + NB + 2)
                                for p in range(2):
                                    if u == gather_after + 2 * p:
                                        gather(pe, n + 1, p)
                    pe.wait_ge(xe_act, passes * (2 * NE) + 2)
                    pe.wait_ge(xe_dve, passes * (2 * NE) + 2)
                    pe.wait_ge(ye_ready, passes * NE + 1)
                    for c in range(4):
                        combine(pe, passes * NE, c)
            end_stage()

        def finish(l):
            rows = at("last_rows", [P, 2, D], F32, R0)
            junk = at("last_junk", [P, 2, 512], F32, R0 + 8192)
            scaled, rows_sum, rows_out, y_out, squared, means, roots, x_out, stored = (
                stage_sem(s) for s in ("scaled", "rows_sum", "rows_out", "y_out", "squared", "means", "roots", "x_out", "stored"))
            with nc.Block() as block:
                @block.sync
                def _(sp):
                    for j in range(2):
                        sp.wait_ge(x_out, j + 1)
                        sp.dma_start(t["out"][0, j * P:(j + 1) * P, :], xres[:, 2 + j, :]).then_inc(stored, 16)
                    sp.wait_ge(stored, 32)

                @block.gpsimd
                def _(pool):
                    post_norm_pool(pool, yacc, X_TILES, scaled, x_out)

                @block.scalar
                def _(act):
                    post_rows_act(act, rows, [0], rows_sum, rows_out, [0, 1, 2, 3])
                    post_norm_act(act, yacc, X_TILES, junk, y_out, squared, means, roots)

                @block.vector
                def _(dve):
                    dve.sem_inc(y_out, 4)
                    post_norm_dve(dve, yacc, rows, X_TILES, squared, means, roots, rows_out, 2, scaled)

                @block.tensor
                def _(pe):
                    post_rows_pe(pe, l, 1, [0], rows_sum, rows_out, [0, 1, 2, 3])
            end_stage()

        setup()
        for l in range(DEPTH):
            tiles = ALL_TILES if l == 0 else X_TILES
            norm(l, ALL_TILES, 0)
            ssm_project(l)
            ssm_mix(l, tiles, [(0, c) for c in range(2, 6)] + [(1, 0), (1, 1)] if l == 0 else [(1, c) for c in range(2, 6)])
            ssm_gate(l, tiles)
            merge(l, 1, tiles, True)
            ret_project(l, tiles)
            ret_mix(l, tiles)
            ret_gate(l, tiles)
            merge(l, 0, tiles, False)
            att_project(l, tiles)
            att_mix(l, tiles)
            merge(l, 2, tiles, False)
            out_project(l, tiles)
            if l == 0:
                norm(l, ALL_TILES, 1)
                ffn_up()
                ffn_down(l)
            else:
                moe_route(l)
                moe_experts()
                finish(l)


INPUTS = ["x", "c", "ctx", "c_ctx", "ada_w", "ada_b", "mix_norm_pre", "mix_norm_post", "ffn_norm_pre",
          "ffn_norm_post", "w_in", "ret_decay", "ssm_conv_w", "ssm_conv_b", "ssm_dt_bias", "ssm_a_log", "ssm_d",
          "ssm_norm_w", "att_sink", "w_branch", "w_out", "ffn_w1", "ffn_w3", "ffn_w2", "moe_router", "moe_w1",
          "moe_w3", "moe_w2"]


def kernel(**inputs):
    import concourse.bacc as bacc
    from concourse.bass_utils import run_bass_kernel_spmd

    nc = bacc.Bacc("TRN2", target_bir_lowering=False, num_devices=1)
    arrays = {name: np.ascontiguousarray(inputs[name]) for name in INPUTS}
    arrays["consts"] = constants()
    t = {name: nc.dram_tensor(f"in_{name}", a.shape, F32, kind="ExternalInput").ap() for name, a in arrays.items()}
    t["out"] = nc.dram_tensor("out", (1, SEQ, D), F32, kind="ExternalOutput").ap()
    program(nc, t)
    r = run_bass_kernel_spmd(nc, [{f"in_{name}": a for name, a in arrays.items()}], core_ids=[0])
    return r.results[0]["out"]
```
